# Optimizing a Trainium2 kernel written in Bass

```python
import math
import jax
import jax.numpy as jnp
from jax import lax
import numpy as np
import jax, jax.numpy as jnp

D_MODEL = 1024
BATCH = 1
SEQ = 1024
DEPTH = 1

EPS = 1e-6
POOL_WINDOWS = (2, 4, 8, 16)
POOL_GROUP = D_MODEL // 8
POOL_WIDTH = len(POOL_WINDOWS) * POOL_GROUP
DIL_PAIRS = ((128, 1), (512, 4), (2048, 16))
DIL_HEADS_PER_GROUP = 4
DIL_HEADS = len(DIL_PAIRS) * DIL_HEADS_PER_GROUP
DIL_HEAD_DIM = 64
DIL_QKV_WIDTH = DIL_HEADS * DIL_HEAD_DIM
DIL_OUT_WIDTH = DIL_HEADS_PER_GROUP * DIL_HEAD_DIM
REL_BUCKETS = 32
REL_MAX_DIST = 2048
SB_HEADS = 4
SB_HEAD_DIM = 128
SB_WIDTH = SB_HEADS * SB_HEAD_DIM
SB_BLOCK = 128
S5_WIDTH = D_MODEL // 2
S5_CH = 16
S5_GROUPS = S5_WIDTH // S5_CH
S5_STATE = 64
FFN_HIDDEN = ((8 * D_MODEL + 3 * 256 - 1) // (3 * 256)) * 256
N_BRANCHES = 4
IN_WIDTH = POOL_WIDTH + 3 * DIL_QKV_WIDTH + 3 * SB_WIDTH + S5_WIDTH
BRANCH_WIDTHS = (POOL_WIDTH, DIL_OUT_WIDTH, SB_WIDTH, S5_WIDTH)
BRANCH_WIDTH = sum(BRANCH_WIDTHS)


def rmsnorm(x, g):
    xf = x.astype(jnp.float32)
    y = xf * lax.rsqrt(jnp.mean(xf * xf, axis=-1, keepdims=True) + EPS)
    return (y * g.astype(jnp.float32)).astype(x.dtype)

def pool_mixer(u, w_grp, scale):
    B_, S_, _ = u.shape
    uf = u.astype(jnp.float32)
    cs = jnp.concatenate([jnp.zeros_like(uf[:, :1]), jnp.cumsum(uf, axis=1)], axis=1)
    t = jnp.arange(S_)
    outs = []
    for gi, w in enumerate(POOL_WINDOWS):
        sl = slice(gi * POOL_GROUP, (gi + 1) * POOL_GROUP)
        lo = jnp.maximum(t + 1 - w, 0)
        cnt = (t + 1 - lo).astype(jnp.float32)
        mean = (cs[:, 1:, sl] - cs[:, lo, sl]) / cnt[None, :, None]
        outs.append(mean - uf[:, :, sl])
    p = jnp.stack(outs, axis=2)
    y = jnp.einsum('bsgc,gcd->bsgd', p, w_grp.astype(jnp.float32)).reshape(B_, S_, POOL_WIDTH)
    return (y * scale.astype(jnp.float32)).astype(u.dtype)

def t5_bucket(dist):
    exact = REL_BUCKETS // 2
    df = jnp.maximum(dist, 1).astype(jnp.float32)
    large = exact + (jnp.log(df / exact) / math.log(REL_MAX_DIST / exact)
                     * (REL_BUCKETS - exact)).astype(jnp.int32)
    large = jnp.minimum(large, REL_BUCKETS - 1)
    return jnp.where(dist < exact, dist, large)

def dilated_group(q, k, v, bias_tab, window, dil):
    B_, S_, H, E = q.shape
    band = window // dil
    L = S_ // dil
    nb = -(-L // band)
    Lp = nb * band

    def to_sub(a):
        a = a.reshape(B_, L, dil, H, E).transpose(0, 2, 3, 1, 4)
        return jnp.pad(a, ((0, 0), (0, 0), (0, 0), (0, Lp - L), (0, 0)))

    def band_keys(a):
        a = jnp.pad(a, ((0, 0), (0, 0), (0, 0), (band, 0), (0, 0))).reshape(B_, dil, H, nb + 1, band, E)
        return jnp.concatenate([a[:, :, :, :-1], a[:, :, :, 1:]], axis=4)

    qb = to_sub(q).reshape(B_, dil, H, nb, band, E)
    kb = band_keys(to_sub(k))
    vb = band_keys(to_sub(v))
    i = jnp.arange(band)[:, None]
    c = jnp.arange(2 * band)[None, :]
    dist_sub = band + i - c
    in_band = (dist_sub >= 0) & (dist_sub <= band)
    n = jnp.arange(nb)[:, None, None]
    mask = in_band[None] & ((n > 0) | (c[None] >= band))
    buckets = t5_bucket(jnp.clip(dist_sub, 0, band) * dil)
    bias = bias_tab.astype(jnp.float32)[buckets].transpose(2, 0, 1)
    s = jnp.einsum('bdhnqe,bdhnke->bdhnqk', qb, kb, preferred_element_type=jnp.float32) / math.sqrt(E)
    s = jnp.where(mask[None, None, None], s + bias[None, None, :, None], -1e30)
    m = jnp.max(s, axis=-1, keepdims=True)
    p = jnp.exp(s - m)
    den = jnp.sum(p, axis=-1, keepdims=True)
    o = jnp.einsum('bdhnqk,bdhnke->bdhnqe', p, vb.astype(jnp.float32)) / den
    lse = (m + jnp.log(den))[..., 0]
    o = o.reshape(B_, dil, H, Lp, E)[:, :, :, :L].transpose(0, 3, 1, 2, 4).reshape(B_, S_, H, E)
    lse = lse.reshape(B_, dil, H, Lp)[:, :, :, :L].transpose(0, 3, 1, 2).reshape(B_, S_, H)
    return o, lse

def dilated_attention(qkv, rel_bias):
    B_, S_ = qkv.shape[:2]
    outs, lses = [], []
    for g, (window, dil) in enumerate(DIL_PAIRS):
        hs = slice(g * DIL_HEADS_PER_GROUP, (g + 1) * DIL_HEADS_PER_GROUP)
        o, lse = dilated_group(qkv[:, :, 0, hs], qkv[:, :, 1, hs], qkv[:, :, 2, hs],
                               rel_bias[:, hs], window, dil)
        outs.append(o)
        lses.append(lse)
    o = jnp.stack(outs, axis=0)
    alpha = jax.nn.softmax(jnp.stack(lses, axis=0), axis=0)
    y = jnp.sum(alpha[..., None] * o, axis=0)
    return y.reshape(B_, S_, DIL_OUT_WIDTH).astype(qkv.dtype)

def stick_breaking_attention(qkv):
    B_, S_, _, H, E = qkv.shape
    nb = S_ // SB_BLOCK
    qh = qkv[:, :, 0].transpose(0, 2, 1, 3)
    kh = qkv[:, :, 1].transpose(0, 2, 1, 3)
    vh = qkv[:, :, 2].transpose(0, 2, 1, 3).astype(jnp.float32)
    qblk = qh.reshape(B_, H, nb, SB_BLOCK, E).transpose(2, 0, 1, 3, 4)
    key_pos = jnp.arange(S_)

    def one_block(args):
        qb, bi = args
        z = jnp.einsum('bhqe,bhke->bhqk', qb, kh, preferred_element_type=jnp.float32) / math.sqrt(E)
        q_pos = bi * SB_BLOCK + jnp.arange(SB_BLOCK)
        mask = key_pos[None, :] < q_pos[:, None]
        log_not = jnp.where(mask, jax.nn.log_sigmoid(-z), 0.0)
        excl = lax.cumsum(log_not, axis=3, reverse=True) - log_not
        w = jnp.where(mask, jnp.exp(jax.nn.log_sigmoid(z) + excl), 0.0)
        return jnp.einsum('bhqk,bhke->bhqe', w, vh)

    o = lax.map(one_block, (qblk, jnp.arange(nb)))
    return o.transpose(1, 0, 3, 2, 4).reshape(B_, S_, SB_WIDTH).astype(qkv.dtype)

def s5_mixer(u, a_re, a_im, log_dt, b_re, b_im, c_re, c_im, d_skip, w_glu):
    B_, S_, _ = u.shape
    f32 = jnp.float32
    uf = u.astype(f32).reshape(B_, S_, S5_GROUPS, S5_CH)
    lam = lax.complex(a_re.astype(f32), a_im.astype(f32))
    dt = jnp.exp(log_dt.astype(f32))[:, None]
    lam_bar = jnp.exp(lam * dt)
    b_t = lax.complex(b_re.astype(f32), b_im.astype(f32))
    b_bar = ((lam_bar - 1.0) / lam)[:, :, None] * b_t
    bu = jnp.einsum('gpc,bsgc->bsgp', b_bar, uf.astype(jnp.complex64))
    a = jnp.broadcast_to(lam_bar, (1, S_) + lam_bar.shape)

    def combine(left, right):
        a_l, b_l = left
        a_r, b_r = right
        return a_r * a_l, a_r * b_l + b_r

    _, h = lax.associative_scan(combine, (a, bu), axis=1)
    c_t = lax.complex(c_re.astype(f32), c_im.astype(f32))
    y = jnp.real(jnp.einsum('gcp,bsgp->bsgc', c_t, h)) + d_skip.astype(f32).reshape(S5_GROUPS, S5_CH) * uf
    y = jax.nn.gelu(y.reshape(B_, S_, S5_WIDTH))
    gl = y @ w_glu.astype(f32)
    y = gl[..., :S5_WIDTH] * jax.nn.sigmoid(gl[..., S5_WIDTH:])
    return y.astype(u.dtype)

def first_inputs(seed: int = 0) -> dict:
    key = jax.random.key(seed)
    ks = jax.random.split(key, 22)
    nrm = jax.random.normal
    f32 = jnp.float32
    x = nrm(ks[0], (BATCH, SEQ, D_MODEL), f32)
    attn_norm_g = 1.0 + 0.02 * nrm(ks[1], (DEPTH, D_MODEL), f32)
    w_in = nrm(ks[2], (DEPTH, D_MODEL, IN_WIDTH), f32) * D_MODEL ** -0.5
    pool_w = nrm(ks[3], (DEPTH, len(POOL_WINDOWS), POOL_GROUP, POOL_GROUP), f32) * POOL_GROUP ** -0.5
    pool_scale = 1.0 + 0.02 * nrm(ks[4], (DEPTH, POOL_WIDTH), f32)
    rel_bias = 0.5 * nrm(ks[5], (REL_BUCKETS, DIL_HEADS), f32)
    s5_a_re = -0.5 + 0.01 * nrm(ks[6], (DEPTH, S5_GROUPS, S5_STATE), f32)
    s5_a_im = jnp.pi * jnp.arange(S5_STATE, dtype=f32)[None, None, :] + 0.01 * nrm(ks[7], (DEPTH, S5_GROUPS, S5_STATE), f32)
    s5_log_dt = jax.random.uniform(ks[8], (DEPTH, S5_GROUPS), f32, minval=math.log(1e-3), maxval=math.log(1e-1))
    s5_b_re = nrm(ks[9], (DEPTH, S5_GROUPS, S5_STATE, S5_CH), f32) * (2 * S5_CH) ** -0.5
    s5_b_im = nrm(ks[10], (DEPTH, S5_GROUPS, S5_STATE, S5_CH), f32) * (2 * S5_CH) ** -0.5
    s5_c_re = nrm(ks[11], (DEPTH, S5_GROUPS, S5_CH, S5_STATE), f32) * S5_STATE ** -0.5
    s5_c_im = nrm(ks[12], (DEPTH, S5_GROUPS, S5_CH, S5_STATE), f32) * S5_STATE ** -0.5
    s5_d = nrm(ks[13], (DEPTH, S5_WIDTH), f32)
    s5_w_glu = nrm(ks[14], (DEPTH, S5_WIDTH, 2 * S5_WIDTH), f32) * S5_WIDTH ** -0.5
    row_scale = jnp.concatenate([jnp.full((w,), w ** -0.5, f32) for w in BRANCH_WIDTHS])
    w_branch = nrm(ks[15], (DEPTH, BRANCH_WIDTH, D_MODEL), f32) * row_scale[None, :, None]
    w_gate = nrm(ks[16], (DEPTH, N_BRANCHES, D_MODEL, D_MODEL), f32) * D_MODEL ** -0.5
    w_out = nrm(ks[17], (DEPTH, D_MODEL, D_MODEL), f32) * D_MODEL ** -0.5
    ffn_norm_g = 1.0 + 0.02 * nrm(ks[18], (DEPTH, D_MODEL), f32)
    w_up = nrm(ks[19], (DEPTH, D_MODEL, 2 * FFN_HIDDEN), f32) * D_MODEL ** -0.5
    w_down = nrm(ks[20], (DEPTH, FFN_HIDDEN, D_MODEL), f32) * FFN_HIDDEN ** -0.5
    final_norm_g = 1.0 + 0.02 * nrm(ks[21], (D_MODEL,), f32)
    return {'x': x, 'attn_norm_g': attn_norm_g, 'w_in': w_in, 'pool_w': pool_w,
            'pool_scale': pool_scale, 'rel_bias': rel_bias, 's5_a_re': s5_a_re,
            's5_a_im': s5_a_im, 's5_log_dt': s5_log_dt, 's5_b_re': s5_b_re, 's5_b_im': s5_b_im,
            's5_c_re': s5_c_re, 's5_c_im': s5_c_im, 's5_d': s5_d, 's5_w_glu': s5_w_glu,
            'w_branch': w_branch, 'w_gate': w_gate, 'w_out': w_out, 'ffn_norm_g': ffn_norm_g,
            'w_up': w_up, 'w_down': w_down, 'final_norm_g': final_norm_g}

def first_block(x, attn_norm_g, w_in, pool_w, pool_scale, rel_bias, s5_a_re, s5_a_im, s5_log_dt,
              s5_b_re, s5_b_im, s5_c_re, s5_c_im, s5_d, s5_w_glu, w_branch, w_gate, w_out,
              ffn_norm_g, w_up, w_down, final_norm_g):
    B_, S_, _ = x.shape
    o1 = POOL_WIDTH
    o2 = o1 + 3 * DIL_QKV_WIDTH
    o3 = o2 + 3 * SB_WIDTH
    for l in range(DEPTH):
        xn = rmsnorm(x, attn_norm_g[l])
        proj = xn @ w_in[l]
        u_pool = proj[..., :o1]
        qkv_dil = proj[..., o1:o2].reshape(B_, S_, 3, DIL_HEADS, DIL_HEAD_DIM)
        qkv_sb = proj[..., o2:o3].reshape(B_, S_, 3, SB_HEADS, SB_HEAD_DIM)
        u_s5 = proj[..., o3:]
        y_pool = pool_mixer(u_pool, pool_w[l], pool_scale[l])
        y_dil = dilated_attention(qkv_dil, rel_bias)
        y_sb = stick_breaking_attention(qkv_sb)
        y_s5 = s5_mixer(u_s5, s5_a_re[l], s5_a_im[l], s5_log_dt[l], s5_b_re[l], s5_b_im[l],
                        s5_c_re[l], s5_c_im[l], s5_d[l], s5_w_glu[l])
        merged = jnp.zeros_like(x)
        row = 0
        for bi, yb in enumerate((y_pool, y_dil, y_sb, y_s5)):
            width = BRANCH_WIDTHS[bi]
            gate = jax.nn.sigmoid(xn @ w_gate[l, bi])
            merged = merged + gate * (yb @ w_branch[l, row:row + width])
            row += width
        x = x + merged @ w_out[l]
        hn = rmsnorm(x, ffn_norm_g[l])
        gu = hn @ w_up[l]
        h = jax.nn.silu(gu[..., :FFN_HIDDEN]) * gu[..., FFN_HIDDEN:]
        x = x + h @ w_down[l]
    return rmsnorm(x, final_norm_g)


DN_HEAD_DIM = 128
DN_WIDTH = D_MODEL // 2
DN_HEADS = DN_WIDTH // DN_HEAD_DIM
SHORT_CONV = 4
GLA_VAL_DIM = 128
GLA_WIDTH = D_MODEL - DN_WIDTH
GLA_HEADS = GLA_WIDTH // GLA_VAL_DIM
GLA_KEY_DIM = GLA_VAL_DIM // 2
GLA_GATE_RANK = 16
GLA_TAU = 16.0
MIX_WIDTH = DN_WIDTH + GLA_WIDTH
IN_SPLITS = (DN_WIDTH, DN_WIDTH, DN_WIDTH, DN_WIDTH, DN_HEADS, DN_HEADS,
             GLA_HEADS * GLA_KEY_DIM, GLA_HEADS * GLA_KEY_DIM, GLA_WIDTH, GLA_WIDTH, GLA_GATE_RANK)
IN_WIDTH_2 = sum(IN_SPLITS)
CHUNK = 64
D_FF = 2816
FFN_CONV = 3
ALPHA = (2.0 * DEPTH) ** 0.25
BETA_INIT = (8.0 * DEPTH) ** -0.25


def layer_norm(x, g, b):
    xf = x.astype(jnp.float32)
    mu = xf.mean(-1, keepdims=True)
    var = jnp.square(xf - mu).mean(-1, keepdims=True)
    return ((xf - mu) * lax.rsqrt(var + EPS) * g.astype(jnp.float32) + b.astype(jnp.float32)).astype(x.dtype)

def rms_norm(x, g):
    xf = x.astype(jnp.float32)
    return (xf * lax.rsqrt(jnp.mean(xf * xf, -1, keepdims=True) + EPS) * g.astype(jnp.float32)).astype(x.dtype)

def l2_norm(x):
    return x * lax.rsqrt(jnp.sum(x * x, -1, keepdims=True) + EPS)

def causal_dwconv(x, w):
    k_w, ch = w.shape
    return lax.conv_general_dilated(x, w[:, None, :].astype(x.dtype), window_strides=(1,),
                                    padding=[(k_w - 1, 0)], dimension_numbers=('NWC', 'WIO', 'NWC'),
                                    feature_group_count=ch)

def to_chunks(x):
    b, t, h, d = x.shape
    return x.reshape(b, t // CHUNK, CHUNK, h, d).transpose(1, 0, 3, 2, 4)

def from_chunks(x):
    n, b, h, c, d = x.shape
    return x.transpose(1, 0, 3, 2, 4).reshape(b, n * c, h, d)

def gated_delta_rule(q, k, v, log_a, beta):
    dt = v.dtype
    q, k, v, log_a, beta = (a.astype(jnp.float32) for a in (q, k, v, log_a, beta))
    bsz, _, nh, dk = q.shape
    dv = v.shape[-1]
    qc, kc, vc = to_chunks(q * dk ** -0.5), to_chunks(k), to_chunks(v)
    G = jnp.cumsum(to_chunks(log_a[..., None])[..., 0], axis=-1)
    bc = to_chunks(beta[..., None])[..., 0]
    causal = jnp.tril(jnp.ones((CHUNK, CHUNK), dtype=bool))
    strict = jnp.tril(jnp.ones((CHUNK, CHUNK), dtype=bool), -1)
    decay = jnp.exp(jnp.where(causal, G[..., :, None] - G[..., None, :], -jnp.inf))
    kb = kc * bc[..., None]
    m_low = jnp.where(strict, jnp.einsum('nbhid,nbhjd->nbhij', kb, kc) * decay, 0.0)
    lhs = m_low + jnp.eye(CHUNK, dtype=jnp.float32)
    rhs = jnp.concatenate([vc * bc[..., None], kb * jnp.exp(G)[..., None]], axis=-1)
    sol = lax.linalg.triangular_solve(lhs, rhs, left_side=True, lower=True, unit_diagonal=True)
    u, w = sol[..., :dv], sol[..., dv:]
    attn = jnp.einsum('nbhid,nbhjd->nbhij', qc, kc) * decay
    q_dec = qc * jnp.exp(G)[..., None]
    k_dec = kc * jnp.exp(G[..., -1:] - G)[..., None]
    g_last = jnp.exp(G[..., -1])

    def step(S, inp):
        u_i, w_i, attn_i, qd_i, kd_i, gl_i = inp
        v_new = u_i - jnp.einsum('bhcd,bhde->bhce', w_i, S)
        o = jnp.einsum('bhcd,bhde->bhce', qd_i, S) + jnp.einsum('bhij,bhje->bhie', attn_i, v_new)
        S = S * gl_i[..., None, None] + jnp.einsum('bhcd,bhce->bhde', kd_i, v_new)
        return S, o

    S0 = jnp.zeros((bsz, nh, dk, dv), jnp.float32)
    _, o = lax.scan(step, S0, (u, w, attn, q_dec, k_dec, g_last))
    return from_chunks(o).astype(dt)

def gla_attention(q, k, v, log_alpha):
    dt = v.dtype
    q, k, v, log_alpha = (a.astype(jnp.float32) for a in (q, k, v, log_alpha))
    bsz, _, nh, dk = q.shape
    dv = v.shape[-1]
    qc, kc, vc = to_chunks(q * dk ** -0.5), to_chunks(k), to_chunks(v)
    b = jnp.cumsum(to_chunks(log_alpha), axis=-2)
    causal = jnp.tril(jnp.ones((CHUNK, CHUNK), dtype=bool))
    q_dec = qc * jnp.exp(b)
    attn = jnp.where(causal, jnp.einsum('nbhid,nbhjd->nbhij', q_dec, kc * jnp.exp(-b)), 0.0)
    o_intra = jnp.einsum('nbhij,nbhje->nbhie', attn, vc)
    k_dec = kc * jnp.exp(b[..., -1:, :] - b)
    g_last = jnp.exp(b[..., -1, :])

    def step(S, inp):
        qd_i, kd_i, v_i, oi_i, gl_i = inp
        o = jnp.einsum('bhcd,bhde->bhce', qd_i, S) + oi_i
        S = S * gl_i[..., :, None] + jnp.einsum('bhcd,bhce->bhde', kd_i, v_i)
        return S, o

    S0 = jnp.zeros((bsz, nh, dk, dv), jnp.float32)
    _, o = lax.scan(step, S0, (q_dec, k_dec, vc, o_intra, g_last))
    return from_chunks(o).astype(dt)

def hybrid_mixer(h, w_in, dn_conv, dn_a_log, dn_dt_bias, dn_norm_g, gla_w_gate2, gla_b_gate, gla_norm_g, w_o):
    bsz, t, _ = h.shape
    proj = h @ w_in
    offsets, acc = [], 0
    for s in IN_SPLITS[:-1]:
        acc += s
        offsets.append(acc)
    (dn_q, dn_k, dn_v, dn_z, dn_a, dn_b, gl_q, gl_k, gl_v, gl_g, gl_r) = jnp.split(proj, offsets, axis=-1)
    qkv = jax.nn.silu(causal_dwconv(jnp.concatenate([dn_q, dn_k, dn_v], -1), dn_conv))
    q, k, v = (a.reshape(bsz, t, DN_HEADS, DN_HEAD_DIM) for a in jnp.split(qkv, 3, axis=-1))
    log_a = -jnp.exp(dn_a_log) * jax.nn.softplus(dn_a + dn_dt_bias)
    beta = jax.nn.sigmoid(dn_b)
    o_dn = gated_delta_rule(l2_norm(q), l2_norm(k), v, log_a, beta)
    o_dn = rms_norm(o_dn, dn_norm_g) * jax.nn.silu(dn_z.reshape(bsz, t, DN_HEADS, DN_HEAD_DIM))
    log_alpha = jax.nn.log_sigmoid(gl_r @ gla_w_gate2 + gla_b_gate) / GLA_TAU
    o_gla = gla_attention(gl_q.reshape(bsz, t, GLA_HEADS, GLA_KEY_DIM),
                          gl_k.reshape(bsz, t, GLA_HEADS, GLA_KEY_DIM),
                          gl_v.reshape(bsz, t, GLA_HEADS, GLA_VAL_DIM),
                          log_alpha.reshape(bsz, t, GLA_HEADS, GLA_KEY_DIM))
    o_gla = rms_norm(o_gla, gla_norm_g) * jax.nn.silu(gl_g.reshape(bsz, t, GLA_HEADS, GLA_VAL_DIM))
    o = jnp.concatenate([o_dn.reshape(bsz, t, DN_WIDTH), o_gla.reshape(bsz, t, GLA_WIDTH)], axis=-1)
    return o @ w_o

def conv_ffn(h, w_up, conv_w, conv_b, w_down):
    u = causal_dwconv(h @ w_up, conv_w) + conv_b
    gate, val = jnp.split(u, 2, axis=-1)
    return (jax.nn.silu(gate) * val) @ w_down

def second_inputs(seed: int = 0) -> dict:
    key = jax.random.key(seed)
    ks = jax.random.split(key, 24)
    nrm = lambda k, shape, s: jax.random.normal(k, shape, jnp.float32) * s
    L, D = DEPTH, D_MODEL
    dt = jnp.exp(jax.random.uniform(ks[9], (L, DN_HEADS), jnp.float32, math.log(1e-3), math.log(1e-1)))
    return {
        "x": nrm(ks[0], (BATCH, SEQ, D), 1.0),
        "c": nrm(ks[1], (BATCH, D), 1.0),
        "ln0_g": 1.0 + nrm(ks[2], (D,), 0.02),
        "ln0_b": nrm(ks[3], (D,), 0.02),
        "w_ada": nrm(ks[4], (L, D, 6 * D), 0.1 * D ** -0.5),
        "b_ada": nrm(ks[5], (L, 6 * D), 0.01),
        "w_in": nrm(ks[6], (L, D, IN_WIDTH_2), D ** -0.5),
        "dn_conv": nrm(ks[7], (L, SHORT_CONV, 3 * DN_WIDTH), SHORT_CONV ** -0.5),
        "dn_a_log": jnp.log(jax.random.uniform(ks[8], (L, DN_HEADS), jnp.float32, 1.0, 16.0)),
        "dn_dt_bias": dt + jnp.log(-jnp.expm1(-dt)),
        "dn_norm_g": 1.0 + nrm(ks[10], (L, DN_HEAD_DIM), 0.02),
        "gla_w_gate2": nrm(ks[11], (L, GLA_GATE_RANK, GLA_HEADS * GLA_KEY_DIM), GLA_GATE_RANK ** -0.5),
        "gla_b_gate": nrm(ks[12], (L, GLA_HEADS * GLA_KEY_DIM), 0.01),
        "gla_norm_g": 1.0 + nrm(ks[13], (L, GLA_VAL_DIM), 0.02),
        "w_o": nrm(ks[14], (L, MIX_WIDTH, D), MIX_WIDTH ** -0.5 * BETA_INIT),
        "ln1_g": 1.0 + nrm(ks[15], (L, D), 0.02),
        "ln1_b": nrm(ks[16], (L, D), 0.02),
        "ffn_w_up": nrm(ks[17], (L, D, 2 * D_FF), D ** -0.5),
        "ffn_conv": nrm(ks[18], (L, FFN_CONV, 2 * D_FF), FFN_CONV ** -0.5),
        "ffn_conv_b": nrm(ks[19], (L, 2 * D_FF), 0.02),
        "ffn_w_down": nrm(ks[20], (L, D_FF, D), D_FF ** -0.5 * BETA_INIT),
        "ln2_g": 1.0 + nrm(ks[21], (L, D), 0.02),
        "ln2_b": nrm(ks[22], (L, D), 0.02),
    }

def second_block(x, c, ln0_g, ln0_b, w_ada, b_ada, w_in, dn_conv, dn_a_log, dn_dt_bias, dn_norm_g,
              gla_w_gate2, gla_b_gate, gla_norm_g, w_o, ln1_g, ln1_b, ffn_w_up, ffn_conv, ffn_conv_b,
              ffn_w_down, ln2_g, ln2_b):
    x = layer_norm(x, ln0_g, ln0_b)
    cond = jax.nn.silu(c)
    for l in range(DEPTH):
        mod = cond @ w_ada[l] + b_ada[l]
        sh_a, sc_a, gt_a, sh_f, sc_f, gt_f = jnp.split(mod[:, None, :], 6, axis=-1)
        h = x * (1.0 + sc_a) + sh_a
        y = hybrid_mixer(h, w_in[l], dn_conv[l], dn_a_log[l], dn_dt_bias[l], dn_norm_g[l],
                         gla_w_gate2[l], gla_b_gate[l], gla_norm_g[l], w_o[l])
        x = layer_norm(ALPHA * x + (1.0 + gt_a) * y, ln1_g[l], ln1_b[l])
        h = x * (1.0 + sc_f) + sh_f
        y = conv_ffn(h, ffn_w_up[l], ffn_conv[l], ffn_conv_b[l], ffn_w_down[l])
        x = layer_norm(ALPHA * x + (1.0 + gt_f) * y, ln2_g[l], ln2_b[l])
    return x


_first_inputs = second_inputs


def second_inputs(seed=0):
    import zlib

    import numpy as np

    out = dict(_first_inputs(seed))
    spreads = {}
    factors = {'b_ada': 5.024,
     'dn_norm_g': 8.0,
     'gla_b_gate': 8.0,
     'gla_norm_g': 8.0,
     'ln1_g': 2.74,
     'ln1_b': 2.749,
     'ffn_conv_b': 7.006,
     'ln2_g': 2.742,
     'ln2_b': 2.828}
    for name, (base, spread) in spreads.items():
        noise = np.random.default_rng([zlib.crc32(name.encode()), seed]).standard_normal(out[name].shape)
        drawn = base * np.exp(spread * noise) if base else spread * noise
        out[name] = __import__('jax').numpy.asarray(drawn.astype(out[name].dtype))
    for name, factor in factors.items():
        out[name] = (out[name] * factor).astype(out[name].dtype)
    return out


_narrow_inputs = second_inputs


def second_inputs(seed=0):

    out = dict(_narrow_inputs(seed))
    wider = {'dn_norm_g': 3.54, 'gla_norm_g': 3.88, 'ln2_g': 3.06, 'ln2_b': 3.08}
    for name, times in wider.items():
        mean = out[name].mean()
        out[name] = (mean + times * (out[name] - mean)).astype(out[name].dtype)
    return out


def setup_inputs(seed=0):
    out = dict(first_inputs(seed))
    for name, value in second_inputs(seed + 1).items():
        if name != "x":
            out[name + "_2"] = value
    return out


def reference(
    x, attn_norm_g, w_in, pool_w, pool_scale, rel_bias, s5_a_re, s5_a_im, s5_log_dt, s5_b_re,
    s5_b_im, s5_c_re, s5_c_im, s5_d, s5_w_glu, w_branch, w_gate, w_out, ffn_norm_g, w_up,
    w_down, final_norm_g, c_2, ln0_g_2, ln0_b_2, w_ada_2, b_ada_2, w_in_2, dn_conv_2,
    dn_a_log_2, dn_dt_bias_2, dn_norm_g_2, gla_w_gate2_2, gla_b_gate_2, gla_norm_g_2, w_o_2,
    ln1_g_2, ln1_b_2, ffn_w_up_2, ffn_conv_2, ffn_conv_b_2, ffn_w_down_2, ln2_g_2, ln2_b_2,
):
    x = first_block(
        x, attn_norm_g, w_in, pool_w, pool_scale, rel_bias, s5_a_re, s5_a_im, s5_log_dt,
        s5_b_re, s5_b_im, s5_c_re, s5_c_im, s5_d, s5_w_glu, w_branch, w_gate, w_out, ffn_norm_g,
        w_up, w_down, final_norm_g,
    )
    return second_block(
        x, c_2, ln0_g_2, ln0_b_2, w_ada_2, b_ada_2, w_in_2, dn_conv_2, dn_a_log_2, dn_dt_bias_2,
        dn_norm_g_2, gla_w_gate2_2, gla_b_gate_2, gla_norm_g_2, w_o_2, ln1_g_2, ln1_b_2,
        ffn_w_up_2, ffn_conv_2, ffn_conv_b_2, ffn_w_down_2, ln2_g_2, ln2_b_2,
    )


_drawn_inputs = setup_inputs


def setup_inputs(seed=0):
    import zlib

    import numpy as np

    out = dict(_drawn_inputs(seed))
    spreads = {}
    factors = {'pool_scale': 3.018,
     's5_a_re': 200.0,
     's5_a_im': 62.72,
     's5_log_dt': 64.0,
     's5_b_re': 64.0,
     's5_b_im': 64.0,
     's5_c_re': 64.0,
     's5_c_im': 64.0,
     'ffn_norm_g': 2.955}
    for name, (base, spread) in spreads.items():
        noise = np.random.default_rng([zlib.crc32(name.encode()), seed]).standard_normal(out[name].shape)
        drawn = base * np.exp(spread * noise) if base else spread * noise
        out[name] = jnp.asarray(drawn.astype(out[name].dtype))
    for name, factor in factors.items():
        out[name] = (out[name] * factor).astype(out[name].dtype)
    return out
```

```python
import math

import numpy as np

import concourse.bass as bass
from concourse import mybir
from concourse.alu_op_type import AluOpType as ALU

F32 = mybir.dt.float32
F32R = mybir.dt.float32r
I32 = mybir.dt.int32
ACT = mybir.ActivationFunctionType
AXX = mybir.AxisListType.X

T = 1024
NEG = -1.0e30
EPS = 1e-6
ALPHA = 2.0 ** 0.25
MAGIC = 12582912.0
FFN_CUT = (6, 6, 5, 5)
DILS = (1, 4, 16)
HN_ = (0, 2, 1, 3)

VCOLS = {}
_at = 0
for _n, _w in (("attn_g", 8), ("ffn_g", 8), ("fin_g", 8), ("ln0_g", 8), ("ln0_b", 8), ("ln1_g", 8), ("ln1_b", 8),
               ("ln2_g", 8), ("ln2_b", 8), ("pool_s", 4), ("s5_d", 4), ("c", 8), ("b_ada", 48), ("conv", 48),
               ("dn_g", 1), ("gla_bg", 2), ("gla_g", 1), ("fconv", 132), ("fconv_b", 44), ("alog", 4), ("dtb", 4),
               ("a_re", 16), ("a_im", 16), ("ldt", 16)):
    VCOLS[_n] = (_at, _w)
    _at += _w
NV = _at


def t5_buckets(dil):
    dist = np.arange(129) * dil
    df = np.maximum(dist, 1).astype(np.float32)
    large = 16 + (np.log(df / np.float32(16)) / np.float32(math.log(2048 / 16)) * np.float32(16)).astype(np.int32)
    large = np.minimum(large, 31)
    return np.where(dist < 16, dist, large)


def shape_constants():
    c = {}
    i = np.arange(128)
    c["ident"] = np.eye(128, dtype=np.float32)
    c["upper"] = (i[:, None] <= i[None, :]).astype(np.float32)
    c["negU"] = -(i[:, None] >= i[None, :]).astype(np.float32)
    c["mS"] = np.where(i[:, None] > i[None, :], 0.0, NEG).astype(np.float32)
    c["mT"] = np.where(i[:, None] <= i[None, :], 0.0, NEG).astype(np.float32)
    lev = np.zeros((7, 128, 128), np.float32)
    for l in range(7):
        s = 1 << l
        lev[l] = ((i[:, None] // s) % 2 == 1) & ((i[None, :] // s) == (i[:, None] // s) - 1)
    c["lev"] = np.ascontiguousarray(lev.transpose(1, 0, 2)).reshape(128, 896)
    c["mG"] = ((i[:, None] <= i[None, :]) & (i[:, None] // 64 == i[None, :] // 64)).astype(np.float32)
    c["scanm"] = np.broadcast_to((np.arange(T) % 64 != 0).astype(np.float32), (128, T))
    c["tpos"] = np.broadcast_to(np.arange(T, dtype=np.float32), (128, T))
    cnt = np.zeros((128, 4, 16), np.float32)
    for g, w in enumerate((2, 4, 8, 16)):
        cnt[:, g, :] = np.float32(1.0) / np.minimum(np.arange(16) + 1, w).astype(np.float32)
    c["cnt"] = cnt.reshape(128, 64)
    hot = np.zeros((32, 3, 384), np.float32)
    pen = np.full((128, 3, 384), NEG, np.float32)
    for g, d in enumerate(DILS):
        b = t5_buckets(d)
        for dist in range(129):
            hot[b[dist], g, dist + 127] = 1.0
            pen[:, g, dist + 127] = 0.0
    c["hot"] = np.concatenate([hot.reshape(32, 1152), np.zeros((96, 1152), np.float32)])
    c["pen"] = pen.reshape(128, 1152)[0:4]
    blk = np.where(i[:, None] // 64 == i[None, :] // 64, 0.0, NEG).astype(np.float32)
    c["blk"] = blk
    return {k: np.ascontiguousarray(v) for k, v in c.items()}


CONST_SHAPES = {k: v.shape for k, v in shape_constants().items()}


class Tok:
    __slots__ = ("q", "sig", "val", "sem")

    def __init__(self, q):
        self.q, self.sig, self.val, self.sem = q, False, 0, None


def points(w):
    if w is None:
        return []
    if isinstance(w, Tok):
        return [w]
    return [t for x in w for t in points(x)]


class Lane:

    def __init__(self, sem):
        self.sem, self.n = sem, 0

    def next(self):
        self.n += 16
        return self.sem, self.n


class Noted:

    def activation(self, *a, **k):
        return lambda e: e.activation(*a, **k)

    def affine_select(self, *a, **k):
        return lambda e: e.affine_select(*a, **k)

    def copy(self, *a, **k):
        return lambda e: e.copy(*a, **k)

    def dma_start(self, *a, **k):
        return lambda e: e.dma_start(*a, **k)

    def matmul(self, *a, **k):
        return lambda e: e.matmul(*a, **k)

    def memset(self, *a, **k):
        return lambda e: e.memset(*a, **k)

    def mul(self, *a, **k):
        return lambda e: e.mul(*a, **k)

    def preload_act_table_set(self, *a, **k):
        return lambda e: e.preload_act_table_set(*a, **k)

    def reciprocal(self, *a, **k):
        return lambda e: e.reciprocal(*a, **k)

    def scalar_tensor_tensor(self, *a, **k):
        return lambda e: e.scalar_tensor_tensor(*a, **k)

    def tensor_copy(self, *a, **k):
        return lambda e: e.tensor_copy(*a, **k)

    def tensor_reduce(self, *a, **k):
        return lambda e: e.tensor_reduce(*a, **k)

    def tensor_scalar(self, *a, **k):
        return lambda e: e.tensor_scalar(*a, **k)

    def tensor_tensor(self, *a, **k):
        return lambda e: e.tensor_tensor(*a, **k)

    def tensor_tensor_scan(self, *a, **k):
        return lambda e: e.tensor_tensor_scan(*a, **k)

    def transpose(self, *a, **k):
        return lambda e: e.transpose(*a, **k)


NOTED = Noted()


class Queue:

    def __init__(self, name, sem):
        self.name, self.sem, self.ops, self.extra, self.last = name, sem, [], [], None

    def op(self, fn, *waits):
        t = Tok(self)
        flat = points(self.extra) + points(waits)
        self.extra = []
        call = fn(NOTED) if fn is not None else None
        self.ops.append((t, flat, call, None))
        self.last = t
        return t

    def dma(self, sem, val, fn, *waits):
        t = self.op(fn, *waits)
        t.sem, t.val = sem, val
        tt, w, f, _ = self.ops.pop()
        self.ops.append((tt, w, f, sem))
        return t

    def mark(self):
        for _, waits, _, _ in self.ops:
            for w in waits:
                w.sig = True

    def number(self):
        n = 0
        for t, _, _, dsem in self.ops:
            if dsem is None and t.sig:
                n += 1
                t.sem, t.val = self.sem, n

    def emit(self, eng):
        seen = {}
        for t, waits, fn, dsem in self.ops:
            need = {}
            for w in waits:
                k = id(w.sem)
                if k not in need or need[k][1] < w.val:
                    need[k] = (w.sem, w.val)
            for k, (sem, val) in need.items():
                if seen.get(k, 0) < val:
                    eng.wait_ge(sem, val)
                    seen[k] = val
            if fn is None:
                continue
            ins = fn(eng)
            if dsem is not None:
                ins.then_inc(dsem, 16)
            elif t.sig:
                ins.then_inc(t.sem, 1)


class Buf:

    def __init__(self, ap):
        self.ap, self.free = ap, []


class Rot:
    def __init__(self, aps):
        self.bufs, self.n = [a if isinstance(a, Buf) else Buf(a) for a in aps], 0

    def take(self):
        b = self.bufs[self.n % len(self.bufs)]
        self.n += 1
        return b


def weight_plan():
    plan = []

    def tiles(name, fts, kt, k0=0):
        for ft in fts:
            plan.append((name, ft, k0, kt))

    def merge(b, kt):
        for ft in range(8):
            plan.append(("w_gate", b * 8 + ft, 0, 8))
            plan.append((f"w_br{b}", ft, 0, kt))

    tiles("w_in", range(34, 38), 8)
    tiles("w_glu", [x for i in range(4) for x in (i, i + 4)], 4)
    merge(3, 4)
    tiles("w_in", range(0, 4), 8)
    merge(0, 4)
    for g in range(3):
        tiles("w_in", [4 + 2 * g, 5 + 2 * g, 10 + 2 * g, 11 + 2 * g, 16 + 2 * g, 17 + 2 * g], 8)
    merge(1, 2)
    for h in range(4):
        tiles("w_in", [22 + h, 26 + h, 30 + h], 8)
    merge(2, 4)
    tiles("w_out", range(8), 8)
    k0 = 0
    for n in FFN_CUT:
        tiles("w_up", [x for i in range(k0, k0 + n) for x in (i, i + 22)], 8)
        tiles("w_down", range(8), n, k0)
        k0 += n
    tiles("w_in2", [28], 8)
    for hp in range(2):
        for h in (2 * hp, 2 * hp + 1):
            tiles("w_in2", [h, 4 + h, 8 + h, 12 + h], 8)
    for hp in range(2):
        tiles("w_in2", [16 + hp, 18 + hp], 8)
        tiles("w_in2", [20 + 2 * hp, 21 + 2 * hp, 24 + 2 * hp, 25 + 2 * hp], 8)
    tiles("w_o", range(8), 8)
    k0 = 0
    for n in FFN_CUT:
        tiles("w_up2", [x for i in range(k0, k0 + n) for x in (i, i + 22)], 8)
        tiles("w_down2", range(8), n, k0)
        k0 += n
    return plan


def build(nc, A, out, scr, spill, bsc, dump=None):
    from contextlib import ExitStack
    ctx = ExitStack()
    with ctx:
        sem_n = [0]

        def new_sem():
            sem_n[0] += 1
            return ctx.enter_context(nc.semaphore(f"s{sem_n[0]}"))

        pe, act, dve, pool, sp = (Queue(n, new_sem()) for n in ("pe", "act", "dve", "pool", "sp"))

        top = [(nc.sbuf_base + 63) // 64 * 64]
        high = [0]
        names = [0]

        def sb(shape, dt=F32):
            n = 4
            for s in shape[1:]:
                n *= s
            names[0] += 1
            h = nc.alloc_sbuf_tensor_at(f"t{names[0]}", list(shape), dt, offset=top[0])
            top[0] += (n + 63) // 64 * 64
            high[0] = max(high[0], top[0])
            return h[tuple(slice(None) for _ in shape)]

        PS = ctx.enter_context(nc.psum_tensor("PS", [128, 8, 512], F32))
        banks = [PS[:, i, :] for i in range(8)]
        pairs = [PS[:, 2 * i:2 * i + 2, :].rearrange("p a b -> p (a b)") for i in range(4)]

        dumps = []

        phase = [[]]
        open_dma = []

        def dma(q, o, i, *waits, lane=None):
            sem, val = lane.next() if lane else (new_sem(), 16)
            return q.dma(sem, val, lambda e: e.dma_start(o, i), phase[0], *waits)

        def lanes(n):
            return [Lane(new_sem()) for _ in range(n)]

        def barrier():
            toks = [q.last for q in (pe, act, dve, pool) if q.last is not None] + open_dma
            for q in (pe, act, dve, pool):
                q.extra = q.extra + toks
            phase[0] = list(toks)
            del open_dma[:]
            return toks

        def probe(name, ap, *waits):
            if dump is not None and name in dump:
                t = dma(sp, dump[name], ap, *waits)
                dumps.append(t)
                open_dma.append(t)

        V = sb([128, NV])
        v_tok = dma(sp, V, A["vecs"])

        def vec(name, i=0, n=1):
            a = VCOLS[name][0]
            return V[:, a + i:a + i + n]

        C = {}
        c_tok = {}

        def const(name):
            C[name] = sb(list(CONST_SHAPES[name]))
            c_tok[name] = dma(sp, C[name], A["c_" + name])
            return C[name], c_tok[name]

        ident, id_tok = const("ident")
        ones = sb([128, 128])
        epsc = sb([128, 1])
        o_tok = dve.op(lambda e: e.memset(ones, 1.0))
        e_tok = dve.op(lambda e: e.memset(epsc, EPS))

        plan = weight_plan()
        RAW, SPL, AHEAD = 3, 3, 2
        raws = [sb([128, 8, 128]) for _ in range(RAW)]
        whis = [sb([128, 8, 128], F32R) for _ in range(SPL)]
        wlos = [sb([128, 8, 128], F32R) for _ in range(SPL)]
        raw_sem = [new_sem() for _ in range(RAW)]
        raw_free = [[] for _ in range(RAW)]
        spl_free = [[] for _ in range(SPL)]
        w_dma, w_ready, w_at = {}, {}, [0, 0, 0]

        def w_load(i):
            name, ft, k0, kt = plan[i]
            s = i % RAW
            src = A[name][ft, :, k0:k0 + kt, :]
            w_dma[i] = sp.dma(raw_sem[s], 16 * (i // RAW + 1), lambda e: e.dma_start(raws[s][:, 0:kt, :], src), raw_free[s])

        def w_split(i):
            name, ft, k0, kt = plan[i]
            s, r = i % SPL, i % RAW
            if i == 0:
                for n in range(RAW):
                    w_load(n)
            a = act.op(lambda e: e.copy(whis[s][:, 0:kt, :], raws[r][:, 0:kt, :]), w_dma[i], spl_free[s])
            d = dve.op(lambda e: e.tensor_tensor(wlos[s][:, 0:kt, :], raws[r][:, 0:kt, :],
                                                 whis[s][:, 0:kt, :].bitcast(F32), ALU.subtract), a, w_dma[i], spl_free[s])
            raw_free[r] = [a, d]
            if i + RAW < len(plan):
                w_load(i + RAW)
            w_ready[i] = [a, d]

        def w_next(name, ft, k0=0):
            i = w_at[2]
            assert plan[i][:3] == (name, ft, k0), (plan[i], name, ft, k0)
            w_at[2] += 1
            while w_at[1] <= min(i + AHEAD, len(plan) - 1):
                w_split(w_at[1])
                w_at[1] += 1
            return i

        pbufs = [Buf(p) for p in pairs]
        mmps = Rot(pbufs[0:3])

        def product(name, ft, xs, evac, k0=0):
            i = w_next(name, ft, k0)
            s, kt = i % SPL, plan[i][3]
            assert kt == len(xs)
            b = mmps.take()
            ps = b.ap
            t = None
            for k in range(kt):
                hi, lo, rdy = xs[k]
                steps = [(whis, hi), (whis, lo), (wlos, hi)]
                for n, (w, x) in enumerate(steps):
                    for h in range(2):
                        def f(e, w=w, x=x, h=h, k=k, n=n):
                            return e.matmul(ps[:, h * 512:(h + 1) * 512], w[s][:, k, :], x[:, h * 512:(h + 1) * 512],
                                            start=(k == 0 and n == 0), stop=(k == kt - 1 and n == 2))
                        t = pe.op(f, (b.free + w_ready[i]) if k == 0 and n == 0 else None, rdy if n == 0 else None)
            spl_free[s] = [t]
            b.free = evac(ps, t)
            return b.free

        def split(dst, src, *waits):
            a = act.op(lambda e: e.copy(dst[0], src), *waits)
            d = dve.op(lambda e: e.tensor_tensor(dst[1], src, dst[0].bitcast(F32), ALU.subtract), a, *waits)
            return [a, d]

        def ones_sum(tiles, ps, free):
            t, n = None, len(tiles)
            out_t = []
            for k, (x, r) in enumerate(tiles):
                for h in range(2):
                    t = pe.op(lambda e, x=x, h=h, k=k: e.matmul(ps[:, h * 512:(h + 1) * 512], ones, x[:, h * 512:(h + 1) * 512],
                                                              start=(k == 0), stop=(k == n - 1)), free if k == 0 else None, r, o_tok)
                out_t.append(t)
            return out_t

        def mean_square_inv(tiles, n, tmp, dst, ps_buf, dst_free=None):
            sq = []
            ps = ps_buf.ap
            toks = []
            for k, (x, r) in enumerate(tiles):
                b = tmp.take()
                a = act.op(lambda e, b=b, x=x: e.activation(b.ap, x, ACT.Square), r, b.free)
                for h in range(2):
                    t = pe.op(lambda e, b=b, h=h, k=k: e.matmul(ps[:, h * 512:(h + 1) * 512], ones, b.ap[:, h * 512:(h + 1) * 512],
                                                                start=(k == 0), stop=(k == len(tiles) - 1)), a, ps_buf.free if k == 0 else None, o_tok)
                b.free = [t]
            a = act.op(lambda e: e.activation(dst, ps, ACT.Sqrt, scale=1.0 / n, bias=epsc), t, e_tok, dst_free)
            ps_buf.free = [a]
            return dve.op(lambda e: e.reciprocal(dst, dst), a)

        def rms_split(X, rdy, gname, dst, tmp, rstd):
            pb = mmps.take()
            r = mean_square_inv([(X[:, k, :], rdy[k]) for k in range(8)], T, tmp, rstd, pb)
            res = []
            for k in range(8):
                b = tmp.take()
                d = dve.op(lambda e, b=b, k=k: e.scalar_tensor_tensor(b.ap, X[:, k, :], vec(gname, k), rstd, ALU.mult, ALU.mult),
                           r, b.free, v_tok)
                rr = split((dst[0][:, k, :], dst[1][:, k, :]), b.ap, d)
                b.free = rr
                res.append(rr)
            return res

        def layer_norm(X, rdy, g, bname, tmp, mu, rstd):
            pb = mmps.take()
            t = ones_sum([(X[:, k, :], rdy[k]) for k in range(8)], pb.ap, pb.free)[-1]
            m = dve.op(lambda e: e.tensor_scalar(mu, pb.ap, 1.0 / T, None, ALU.mult), t)
            pb.free = [m]
            xc = [dve.op(lambda e, k=k: e.tensor_tensor(X[:, k, :], X[:, k, :], mu, ALU.subtract), m, rdy[k], t) for k in range(8)]
            pb = mmps.take()
            r = mean_square_inv([(X[:, k, :], [xc[k]]) for k in range(8)], T, tmp, rstd, pb)
            res = []
            for k in range(8):
                d = dve.op(lambda e, k=k: e.scalar_tensor_tensor(X[:, k, :], X[:, k, :], vec(g, k), rstd, ALU.mult, ALU.mult), r, v_tok)
                res.append([act.op(lambda e, k=k: e.activation(X[:, k, :], X[:, k, :], ACT.Identity, bias=vec(bname, k)), d, v_tok)])
            return res

        def transposes(src, dst_evac, n, ready, ps_buf):
            t = None
            for j in range(n):
                t = pe.op(lambda e, j=j: e.transpose(ps_buf.ap[:, j * 128:(j + 1) * 128], src[:, j * 128:(j + 1) * 128], ident),
                          ready if j == 0 else None, ps_buf.free if j == 0 else None, id_tok)
            ps_buf.free = dst_evac(ps_buf.ap, t)
            return ps_buf.free

        base0 = top[0]
        XH = (sb([128, 8, T], F32R), sb([128, 8, T], F32R))
        base_x = top[0]

        def bias_rows():
            hot, h_t = const("hot")
            pen, p_t = const("pen")
            rb = sb([128, 12])
            rb_t = dma(sp, rb, A["rel_bias"])
            wr = []
            brow = sb([4, 3, 384])
            for g in range(3):
                b = mmps.take()
                t = pe.op(lambda e, b=b, g=g: e.matmul(b.ap[0:4, 0:384], rb[:, 4 * g:4 * g + 4], hot[:, 384 * g:384 * g + 384],
                                                       start=True, stop=True), h_t, rb_t, b.free)
                d = dve.op(lambda e, b=b, g=g: e.tensor_tensor(brow[:, g, :], b.ap[0:4, 0:384], pen[:, 384 * g:384 * g + 384], ALU.add), t, p_t)
                b.free = [d]
                wr.append(d)
            bs_t = dma(sp, bsc, brow, wr)
            return bs_t

        X = sb([128, 8, T])
        tmp = Rot([sb([128, T]) for _ in range(2)])
        rstd = sb([128, T])
        lane8 = lanes(8)
        x_tok = [[dma(sp, X[:, k, :], A["xT"][:, k, :], lane=lane8[k])] for k in range(8)]
        bs_t = bias_rows()
        xn = rms_split(X, x_tok, "attn_g", XH, tmp, rstd)
        XN = [(XH[0][:, k, :], XH[1][:, k, :], xn[k]) for k in range(8)]
        top[0] = base_x

        merged = sb([128, 8, T])
        m_tok = [None] * 8
        y_addr = top[0]
        Y = (sb([128, 4, T], F32R), sb([128, 4, T], F32R))
        base_y = top[0]
        first_merge = [True]

        def merge(b, kt, ytok):
            barrier()
            mark = top[0]
            sg = Rot([sb([128, T]) for _ in range(2)])
            ys = [(Y[0][:, k, :], Y[1][:, k, :], ytok[k]) for k in range(kt)]
            for ft in range(8):
                g = sg.take()

                def gate(ps, t):
                    return [act.op(lambda e: e.activation(g.ap, ps, ACT.Sigmoid), t, g.free)]

                gt = product("w_gate", b * 8 + ft, XN, gate)

                def br(ps, t):
                    if first_merge[0]:
                        d = dve.op(lambda e: e.tensor_tensor(merged[:, ft, :], ps, g.ap, ALU.mult), t, gt)
                        g.free = [d]
                        m_tok[ft] = [d]
                        return [d]
                    d = dve.op(lambda e: e.tensor_tensor(g.ap, ps, g.ap, ALU.mult), t, gt)
                    d2 = dve.op(lambda e: e.tensor_tensor(merged[:, ft, :], merged[:, ft, :], g.ap, ALU.add), d, m_tok[ft])
                    g.free = [d2]
                    m_tok[ft] = [d2]
                    return [d]

                product(f"w_br{b}", ft, ys, br)
            first_merge[0] = False
            barrier()
            top[0] = mark

        def s5():
            U = sb([128, 4, T])
            ut = []
            for i in range(4):
                ut.append(product("w_in", 34 + i, XN, lambda ps, t, i=i: [act.op(lambda e: e.copy(U[:, i, :], ps), t)]))
            W = [sb([128, 16]) for _ in range(14)]
            WI = sb([128, 16], I32)
            last = [v_tok]

            def d(fn):
                last[0] = dve.op(fn, last[0])
                return last[0]

            def ts(o, i, s1, s2, op0, op1=None):
                if s2 is None:
                    return d(lambda e: e.tensor_scalar(o, i, s1, None, op0))
                return d(lambda e: e.tensor_scalar(o, i, s1, s2, op0, op1))

            def tt(o, a, b, op):
                return d(lambda e: e.tensor_tensor(o, a, b, op))

            def stt(o, a, s, b, op0, op1):
                return d(lambda e: e.scalar_tensor_tensor(o, a, s, b, op0, op1))

            def exact_exp(o, x, k, r, q):
                ts(r, x, -87.5, 88.9, ALU.max, ALU.min)
                ts(k, r, 1.4426950408889634, MAGIC, ALU.mult, ALU.add)
                ts(k, k, MAGIC, None, ALU.subtract)
                stt(r, k, -0.693359375, r, ALU.mult, ALU.add)
                stt(r, k, 2.12194440054690583e-4, r, ALU.mult, ALU.add)
                ts(q, r, 1.0 / 5040, 1.0 / 720, ALU.mult, ALU.add)
                for cf in (1.0 / 120, 1.0 / 24, 1.0 / 6, 0.5, 1.0, 1.0):
                    tt(q, q, r, ALU.mult)
                    ts(q, q, cf, None, ALU.add)
                ts(k, k, 126.0, 8388608.0, ALU.add, ALU.mult)
                d(lambda e: e.tensor_copy(WI, k))
                stt(o, q, 2.0, WI.bitcast(F32), ALU.mult, ALU.mult)
                ts(k, x, -87.3, None, ALU.is_ge)
                tt(o, o, k, ALU.mult)

            ar, ai = vec("a_re", 0, 16), vec("a_im", 0, 16)
            dt_, mag, th, t1, t2, t3, co, si, cr, ci, tau, t4, nr, ni = W
            exact_exp(dt_, vec("ldt", 0, 16), t1, t2, t3)
            tt(t4, ar, dt_, ALU.mult)
            exact_exp(mag, t4, t1, t2, t3)
            tt(th, ai, dt_, ALU.mult)
            ts(t1, th, 1.0 / (2 * math.pi), MAGIC, ALU.mult, ALU.add)
            ts(t1, t1, MAGIC, None, ALU.subtract)
            c1 = 6.28125
            c2 = float(np.float32(np.round((2 * math.pi - c1) * 2 ** 18) / 2 ** 18))
            c3 = 2 * math.pi - c1 - c2
            stt(th, t1, -c1, th, ALU.mult, ALU.add)
            stt(th, t1, -c2, th, ALU.mult, ALU.add)
            stt(th, t1, -c3, th, ALU.mult, ALU.add)
            ts(tau, th, 1.0 / (2 * math.pi), None, ALU.mult)
            ts(t1, th, 0.25, None, ALU.mult)
            tt(t2, t1, t1, ALU.mult)
            ts(t3, t2, 1.0 / 362880, -1.0 / 5040, ALU.mult, ALU.add)
            for cf in (1.0 / 120, -1.0 / 6, 1.0):
                tt(t3, t3, t2, ALU.mult)
                ts(t3, t3, cf, None, ALU.add)
            tt(si, t3, t1, ALU.mult)
            ts(t3, t2, -1.0 / 3628800, 1.0 / 40320, ALU.mult, ALU.add)
            for cf in (-1.0 / 720, 1.0 / 24, -0.5, 1.0):
                tt(t3, t3, t2, ALU.mult)
                ts(t3, t3, cf, None, ALU.add)
            d(lambda e: e.tensor_copy(co, t3))
            for _ in range(2):
                tt(t1, si, si, ALU.mult)
                stt(si, si, 2.0, co, ALU.mult, ALU.mult)
                ts(co, t1, -2.0, 1.0, ALU.mult, ALU.add)
            tt(nr, mag, co, ALU.mult)
            ts(nr, nr, -1.0, None, ALU.add)
            tt(ni, mag, si, ALU.mult)
            tt(t1, ar, ar, ALU.mult)
            tt(t2, ai, ai, ALU.mult)
            tt(t1, t1, t2, ALU.add)
            d(lambda e: e.reciprocal(t1, t1))
            tt(cr, nr, ar, ALU.mult)
            tt(t2, ni, ai, ALU.mult)
            tt(cr, cr, t2, ALU.add)
            tt(cr, cr, t1, ALU.mult)
            tt(ci, ni, ar, ALU.mult)
            tt(t2, nr, ai, ALU.mult)
            tt(ci, ci, t2, ALU.subtract)
            tt(ci, ci, t1, ALU.mult)
            probe("s5c", cr, last[0])
            keep = top[0]
            top[0] = y_addr
            BC = sb([128, 4, 256])
            bct = dma(sp, BC, A["s5bc"])
            tpos = sb([128, T])
            tp_tok = dma(sp, tpos, A["c_tpos"])
            big = [sb([128, T]) for _ in range(5)]
            assert top[0] <= base_y
            top[0] = keep
            sgl = Rot([sb([128, T]) for _ in range(2)])
            bz = [sb([128, 128]) for _ in range(2)]
            cz = [[sb([128, 128]) for _ in range(2)] for _ in range(2)]
            bT = [sb([128, 128]) for _ in range(2)]
            prev_tail = []
            yt = []
            yps = Buf(pairs[3])
            bups = [Buf(pairs[1]), Buf(pairs[2])]
            bups[0].free, bups[1].free = list(mmps.bufs[1].free), list(mmps.bufs[2].free)
            tps = Buf(pairs[0])
            tps.free = list(mmps.bufs[0].free)
            cz_free = [[], []]
            tail = [last[0]]
            for i in range(16):
                j, f = i % 4, i // 4
                par = i % 2
                z = []
                for m in (bz[0], bz[1], cz[par][0], cz[par][1]):
                    z.append(dve.op(lambda e, m=m: e.memset(m, 0.0), tail, cz_free[par]))
                bt = []
                for gl in range(2):
                    rows = slice(64 * gl, 64 * gl + 64)
                    cols = slice(32 * j + 16 * gl, 32 * j + 16 * gl + 16)
                    src = [BC[rows, n, 16 * i:16 * i + 16] for n in range(4)]
                    for n, (a, b_, op) in enumerate(((0, 1, ALU.subtract), (1, 0, ALU.add))):
                        m = bz[n]
                        u1 = dve.op(lambda e, m=m, b_=b_: e.tensor_scalar(m[rows, cols], src[b_], ci[rows, i:i + 1], None, ALU.mult),
                                    z, bct, last[0])
                        sc = cr
                        bt.append(dve.op(lambda e, m=m, a=a, op=op: e.scalar_tensor_tensor(
                            m[rows, cols], src[a], cr[rows, i:i + 1], m[rows, cols], ALU.mult, op), u1))
                    bt.append(dve.op(lambda e: e.tensor_copy(cz[par][0][rows, cols], src[2]), z))
                    bt.append(dve.op(lambda e: e.tensor_scalar(cz[par][1][rows, cols], src[3], -1.0, None, ALU.mult), z))
                t = None
                for n in range(2):
                    t = pe.op(lambda e, n=n: e.transpose(tps.ap[:, n * 128:(n + 1) * 128], bz[n], ident), bt, tps.free, id_tok)
                tb = [act.op(lambda e, n=n: e.copy(bT[n], tps.ap[:, n * 128:(n + 1) * 128]), t, prev_tail) for n in range(2)]
                tps.free = tb
                bu = []
                for n in range(2):
                    for h in range(2):
                        bu.append(pe.op(lambda e, n=n, h=h: e.matmul(bups[n].ap[:, h * 512:(h + 1) * 512], bT[n],
                                                                     U[:, f, h * 512:(h + 1) * 512], start=True, stop=True),
                                        tb, ut[f], bups[n].free))
                prev_tail = [bu[-1]]
                S, Cc, P, Q, R = big
                q = dve.op(lambda e: e.tensor_scalar(P, tpos, tau[:, i:i + 1], None, ALU.mult), tail, tp_tok)
                k1 = dve.op(lambda e: e.tensor_scalar(Q, P, MAGIC, MAGIC, ALU.add, ALU.subtract), q)
                k2 = dve.op(lambda e: e.tensor_tensor(Q, P, Q, ALU.subtract), k1)
                s_t = act.op(lambda e: e.activation(S, Q, ACT.Sin, scale=2 * math.pi), k2)
                k3 = dve.op(lambda e: e.tensor_scalar(P, P, 0.25, None, ALU.add), k2)
                k4 = dve.op(lambda e: e.tensor_scalar(R, P, MAGIC, MAGIC, ALU.add, ALU.subtract), k3)
                k5 = dve.op(lambda e: e.tensor_tensor(R, P, R, ALU.subtract), k4)
                c_t = act.op(lambda e: e.activation(Cc, R, ACT.Sin, scale=2 * math.pi), k5)
                br, bi = bups[0].ap, bups[1].ap
                a1 = dve.op(lambda e: e.tensor_tensor(P, Cc, br, ALU.mult), bu, c_t, s_t)
                a2 = dve.op(lambda e: e.tensor_tensor(R, S, bi, ALU.mult), c_t)
                a3 = dve.op(lambda e: e.tensor_tensor(P, P, R, ALU.add), a1, a2)
                a4 = dve.op(lambda e: e.tensor_tensor(Q, Cc, bi, ALU.mult), s_t)
                a5 = dve.op(lambda e: e.tensor_tensor(R, S, br, ALU.mult), a3)
                a6 = dve.op(lambda e: e.tensor_tensor(Q, Q, R, ALU.subtract), a4, a5)
                bups[0].free = [a5]
                bups[1].free = [a5]
                rb = mag[:, i:i + 1].to_broadcast([128, T])
                g1 = dve.op(lambda e: e.tensor_tensor_scan(P, rb, P, 0.0, ALU.mult, ALU.add), a3)
                g2 = dve.op(lambda e: e.tensor_tensor_scan(Q, rb, Q, 0.0, ALU.mult, ALU.add), a6)
                b1 = dve.op(lambda e: e.tensor_tensor(R, S, Q, ALU.mult), g2)
                b2 = dve.op(lambda e: e.tensor_tensor(S, S, P, ALU.mult), b1, g1)
                b3 = dve.op(lambda e: e.tensor_tensor(P, Cc, P, ALU.mult), b2)
                b4 = dve.op(lambda e: e.tensor_tensor(Q, Cc, Q, ALU.mult), b1)
                b5 = dve.op(lambda e: e.tensor_tensor(P, P, R, ALU.subtract), b3)
                b6 = dve.op(lambda e: e.tensor_tensor(Q, Q, S, ALU.add), b4, b2)
                ym = None
                for n, (w, x, r) in enumerate(((cz[par][0], P, b5), (cz[par][1], Q, b6))):
                    for h in range(2):
                        ym = pe.op(lambda e, w=w, x=x, h=h, n=n, j=j: e.matmul(
                            yps.ap[:, h * 512:(h + 1) * 512], w, x[:, h * 512:(h + 1) * 512],
                            start=(j == 0 and n == 0), stop=(j == 3 and n == 1)), r, bt, yps.free if j == 0 and n == 0 else None)
                cz_free[par] = [ym]
                tail = [ym]
                if j == 3:
                    y1 = dve.op(lambda e: e.scalar_tensor_tensor(U[:, f, :], U[:, f, :], vec("s5_d", f), yps.ap, ALU.mult, ALU.add), ym)
                    yps.free = [y1]
                    yt.append(y1)
            barrier()
            yr = []
            for f in range(4):
                y2 = act.op(lambda e, f=f: e.activation(U[:, f, :], U[:, f, :], ACT.Gelu_apprx_tanh), yt[f])
                yr.append(y2)
            gx = []
            for f in range(4):
                r = split((Y[0][:, f, :], Y[1][:, f, :]), U[:, f, :], yr[f])
                gx.append((Y[0][:, f, :], Y[1][:, f, :], r))
            for bb in mmps.bufs:
                bb.free = []
            res = []
            outs = []
            for f in range(4):
                g = sgl.take()

                hold = {}

                def lin(ps, t):
                    hold["d"] = dve.op(lambda e, f=f: e.tensor_copy(U[:, f, :], ps), t)
                    return [hold["d"]]

                product("w_glu", f, gx, lin)

                def sig(ps, t):
                    a = act.op(lambda e: e.activation(g.ap, ps, ACT.Sigmoid), t, g.free)
                    dd = dve.op(lambda e, f=f: e.tensor_tensor(U[:, f, :], U[:, f, :], g.ap, ALU.mult), a, hold["d"])
                    g.free = [dd]
                    outs.append(dd)
                    return [a]

                lastmm = product("w_glu", f + 4, gx, sig)
            barrier()
            probe("s5", U, outs)
            for f in range(4):
                res.append(split((Y[0][:, f, :], Y[1][:, f, :]), U[:, f, :], outs[f]))
            return res

        mark = top[0]
        barrier()
        yt = s5()
        barrier()
        top[0] = mark
        merge(3, 4, yt)

        def pool_branch():
            PADW = 16
            cnt, cn_t = const("cnt")
            pw = sb([128, 4, 128])
            pw_t = dma(sp, pw, A["pool_w"])
            res = []
            bufs = [sb([128, PADW + T]) for _ in range(3)]
            z = [dve.op(lambda e, b=b: e.memset(b[:, 0:PADW], 0.0)) for b in bufs]
            tail = []
            for g in range(4):
                w = (2, 4, 8, 16)[g]
                u, s, s2 = bufs
                ut = product("w_in", g, XN, lambda ps, t: [act.op(lambda e: e.copy(u[:, PADW:], ps), t, tail)])
                src, dst, lt, step = u, s, ut, 1
                while step < w:
                    sh = step
                    lt = [dve.op(lambda e, src=src, dst=dst, sh=sh: e.tensor_tensor(
                        dst[:, PADW:], src[:, PADW:], src[:, PADW - sh:PADW + T - sh], ALU.add), lt, z, tail)]
                    src, dst = dst, (s2 if dst is s else s)
                    step *= 2
                m1 = dve.op(lambda e, src=src: e.tensor_tensor(dst[:, PADW:PADW + 16], src[:, PADW:PADW + 16],
                                                               cnt[:, 16 * g:16 * g + 16], ALU.mult), lt, cn_t)
                m2 = dve.op(lambda e, src=src: e.tensor_scalar(dst[:, PADW + 16:], src[:, PADW + 16:], 1.0 / w, None, ALU.mult), lt)
                m3 = dve.op(lambda e: e.tensor_tensor(dst[:, PADW:], dst[:, PADW:], u[:, PADW:], ALU.subtract), m1, m2)
                b = mmps.take()
                for h in range(2):
                    t = pe.op(lambda e, h=h, b=b, dst=dst: e.matmul(b.ap[:, h * 512:(h + 1) * 512], pw[:, g, :],
                                                                    dst[:, PADW + h * 512:PADW + (h + 1) * 512], start=True, stop=True),
                              m3, b.free, pw_t)
                y = act.op(lambda e, b=b, src=src: e.activation(src[:, PADW:], b.ap, ACT.Identity, scale=vec("pool_s", g)), t, m3)
                b.free = [y]
                r = split((Y[0][:, g, :], Y[1][:, g, :]), src[:, PADW:], y)
                tail = r
                res.append(r)
            return res

        barrier()
        yt = pool_branch()
        probe("pool0", Y[0].bitcast(F32), yt)
        barrier()
        top[0] = mark
        merge(0, 4, yt)

        def dil_branch():
            blkm, bk_t = const("blk")
            bias = sb([128, 4, 256])
            QK = sb([128, 4, T])
            Vf = sb([128, 2, T])
            Vt = sb([128, 8, 256])
            sbuf_s = Rot([sb([128, 4, 256]) for _ in range(3)])
            pT = Rot([sb([128, 4, 2, 128]) for _ in range(2)])
            stat = Rot([sb([128, 8]) for _ in range(3)])
            ot = Rot([sb([128, 264]) for _ in range(4)])
            last_pe = []
            stores = []
            blane, olane = lanes(4), [lanes(2) for _ in range(4)]
            sc_ps, tr_ps, ou_ps = Rot([pbufs[3], pbufs[0]]), Rot([pbufs[1]]), Rot([pbufs[2]])
            for g in range(3):
                dil = DILS[g]
                L = T // dil
                bl = []
                for n, h in enumerate(HN_):
                    src = bass.AP(tensor=bsc.tensor, offset=bsc.offset + (h * 3 + g) * 384, ap=[[1, 128], [1, 256]])
                    bl.append(dma(sp, bias[:, n, :], src, bs_t, last_pe, lane=blane[n]))
                qk_t = []
                for n, ft in enumerate((4 + 2 * g, 5 + 2 * g, 10 + 2 * g, 11 + 2 * g)):
                    def ev(ps, t, n=n):
                        o = QK[:, n, :].rearrange("p (r l) -> p l r", r=dil)
                        i = ps.rearrange("p (l r) -> p l r", r=dil)
                        return [act.op(lambda e: e.copy(o, i), t, last_pe)]
                    qk_t += product("w_in", ft, XN, ev)
                vt_t = []
                for n, ft in enumerate((16 + 2 * g, 17 + 2 * g)):
                    def ev(ps, t, n=n):
                        o = Vf[:, n, :].rearrange("p (r l) -> p l r", r=dil)
                        i = ps.rearrange("p (l r) -> p l r", r=dil)
                        return [act.op(lambda e: e.copy(o, i), t, last_pe)]
                    vv = product("w_in", ft, XN, ev)
                    pb = mmps.take()

                    def ev2(ps, t, n=n):
                        return [dve.op(lambda e: e.tensor_copy(Vt[:, :, 128 * n:128 * n + 128],
                                                               ps.rearrange("p (b f) -> p b f", b=8)), t, last_pe)]
                    vt_t += transposes(Vf[:, n, :], ev2, 8, vv, pb)
                def block_scores(u):
                    blk = u["blk"]
                    full = (g == 0 and blk > 0) or (g == 1 and blk % 2 == 1)
                    W = 256 if full else 128
                    pb = sc_ps.take()
                    s4 = pb.ap.rearrange("p (h c) -> p h c", h=4)
                    k0 = (blk - 1) * 128 if full else blk * 128
                    for n, h in enumerate(HN_):
                        rows = slice(64 * (h % 2), 64 * (h % 2) + 64)
                        t = pe.op(lambda e: e.matmul(s4[:, n, 256 - W:256], QK[rows, h // 2, blk * 128:blk * 128 + 128],
                                                     QK[rows, 2 + h // 2, k0:k0 + W], start=True, stop=True), pb.free, qk_t)
                    S = sbuf_s.take()
                    cs = slice(256 - W, 256)
                    bv = bias[:, :, ::-1]
                    d = dve.op(lambda e: e.scalar_tensor_tensor(S.ap[:, :, cs], s4[:, :, cs], 0.125, bv[:, :, cs], ALU.mult, ALU.add),
                               t, S.free, bl)
                    pb.free = [d]
                    if g == 2:
                        d = dve.op(lambda e: e.tensor_tensor(S.ap[:, :, cs], S.ap[:, :, cs],
                                                             blkm.unsqueeze(1).to_broadcast([128, 4, 128]), ALU.add), d, bk_t)
                    st = stat.take()
                    O = ot.take()
                    d2 = dve.op(lambda e: e.tensor_reduce(O.ap[:, 256:260], S.ap[:, :, cs], AXX, ALU.max), d, O.free)
                    d3 = dve.op(lambda e: e.tensor_scalar(st.ap[:, 0:4], O.ap[:, 256:260], -1.0, None, ALU.mult), d2, st.free)
                    ex = []
                    for h in range(4):
                        ex.append(act.op(lambda e: e.activation(S.ap[:, h, cs], S.ap[:, h, cs], ACT.Exp, bias=st.ap[:, h:h + 1],
                                                                accum_out=O.ap[:, 260 + h:261 + h]), d3, O.free))
                    st.free = [ex[-1]]
                    u.update(W=W, k0=k0, S=S, O=O, ex=ex, d2=d2)

                def block_values(u):
                    blk, W, k0, S, O, ex, d2 = (u[n] for n in ("blk", "W", "k0", "S", "O", "ex", "d2"))
                    tb = tr_ps.take()
                    nk = W // 128
                    tv = tb.ap.rearrange("p (h k q) -> p h k q", h=4, k=2)
                    for h in range(4):
                        for k in range(nk):
                            c0 = 256 - W + 128 * k
                            t = pe.op(lambda e: e.transpose(tv[:, h, k, :], S.ap[:, h, c0:c0 + 128], ident), ex[h], tb.free)
                    S.free = [t]
                    p = pT.take()
                    pc = act.op(lambda e: e.copy(p.ap[:, :, 0:nk, :], tv[:, :, 0:nk, :]), t, p.free)
                    tb.free = [pc]
                    u.update(p=p, pc=pc)

                def block_out(u):
                    blk, W, k0, O, ex, d2, p, pc = (u[n] for n in ("blk", "W", "k0", "O", "ex", "d2", "p", "pc"))
                    nk = W // 128
                    ob = ou_ps.take()
                    for n, h in enumerate(HN_):
                        for k in range(nk):
                            t = pe.op(lambda e: e.matmul(ob.ap[:, 64 * h:64 * h + 64], p.ap[:, n, k, :],
                                                         Vt[:, k0 // 128 + k, 64 * h:64 * h + 64],
                                                         start=(k == 0), stop=(k == nk - 1)), pc, vt_t, ob.free)
                    p.free = [t]
                    oc = dve.op(lambda e: e.tensor_copy(O.ap[:, 0:256], ob.ap[:, 0:256]), t, O.free)
                    ob.free = [oc]
                    v = scr[g].rearrange("(l r) c -> r l c", r=dil)
                    if g == 2:
                        dd = [dma(sp, v[2 * blk + x], O.ap[64 * x:64 * x + 64, :], oc, ex, d2, lane=olane[blk % 4][x]) for x in range(2)]
                    else:
                        nb = 8 // dil
                        dst = v[blk // nb, (blk % nb) * 128:(blk % nb) * 128 + 128, :]
                        dd = [dma(sp, dst, O.ap, oc, ex, d2, lane=olane[blk % 4][0])]
                    O.free = dd
                    stores.extend(dd)
                    return t

                units = [dict(blk=b) for b in range(8)]
                for i in range(11):
                    if i < 8:
                        block_scores(units[i])
                    if 0 <= i - 2 < 8:
                        block_values(units[i - 2])
                    if 0 <= i - 3 < 8:
                        t = block_out(units[i - 3])
                last_pe = [t]
            return stores

        def dil_combine(stores):
            R = sb([128, 3, 8, 264])
            rt = [dma(sp, R[:, g, :, :], scr[g].rearrange("(a p) c -> p a c", p=128), stores) for g in range(3)]
            M = sb([128, 8, 4])
            E = sb([128, 3, 8, 4])
            D = sb([128, 8, 4])
            D2 = sb([128, 8, 4])
            m = [R[:, g, :, 256:260] for g in range(3)]
            dn = [R[:, g, :, 260:264] for g in range(3)]
            a = dve.op(lambda e: e.tensor_tensor(M, m[0], m[1], ALU.max), rt)
            a = dve.op(lambda e: e.tensor_tensor(M, M, m[2], ALU.max), a)
            x = []
            for g in range(3):
                s = dve.op(lambda e, g=g: e.tensor_tensor(E[:, g, :, :], m[g], M, ALU.subtract), a)
                x.append(act.op(lambda e, g=g: e.activation(E[:, g, :, :], E[:, g, :, :], ACT.Exp), s))
            d = dve.op(lambda e: e.tensor_tensor(D, E[:, 0, :, :], dn[0], ALU.mult), x)
            for g in (1, 2):
                d1 = dve.op(lambda e, g=g: e.tensor_tensor(D2, E[:, g, :, :], dn[g], ALU.mult), d)
                d = dve.op(lambda e: e.tensor_tensor(D, D, D2, ALU.add), d1)
            d = dve.op(lambda e: e.reciprocal(D, D), d)
            o = []
            for g in range(3):
                f = dve.op(lambda e, g=g: e.tensor_tensor(E[:, g, :, :], E[:, g, :, :], D, ALU.mult), d)
                for h in range(4):
                    v = R[:, g, :, 64 * h:64 * h + 64]
                    o.append(dve.op(lambda e, g=g, v=v, h=h: e.tensor_tensor(
                        v, v, E[:, g, :, HN_[h]:HN_[h] + 1].to_broadcast([128, 8, 64]), ALU.mult), f))
            y = R[:, 0, :, 0:256]
            s1 = dve.op(lambda e: e.tensor_tensor(y, y, R[:, 1, :, 0:256], ALU.add), o)
            s2 = dve.op(lambda e: e.tensor_tensor(y, y, R[:, 2, :, 0:256], ALU.add), s1)
            probe("dil", R[:, 0, :, 0:256], s2)
            res = []
            yc = sb([128, T])
            yc_free = []
            for f in range(2):
                pb = mmps.take()
                for a_ in range(8):
                    t = pe.op(lambda e, a_=a_, f=f, pb=pb: e.transpose(pb.ap[:, a_ * 128:(a_ + 1) * 128],
                                                                       R[:, 0, a_, 128 * f:128 * f + 128], ident), s2, pb.free)
                c = dve.op(lambda e, pb=pb: e.tensor_copy(yc, pb.ap), t, yc_free)
                pb.free = [c]
                r = split((Y[0][:, f, :], Y[1][:, f, :]), yc, c)
                yc_free = r
                res.append(r)
            return res

        barrier()
        top[0] = y_addr
        st = dil_branch()
        barrier()
        top[0] = mark
        yt = dil_combine(st)
        barrier()
        top[0] = mark
        merge(1, 2, yt)

        def sb_branch():
            negU, nu_t = const("negU")
            negO = sb([128, 128])
            no_t = dve.op(lambda e: e.memset(negO, -1.0))
            qT, kT, vf = sb([128, T]), sb([128, T]), sb([128, T])
            Vt = sb([128, 8, 128])
            wk = Rot([(sb([128, 512]), sb([128, 512])) for _ in range(5)])
            acc = sb([128, 512])
            zp = Rot(banks[2:6])
            op = Rot(banks[6:8])
            prp = Rot([pairs[0]])
            res = []
            prev = []
            acc_t = [None]
            nonlocal mmps
            keep = mmps
            mmps = prp

            def scores(u):
                kb, cs, qs, ds = u["kb"], u["cs"], u["qs"], u["ds"]
                z = u["z"] = zp.take()
                w = u["w"] = wk.take()
                t1, t2 = w.ap
                zt = pe.op(lambda e: e.matmul(z.ap[:, cs], kT[:, kb * 128:kb * 128 + 128], qT[:, qs], start=True, stop=True),
                           u["rdy"], z.free)
                x = act.op(lambda e: e.activation(t1[:, cs], z.ap[:, cs], ACT.Abs), zt, w.free)
                x = act.op(lambda e: e.activation(t1[:, cs], t1[:, cs], ACT.Exp, scale=-1.0), x)
                x = act.op(lambda e: e.activation(t1[:, cs], t1[:, cs], ACT.Ln, bias=1.0), x)
                u["x"] = x
                s = dve.op(lambda e: e.scalar_tensor_tensor(t2[:, cs], z.ap[:, cs], 0.0, t1[:, cs], ALU.max, ALU.add), x, w.free)
                if ds is not None:
                    s = pool.op(lambda e: e.affine_select(out=t2[:, ds], in_=t2[:, ds], pattern=[[1, 128]], compare_op=ALU.is_gt,
                                                          fill=0.0, base=0, channel_multiplier=-1), s)
                u["s"] = s

            def weights(u):
                cs, ds, z, s = u["cs"], u["ds"], u["z"], u["s"]
                t1, t2 = u["w"].ap
                if u["first"]:
                    acc_t[0] = dve.op(lambda e: e.memset(acc, 0.0), acc_t[0])
                pe.op(lambda e: e.matmul(z.ap[:, cs], negU, t2[:, cs], start=False, stop=True, skip_group_check=True), s, nu_t)
                m2 = pe.op(lambda e: e.matmul(z.ap[:, cs], negO, acc[:, cs], start=False, stop=True, skip_group_check=True), acc_t[0], no_t)
                acc_t[0] = dve.op(lambda e: e.tensor_tensor(acc[:, cs], acc[:, cs], t2[:, cs], ALU.add), m2, s, acc_t[0])
                y = act.op(lambda e: e.activation(t1[:, cs], z.ap[:, cs], ACT.Exp), m2, s)
                z.free = [y]
                if ds is not None:
                    y = pool.op(lambda e: e.affine_select(out=t1[:, ds], in_=t1[:, ds], pattern=[[1, 128]], compare_op=ALU.is_gt,
                                                          fill=0.0, base=0, channel_multiplier=-1), y)
                u["y"], u["a"] = y, acc_t[0]

            def values(u):
                kb, cs, t1 = u["kb"], u["cs"], u["w"].ap[0]
                if u["first"]:
                    u["o"]["b"] = op.take()
                ob = u["o"]["b"]
                t = pe.op(lambda e: e.matmul(ob.ap[:, cs], Vt[:, kb, :], t1[:, cs], start=u["first"], stop=(kb == 0), skip_group_check=True),
                          u["y"], u["rdy"], ob.free)
                u["w"].free = [t, u["a"]]
                u["t"] = t
                if kb == 0:
                    h, qs = u["h"], slice(u["qc"] * 512, u["qc"] * 512 + 512)
                    r = split((Y[0][:, h, qs], Y[1][:, h, qs]), ob.ap, t)
                    ob.free = r
                    u["o"]["r"].extend(r)

            act.op(lambda e: e.preload_act_table_set("natural_log_exp_and_others"))
            for h in range(4):
                q_t = product("w_in", 22 + h, XN, lambda ps, t: [act.op(lambda e: e.mul(qT, ps, 128.0 ** -0.5), t, prev)])
                k_t = product("w_in", 26 + h, XN, lambda ps, t: [dve.op(lambda e: e.tensor_copy(kT, ps), t, prev)])
                v_t = product("w_in", 30 + h, XN, lambda ps, t: [act.op(lambda e: e.copy(vf, ps), t, prev)])
                vt_t = transposes(vf, lambda ps, t: [dve.op(lambda e: e.tensor_copy(Vt.rearrange("p a b -> p (a b)"), ps), t, prev)],
                                  8, v_t, prp.take())
                units = []
                r = []
                for qc in range(2):
                    nk = 4 * qc + 4
                    o = {"r": r}
                    for kb in range(nk - 1, -1, -1):
                        off = max(0, kb - 4 * qc) * 128
                        units.append(dict(h=h, qc=qc, kb=kb, cs=slice(off, 512), qs=slice(qc * 512 + off, qc * 512 + 512),
                                          ds=slice(off, off + 128) if kb >= 4 * qc else None, first=(kb == nk - 1), o=o,
                                          rdy=[q_t, k_t, vt_t]))
                n = len(units)
                for i in range(n + 3):
                    if i < n:
                        scores(units[i])
                    if 0 <= i - 2 < n:
                        weights(units[i - 2])
                    if 0 <= i - 3 < n:
                        values(units[i - 3])
                prev = [units[-1]["t"], units[-1]["a"]]
                res.append(r)
            mmps = keep
            return res

        barrier()
        yt = sb_branch()
        probe("sb0", Y[0].bitcast(F32), yt)
        barrier()
        for b_ in mmps.bufs:
            b_.free = []
        top[0] = mark
        merge(2, 4, yt)
        probe("merged", merged, m_tok)

        barrier()
        mx = []
        for k in range(8):
            r = split((XH[0][:, k, :], XH[1][:, k, :]), merged[:, k, :], m_tok[k])
            mx.append((XH[0][:, k, :], XH[1][:, k, :], r))
        X2 = merged
        xl = Rot([sb([128, T]) for _ in range(2)])
        x2_tok = [None] * 8
        barrier()
        xlane = lanes(2)
        for ft in range(8):
            b = xl.take()
            ld = dma(sp, b.ap, A["xT"][:, ft, :], b.free, lane=xlane[ft % 2])

            def ev(ps, t):
                d = dve.op(lambda e: e.tensor_tensor(X2[:, ft, :], ps, b.ap, ALU.add), t, ld, mx[ft][2])
                b.free = [d]
                x2_tok[ft] = [d]
                return [d]
            product("w_out", ft, mx, ev)
        probe("x2", X2, x2_tok)
        barrier()
        top[0] = y_addr

        mod = sb([128, 48])
        cond = sb([128, 8])

        def ffn(Xacc, rdy, wu, wd, hx, gname, conv, out_scale):
            mark = top[0]
            H = (sb([128, 6, T], F32R), sb([128, 6, T], F32R))
            PADW = 2
            sg = Rot([sb([128, T + PADW]) for _ in range(2)])
            cb = Rot([sb([128, T]) for _ in range(2)]) if conv else None
            uv = Rot([sb([128, T]) for _ in range(2)])
            acc_t = list(rdy)
            zt = None
            if conv:
                zt = [dve.op(lambda e, b=b: e.memset(b.ap[:, 0:PADW], 0.0)) for b in sg.bufs]
            h_free = []
            k0 = 0
            for n in FFN_CUT:
                hs = []
                for i in range(n):
                    u = uv.take()
                    got = {}

                    def conved(ps, t, ft, dst, dfree):
                        raw = sg.take()
                        a = act.op(lambda e: e.copy(raw.ap[:, PADW:], ps), t, raw.free, zt)
                        w = [vec("fconv", 44 * j + ft) for j in range(3)]
                        x = dve.op(lambda e: e.tensor_scalar(dst, raw.ap[:, 2:], w[2], vec("fconv_b", ft), ALU.mult, ALU.add), a, dfree, v_tok)
                        x = dve.op(lambda e: e.scalar_tensor_tensor(dst, raw.ap[:, 1:T + 1], w[1], dst, ALU.mult, ALU.add), x)
                        x = dve.op(lambda e: e.scalar_tensor_tensor(dst, raw.ap[:, 0:T], w[0], dst, ALU.mult, ALU.add), x)
                        raw.free = [x]
                        return a, x

                    if conv:
                        gb, vb = cb.bufs

                        def gate(ps, t):
                            a, x = conved(ps, t, k0 + i, gb.ap, gb.free)
                            got["g"] = act.op(lambda e: e.activation(gb.ap, gb.ap, ACT.Silu), x)
                            return [a]

                        def val(ps, t):
                            a, x = conved(ps, t, 22 + k0 + i, vb.ap, vb.free)
                            got["v"] = dve.op(lambda e: e.tensor_tensor(u.ap, gb.ap, vb.ap, ALU.mult), x, got["g"], u.free)
                            gb.free = vb.free = [got["v"]]
                            return [a]
                    else:
                        s = sg.take()

                        def gate(ps, t):
                            got["g"] = act.op(lambda e: e.activation(s.ap[:, 0:T], ps, ACT.Silu), t, s.free)
                            return [got["g"]]

                        def val(ps, t):
                            got["v"] = dve.op(lambda e: e.tensor_tensor(u.ap, ps, s.ap[:, 0:T], ALU.mult), t, got["g"], u.free)
                            s.free = [got["v"]]
                            return [got["v"]]

                    product(wu, k0 + i, hx, gate)
                    product(wu, 22 + k0 + i, hx, val)
                    r = split((H[0][:, i, :], H[1][:, i, :]), u.ap, got["v"], h_free)
                    u.free = r
                    hs.append((H[0][:, i, :], H[1][:, i, :], r))
                for ft in range(8):
                    def ev(ps, t):
                        if out_scale is None:
                            d = dve.op(lambda e: e.tensor_tensor(Xacc[:, ft, :], ps, Xacc[:, ft, :], ALU.add), t, acc_t[ft])
                        else:
                            d = dve.op(lambda e: e.scalar_tensor_tensor(Xacc[:, ft, :], ps, out_scale(ft), Xacc[:, ft, :], ALU.mult, ALU.add),
                                       t, acc_t[ft])
                        acc_t[ft] = [d]
                        return [d]
                    product(wd, ft, hs, ev, k0)
                h_free = [pe.last]
                k0 += n
            top[0] = mark
            return acc_t

        mark = top[0]
        tmp = Rot([sb([128, T]) for _ in range(2)])
        rstd = sb([128, T])
        hn = rms_split(X2, x2_tok, "ffn_g", XH, tmp, rstd)
        HN = [(XH[0][:, k, :], XH[1][:, k, :], hn[k]) for k in range(8)]
        barrier()
        top[0] = mark
        acc = ffn(X2, [None] * 8, "w_up", "w_down", HN, None, False, None)
        probe("x3", X2, acc)
        barrier()
        top[0] = mark

        tmp = Rot([sb([128, T]) for _ in range(2)])
        rstd, mu = sb([128, T]), sb([128, T])
        pb = mmps.take()
        r = mean_square_inv([(X2[:, k, :], None) for k in range(8)], T, tmp, rstd, pb)
        fx = [[dve.op(lambda e, k=k: e.scalar_tensor_tensor(X2[:, k, :], X2[:, k, :], vec("fin_g", k), rstd, ALU.mult, ALU.mult), r)]
              for k in range(8)]
        probe("b1", X2, fx)
        if dump is not None and "b1" in dump:
            barrier()
        x1 = layer_norm(X2, fx, "ln0_g", "ln0_b", tmp, mu, rstd)
        sp_t = [dma(sp, spill[:, k, :], X2[:, k, :], x1[k], lane=lane8[k]) for k in range(8)]

        adr = Rot([sb([128, T]) for _ in range(3)])
        ada = [sb([128, T]) for _ in range(2)]
        cs = act.op(lambda e: e.activation(cond, vec("c", 0, 8), ACT.Silu), v_tok)
        mb = Buf(banks[7])
        ada_free = [[], []]
        mt = None
        barrier()
        alane = lanes(3)
        for j in range(6):
            a = ada[j % 2]
            d = None
            for k in range(8):
                b = adr.take()
                ld = dma(sp, b.ap, A["w_ada"][k, :, j * T:(j + 1) * T], b.free, lane=alane[(8 * j + k) % 3])
                if k == 0:
                    d = dve.op(lambda e, a=a, b=b: e.tensor_scalar(a, b.ap, cond[:, 0:1], None, ALU.mult), ld, cs, ada_free[j % 2])
                else:
                    d = dve.op(lambda e, a=a, b=b, k=k: e.scalar_tensor_tensor(a, b.ap, cond[:, k:k + 1], a, ALU.mult, ALU.add), ld, cs, d)
                b.free = [d]
            for f in range(8):
                mt = pe.op(lambda e, a=a, f=f, j=j: e.matmul(mb.ap[:, 8 * j + f:8 * j + f + 1], a[:, f * 128:(f + 1) * 128], ones[:, 0:1],
                                                             start=True, stop=True), d, o_tok)
            ada_free[j % 2] = [mt]
        md = dve.op(lambda e: e.tensor_tensor(mod, mb.ap[:, 0:48], vec("b_ada", 0, 48), ALU.add), mt, v_tok)
        md2 = [dve.op(lambda e, o=o: e.tensor_scalar(mod[:, o:o + 8], mod[:, o:o + 8], 1.0, None, ALU.add), md) for o in (8, 16, 32, 40)]
        sh_a, sc_a, gt_a, sh_f, sc_f, gt_f = (lambda k, o=o: mod[:, o + k:o + k + 1] for o in (0, 8, 16, 24, 32, 40))

        def modulate(X, rdy, sc, sh):
            res = []
            for k in range(8):
                b = tmp.take()
                d = dve.op(lambda e, b=b, k=k: e.tensor_scalar(b.ap, X[:, k, :], sc(k), sh(k), ALU.mult, ALU.add), rdy[k], md2, b.free)
                rr = split((XH[0][:, k, :], XH[1][:, k, :]), b.ap, d)
                b.free = rr
                res.append((XH[0][:, k, :], XH[1][:, k, :], rr))
            return res

        HX = modulate(X2, x1, sc_a, sh_a)
        barrier()
        for q in (act, dve, pe, pool):
            q.extra += sp_t
        top[0] = mark
        top_mixer = top[0]
        X1 = X2
        O = X1

        sm = sb([128, T])
        smt = product("w_in2", 28, HX, lambda ps, t: [act.op(lambda e: e.copy(sm, ps), t)])
        upper, up_t = const("upper")
        rstd = sb([128, T])
        base_g = top[0]

        def delta():
            mS, ms_t = const("mS")
            mT, mt_t = const("mT")
            lev, lv_t = const("lev")
            abt = sb([128, 8, 8])
            pb = mmps.take()

            def ev(ps, t):
                v = ps.rearrange("p (a c) -> p a c", a=8)
                return [dve.op(lambda e: e.tensor_copy(abt[:, :, 0:4], v[:, :, 0:4]), t),
                        dve.op(lambda e: e.tensor_copy(abt[:, :, 4:8], v[:, :, 32:36]), t)]
            at_ = transposes(sm, ev, 8, smt, pb)
            beta, la, t1, t2 = (sb([128, 8, 4]) for _ in range(4))
            na = sb([128, 4])
            bet = act.op(lambda e: e.activation(beta, abt[:, :, 4:8], ACT.Sigmoid), at_)
            nat = act.op(lambda e: e.activation(na, vec("alog", 0, 4), ACT.Exp), v_tok)
            x = dve.op(lambda e: e.tensor_tensor(la, abt[:, :, 0:4], vec("dtb", 0, 4).unsqueeze(1).to_broadcast([128, 8, 4]), ALU.add), at_, v_tok)
            x1_ = act.op(lambda e: e.activation(t1, la, ACT.Abs), x)
            x1_ = act.op(lambda e: e.activation(t1, t1, ACT.Exp, scale=-1.0), x1_)
            x1_ = act.op(lambda e: e.activation(t1, t1, ACT.Ln, bias=1.0), x1_)
            x2_ = dve.op(lambda e: e.scalar_tensor_tensor(la, la, 0.0, t1, ALU.max, ALU.add), x1_, x)
            x3_ = dve.op(lambda e: e.tensor_scalar(na, na, -1.0, None, ALU.mult), nat)
            lat = dve.op(lambda e: e.tensor_tensor(la, la, na.unsqueeze(1).to_broadcast([128, 8, 4]), ALU.mult), x2_, x3_)
            pb = mmps.take()
            t = pe.op(lambda e, pb=pb: e.matmul(pb.ap[:, 0:32], upper, la.rearrange("p a b -> p (a b)"), start=True, stop=True), lat, up_t, pb.free)
            G, nG, eG, kl = (sb([128, 8, 4]) for _ in range(4))
            fl = lambda z: z.rearrange("p a b -> p (a b)")
            g1 = dve.op(lambda e, pb=pb: e.tensor_copy(fl(G), pb.ap[:, 0:32]), t)
            g2 = dve.op(lambda e, pb=pb: e.tensor_scalar(fl(nG), pb.ap[:, 0:32], -1.0, None, ALU.mult), t)
            pb.free = [g1, g2]
            pb = mmps.take()
            t = pe.op(lambda e, pb=pb: e.matmul(pb.ap[:, 0:32], ones, la.rearrange("p a b -> p (a b)"), start=True, stop=True), lat, pb.free)
            gl = sb([128, 8, 4])
            glt = act.op(lambda e, pb=pb: e.activation(fl(gl), pb.ap[:, 0:32], ACT.Exp), t)
            klt = dve.op(lambda e, pb=pb: e.tensor_tensor(fl(kl), pb.ap[:, 0:32], fl(G), ALU.subtract), t, g1, glt)
            pb.free = [glt, klt]
            klt = act.op(lambda e: e.activation(fl(kl), fl(kl), ACT.Exp), klt)
            egt = act.op(lambda e: e.activation(fl(eG), fl(G), ACT.Exp), g1)
            nbt = dve.op(lambda e: e.scalar_tensor_tensor(fl(eG), fl(eG), -1.0, fl(beta), ALU.mult, ALU.mult), egt, bet)
            small = [g1, g2, glt, klt, nbt, bet, lat]
            base_d = top[0]
            res = []
            for hp in range(2):
                barrier()
                top[0] = base_d
                FT = [[sb([128, T]) for _ in range(3)] for _ in range(2)]
                KT, VT = [[sb([128, 8, 128]) for _ in range(2)] for _ in range(2)]
                ovl = top[0]
                raw = Rot([sb([128, T + 3]) for _ in range(2)])
                tmpR = Rot([sb([128, T]) for _ in range(2)])
                zt = [dve.op(lambda e, b=b: e.memset(b.ap[:, 0:3], 0.0)) for b in raw.bufs]
                f_tok, k_tok, v2_tok = [], [], []
                for hh in range(2):
                    h = 2 * hp + hh
                    toks = []
                    for part in range(3):
                        dst = FT[hh][part]
                        r = raw.take()
                        ft = 4 * part + h
                        pt = product("w_in2", ft, HX, lambda ps, t: [act.op(lambda e: e.copy(r.ap[:, 3:], ps), t, r.free, zt)])
                        w = [vec("conv", 12 * j + ft) for j in range(4)]
                        x = dve.op(lambda e: e.tensor_scalar(dst, r.ap[:, 3:], w[3], None, ALU.mult), pt, v_tok)
                        for j in range(3):
                            x = dve.op(lambda e, j=j: e.scalar_tensor_tensor(dst, r.ap[:, j:j + T], w[j], dst, ALU.mult, ALU.add), x)
                        r.free = [x]
                        x = act.op(lambda e: e.activation(dst, dst, ACT.Silu), x)
                        if part < 2:
                            b = tmpR.take()
                            sq = act.op(lambda e, b=b, dst=dst: e.activation(b.ap, dst, ACT.Square), x, b.free)
                            pb = mmps.take()
                            t = ones_sum([(b.ap, sq)], pb.ap, pb.free)[-1]
                            a = act.op(lambda e, b=b, pb=pb: e.activation(b.ap, pb.ap, ACT.Sqrt, bias=epsc), t)
                            pb.free = [a]
                            d = dve.op(lambda e, b=b: e.reciprocal(b.ap, b.ap), a)
                            sc = 128.0 ** -0.5 if part == 0 else 1.0
                            x = dve.op(lambda e, b=b, dst=dst, sc=sc: e.scalar_tensor_tensor(dst, dst, sc, b.ap, ALU.mult, ALU.mult), d)
                            b.free = [x]
                        toks.append(x)
                    f_tok.append(toks)
                    pb = mmps.take()

                    def evk(ps, t):
                        return [act.op(lambda e, c=c: e.activation(KT[hh][:, c, :], ps[:, c * 128:(c + 1) * 128], ACT.Identity,
                                                                   scale=kl[:, c, h:h + 1]), t, klt) for c in range(8)][-1:]
                    k_tok.append(transposes(FT[hh][1], evk, 8, toks[1], pb))
                    pb = mmps.take()

                    def evv(ps, t):
                        return [dve.op(lambda e, c=c: e.tensor_scalar(VT[hh][:, c, :], ps[:, c * 128:(c + 1) * 128], beta[:, c, h:h + 1],
                                                                      None, ALU.mult), t, bet) for c in range(8)][-1:]
                    v2_tok.append(transposes(FT[hh][2], evv, 8, toks[2], pb))
                    zdst = FT[hh][2]
                    zz = product("w_in2", 12 + h, HX, lambda ps, t: [act.op(lambda e: e.activation(zdst, ps, ACT.Silu), t, v2_tok[hh], k_tok[hh])])
                    f_tok[hh].append(zz)
                barrier()
                top[0] = ovl
                Z = O[:, 4:6, :].rearrange("p a (b c) -> p (a b) c", b=2)
                AT = O[:, 6:8, :].rearrange("p a (b c) -> p (a b) c", b=2)
                units = [[(2 * b + x, hh) for x in range(2) for hh in range(2)] for b in range(4)]
                WB = [dict(M=sb([128, 512]), Tm=sb([128, 512]), Y=sb([128, 512]), Ml=sb([128, 512])) for _ in range(2)]
                rot = Rot(banks[0:8])
                u_tok = []

                def prep(b, wb):
                    us = units[b]
                    Mm, Tm, Yy, Ml = wb["M"], wb["Tm"], wb["Y"], wb["Ml"]
                    Zb, ATb = Z[:, b, :], AT[:, b, :]
                    fr = wb.get("free", [])
                    sl = [slice(128 * n, 128 * n + 128) for n in range(4)]
                    lb = [dve.op(lambda e, n=n, c=c, hh=hh: e.tensor_scalar(Ml[:, sl[n]], ones, la[:, c, 2 * hp + hh:2 * hp + hh + 1], None, ALU.mult),
                                 fr, lat, o_tok) for n, (c, hh) in enumerate(us)]
                    bg, ba, bq = rot.take(), rot.take(), rot.take()
                    for n in range(4):
                        tg = pe.op(lambda e, n=n: e.matmul(bg.ap[:, sl[n]], Ml[:, sl[n]], upper, start=True, stop=True), lb, bg.free, up_t)
                    yield
                    for n, (c, hh) in enumerate(us):
                        kx, qx = FT[hh][1], FT[hh][0]
                        cc = slice(128 * c, 128 * c + 128)
                        ta = pe.op(lambda e, n=n, kx=kx, cc=cc: e.matmul(ba.ap[:, sl[n]], kx[:, cc], kx[:, cc], start=True, stop=True), ba.free)
                        tq = pe.op(lambda e, n=n, kx=kx, qx=qx, cc=cc: e.matmul(bq.ap[:, sl[n]], kx[:, cc], qx[:, cc], start=True, stop=True), bq.free)
                    m3 = mS.unsqueeze(1).to_broadcast([128, 4, 128])
                    m4 = mT.unsqueeze(1).to_broadcast([128, 4, 128])
                    v3 = lambda z: z.rearrange("p (n c) -> p n c", n=4)
                    d1 = dve.op(lambda e: e.scalar_tensor_tensor(v3(Tm), v3(bg.ap), -1.0, m3, ALU.mult, ALU.add), tg, fr, ms_t)
                    d2 = dve.op(lambda e: e.tensor_tensor(v3(Yy), v3(bg.ap), m4, ALU.add), tg, fr, mt_t)
                    bg.free = [d2]
                    e1 = [act.op(lambda e, n=n, c=c, hh=hh: e.activation(Tm[:, sl[n]], Tm[:, sl[n]], ACT.Exp, bias=G[:, c, 2 * hp + hh:2 * hp + hh + 1]),
                                 d1, g1) for n, (c, hh) in enumerate(us)]
                    e2 = [act.op(lambda e, n=n, c=c, hh=hh: e.activation(Yy[:, sl[n]], Yy[:, sl[n]], ACT.Exp, bias=nG[:, c, 2 * hp + hh:2 * hp + hh + 1]),
                                 d2, g2) for n, (c, hh) in enumerate(us)]
                    yield
                    ms = [dve.op(lambda e, n=n, c=c, hh=hh: e.scalar_tensor_tensor(Mm[:, sl[n]], ba.ap[:, sl[n]], beta[:, c, 2 * hp + hh:2 * hp + hh + 1],
                                                                                  Tm[:, sl[n]], ALU.mult, ALU.mult), ta, e1, fr)
                          for n, (c, hh) in enumerate(us)]
                    ba.free = [ms[-1]]
                    at = dve.op(lambda e: e.tensor_tensor(ATb, bq.ap, Yy, ALU.mult), tq, e2)
                    bq.free = [at]
                    i3 = ident.unsqueeze(1).to_broadcast([128, 4, 128])

                    def lmask(l, w):
                        m = lev[:, 128 * l:128 * l + 128].unsqueeze(1).to_broadcast([128, 4, 128])
                        return dve.op(lambda e: e.tensor_tensor(v3(Ml), v3(Mm), m, ALU.mult), w, ms, lv_t)
                    ml = lmask(0, tg)
                    bt = rot.take()
                    for n in range(4):
                        tt_ = pe.op(lambda e, n=n: e.transpose(bt.ap[:, sl[n]], Ml[:, sl[n]], ident), ml, bt.free)
                    zt_ = dve.op(lambda e: e.scalar_tensor_tensor(v3(Zb), v3(bt.ap), -1.0, i3, ALU.mult, ALU.add), tt_)
                    bt.free = [zt_]
                    tm_ = dve.op(lambda e: e.scalar_tensor_tensor(v3(Tm), v3(Ml), -1.0, i3, ALU.mult, ALU.add), ml, ms)
                    yield
                    for l in range(1, 7):
                        ml = lmask(l, [tt_, tm_])
                        b1 = rot.take()
                        for n in range(4):
                            ty = pe.op(lambda e, n=n: e.matmul(b1.ap[:, sl[n]], Ml[:, sl[n]], Zb[:, sl[n]], start=True, stop=True), ml, zt_, b1.free)
                        ye = act.op(lambda e: e.copy(Yy, b1.ap), ty, at)
                        b1.free = [ye]
                        yield
                        b2, b3 = rot.take(), rot.take()
                        for n in range(4):
                            tx = pe.op(lambda e, n=n: e.matmul(b2.ap[:, sl[n]], Tm[:, sl[n]], Yy[:, sl[n]], start=True, stop=True), ye, tm_, b2.free)
                        if l < 6:
                            for n in range(4):
                                tt_ = pe.op(lambda e, n=n: e.matmul(b3.ap[:, sl[n]], Yy[:, sl[n]], Tm[:, sl[n]], start=True, stop=True), b3.free)
                        zt_ = dve.op(lambda e: e.tensor_tensor(Zb, Zb, b2.ap, ALU.subtract), tx, ty)
                        b2.free = [zt_]
                        if l < 6:
                            tm_ = dve.op(lambda e: e.tensor_tensor(Tm, Tm, b3.ap, ALU.subtract), tt_, tx)
                            b3.free = [tm_]
                        else:
                            tt_ = tx
                        yield
                    wb["free"] = [zt_, tx]
                    u_tok.append([zt_, at])

                for b in (0, 2):
                    gens = [prep(b, WB[0]), prep(b + 1, WB[1])]
                    live = True
                    while live:
                        live = False
                        for gnr in gens:
                            try:
                                next(gnr)
                                live = True
                            except StopIteration:
                                pass
                barrier()
                ex = WB[1]["M"]
                qd_t = []
                ex_free = []
                lbuf = WB[0]["Ml"]
                for hh in range(2):
                    for c4 in range(2):
                        lb = [dve.op(lambda e, n=n, hh=hh, c4=c4: e.tensor_scalar(lbuf[:, 128 * n:128 * n + 128], ones,
                                                                               la[:, 4 * c4 + n, 2 * hp + hh:2 * hp + hh + 1], None, ALU.mult), ex_free)
                              for n in range(4)]
                        bg = rot.take()
                        for n in range(4):
                            tg = pe.op(lambda e, n=n, bg=bg: e.matmul(bg.ap[:, 128 * n:128 * n + 128], lbuf[:, 128 * n:128 * n + 128], upper,
                                                                      start=True, stop=True), lb, bg.free)
                        a = act.op(lambda e, bg=bg: e.activation(ex, bg.ap, ACT.Exp), tg, ex_free)
                        bg.free = [a]
                        q = FT[hh][0][:, 512 * c4:512 * c4 + 512]
                        d = dve.op(lambda e, q=q: e.tensor_tensor(q, q, ex, ALU.mult), a)
                        ex_free = [d, tg]
                        qd_t.append(d)
                cut = lambda w, n: w[:, 128 * n:128 * n + 128]
                S = [[cut(WB[1]["Tm"], 2 * x + y) for y in range(2)] for x in range(2)]
                rb_ = [cut(WB[0]["Y"], x) for x in range(2)]
                vn = [[cut(WB[1]["Y"], 2 * x + y) for y in range(2)] for x in range(2)]
                s_tok = [None, None]
                o_last = [None, None]
                vn_free = [[[], []], [[], []]]
                s_read = [[[], []], [[], []]]
                rb_free = [[], []]
                oe = [[], []]
                for c in range(8):
                    for hh in range(2):
                        h = 2 * hp + hh
                        cc = slice(128 * c, 128 * c + 128)
                        b, n = c // 2, 2 * (c % 2) + hh
                        un = slice(128 * n, 128 * n + 128)
                        So, Sn = S[hh][c % 2], S[hh][(c + 1) % 2]
                        vb = VT[hh][:, c, :]
                        if c > 0:
                            p1 = rot.take()
                            t = pe.op(lambda e, p1=p1, hh=hh, cc=cc, So=So: e.matmul(p1.ap[:, 0:128], FT[hh][1][:, cc], So, start=True, stop=True),
                                      p1.free, s_tok[hh])
                            d = dve.op(lambda e, p1=p1, hh=hh, c=c, h=h, vb=vb: e.scalar_tensor_tensor(
                                rb_[hh], p1.ap[:, 0:128], eG[:, c, h:h + 1], vb, ALU.mult, ALU.add), t, rb_free[hh])
                            p1.free = [d]
                            rx = rb_[hh]
                        else:
                            d, rx = None, vb
                        p2 = rot.take()
                        t = pe.op(lambda e, p2=p2, b=b, un=un, rx=rx: e.matmul(p2.ap[:, 0:128], Z[:, b, un], rx, start=True, stop=True), p2.free, d)
                        rb_free[hh] = [t]
                        vx = vn[hh][c % 2]
                        va = act.op(lambda e, p2=p2, vx=vx: e.copy(vx, p2.ap[:, 0:128]), t, vn_free[hh][c % 2])
                        p2.free = [va]
                        p4 = rot.take()
                        if c > 0:
                            pe.op(lambda e, p4=p4, So=So, hh=hh, cc=cc: e.matmul(p4.ap[:, 0:128], So, FT[hh][0][:, cc], start=True, stop=False),
                                  p4.free, qd_t)
                        to = pe.op(lambda e, p4=p4, vx=vx, b=b, un=un, c=c: e.matmul(p4.ap[:, 0:128], vx, AT[:, b, un], start=(c == 0), stop=True),
                                   va, p4.free)
                        oa = act.op(lambda e, p4=p4, h=h, cc=cc: e.copy(O[:, h, cc], p4.ap[:, 0:128]), to)
                        p4.free = [oa]
                        s_read[hh][c % 2] = [to]
                        oe[hh] = [oa]
                        tl = to
                        if c < 7:
                            p3 = rot.take()
                            t3 = pe.op(lambda e, p3=p3, hh=hh, c=c, vx=vx: e.matmul(p3.ap[:, 0:128], KT[hh][:, c, :], vx, start=True, stop=True), p3.free, va)
                            tl = t3
                            if c == 0:
                                s_tok[hh] = dve.op(lambda e, p3=p3, Sn=Sn: e.tensor_copy(Sn, p3.ap[:, 0:128]), t3, s_read[hh][(c + 1) % 2])
                            else:
                                s_tok[hh] = dve.op(lambda e, p3=p3, Sn=Sn, So=So, c=c, h=h: e.scalar_tensor_tensor(
                                    Sn, So, gl[:, c, h:h + 1], p3.ap[:, 0:128], ALU.mult, ALU.add), t3, s_read[hh][(c + 1) % 2], s_tok[hh])
                            p3.free = [s_tok[hh]]
                        vn_free[hh][c % 2] = [tl]
                barrier()
                for b_ in mmps.bufs:
                    b_.free = []
                top[0] = ovl
                tmpR = Rot([sb([128, T]) for _ in range(2)])
                for hh in range(2):
                    h = 2 * hp + hh
                    pb = mmps.take()
                    probe(f"odn{h}", O[:, h, :], oe[hh])
                    r = mean_square_inv([(O[:, h, :], None)], 128, tmpR, rstd, pb, res[-1] if res else None)
                    d = dve.op(lambda e, h=h: e.scalar_tensor_tensor(O[:, h, :], O[:, h, :], vec("dn_g"), rstd, ALU.mult, ALU.mult), r)
                    d2 = dve.op(lambda e, h=h, hh=hh: e.tensor_tensor(O[:, h, :], O[:, h, :], FT[hh][2], ALU.mult), d)
                    res.append([d2])
            return res

        o_tok = [o_tok] if not isinstance(o_tok, list) else o_tok
        otk = delta()
        barrier()
        top[0] = base_g

        def gla():
            mG, mg_t = const("mG")
            scanm, sc_t = const("scanm")
            g2 = sb([128, 256])
            g2_t = dma(sp, g2, A["gate2"])
            base = top[0]
            res = []
            for hp in range(2):
                barrier()
                top[0] = base
                q, k, bb, tA, tB = (sb([128, T]) for _ in range(5))
                kdt = sb([128, 8, 128])
                vt = sb([128, 8, 256])
                zs = [sb([128, T]) for _ in range(2)]
                bl = sb([128, 16])
                egl = sb([128, 16])
                St = sb([128, 16, 128])
                at = sb([128, 2, 8, 128])
                pb = mmps.take()
                for h in range(2):
                    t = pe.op(lambda e, h=h, pb=pb: e.matmul(pb.ap[:, 512 * h:512 * h + 512], g2[:, 128 * hp:128 * hp + 128],
                                                             sm[:, 512 * h:512 * h + 512], start=True, stop=True), g2_t, smt, pb.free)
                a = act.op(lambda e, pb=pb: e.activation(tA, pb.ap, ACT.Identity, bias=vec("gla_bg", hp)), t, v_tok)
                pb.free = [a]
                x = act.op(lambda e: e.activation(tB, tA, ACT.Abs), a)
                x = act.op(lambda e: e.activation(tB, tB, ACT.Exp, scale=-1.0), x)
                x = act.op(lambda e: e.activation(tB, tB, ACT.Ln, bias=1.0), x)
                d = dve.op(lambda e: e.scalar_tensor_tensor(tA, tA, 0.0, tB, ALU.min, ALU.subtract), x)
                d = dve.op(lambda e: e.tensor_scalar(tA, tA, 1.0 / 16, None, ALU.mult), d)
                bt = dve.op(lambda e: e.tensor_tensor_scan(bb, scanm, tA, 0.0, ALU.mult, ALU.add), d, sc_t)
                b3 = bb.rearrange("p (c t) -> p c t", t=64)
                blt = dve.op(lambda e: e.tensor_copy(bl.unsqueeze(2), b3[:, :, 63:64]), bt)
                egt = act.op(lambda e: e.activation(egl, bl, ACT.Exp), blt)
                qt = product("w_in2", 16 + hp, HX, lambda ps, t: [act.op(lambda e: e.mul(q, ps, 0.125), t)])
                kt = product("w_in2", 18 + hp, HX, lambda ps, t: [act.op(lambda e: e.copy(k, ps), t)])
                e1 = act.op(lambda e: e.activation(tA, bb, ACT.Exp), bt)
                qd = dve.op(lambda e: e.tensor_tensor(q, q, tA, ALU.mult), e1, qt)
                d = dve.op(lambda e: e.tensor_tensor(tB.rearrange("p (c t) -> p c t", t=64), bl.unsqueeze(2).to_broadcast([128, 16, 64]),
                                                     b3, ALU.subtract), blt)
                e2 = act.op(lambda e: e.activation(tB, tB, ACT.Exp), d)
                kd = dve.op(lambda e: e.tensor_tensor(tB, tB, k, ALU.mult), e2, kt)
                pb = mmps.take()
                kdT = transposes(tB, lambda ps, t: [dve.op(lambda e: e.tensor_copy(kdt.rearrange("p a b -> p (a b)"), ps), t)], 8, kd, pb)
                e3 = act.op(lambda e: e.activation(tA, bb, ACT.Exp, scale=-1.0), qd)
                kn = dve.op(lambda e: e.tensor_tensor(k, k, tA, ALU.mult), e3, kd)
                vtk = []
                for hh in range(2):
                    vv = product("w_in2", 20 + 2 * hp + hh, HX, lambda ps, t: [act.op(lambda e: e.copy(bb, ps), t, e3, vtk)])
                    pb = mmps.take()
                    vtk = transposes(bb, lambda ps, t: [dve.op(lambda e: e.tensor_copy(
                        vt[:, :, 128 * hh:128 * hh + 128], ps.rearrange("p (a b) -> p a b", a=8)), t)], 8, vv, pb)
                zt = []
                for hh in range(2):
                    zt.append(product("w_in2", 24 + 2 * hp + hh, HX, lambda ps, t: [act.op(lambda e: e.activation(zs[hh], ps, ACT.Silu), t)]))
                att = []
                for hh in range(2):
                    rows = slice(64 * hh, 64 * hh + 64)
                    pb = mmps.take()
                    for a_ in range(8):
                        cc = slice(128 * a_, 128 * a_ + 128)
                        t = pe.op(lambda e, cc=cc, rows=rows, pb=pb: e.matmul(pb.ap[:, cc], k[rows, cc], q[rows, cc], start=True, stop=True),
                                  kn, qd, pb.free)
                    d = dve.op(lambda e, hh=hh, pb=pb: e.tensor_tensor(at[:, hh, :, :], pb.ap.rearrange("p (a b) -> p a b", a=8),
                                                                       mG.unsqueeze(1).to_broadcast([128, 8, 128]), ALU.mult), t, mg_t)
                    pb.free = [d]
                    att.append(d)
                st = [dve.op(lambda e: e.memset(St[:, 0, :], 0.0))]
                for c in range(15):
                    a_, r = c // 2, slice(64 * (c % 2), 64 * (c % 2) + 64)
                    pb = mmps.take()
                    t = pe.op(lambda e, a_=a_, r=r, pb=pb: e.matmul(pb.ap[:, 0:256], kdt[r, a_, :], vt[r, a_, :], start=True, stop=True),
                              kdT, vtk, pb.free)
                    ns = []
                    for hh in range(2):
                        rows = slice(64 * hh, 64 * hh + 64)
                        ns.append(dve.op(lambda e, c=c, rows=rows, hh=hh, pb=pb: e.scalar_tensor_tensor(
                            St[rows, c + 1, :], St[rows, c, :], egl[rows, c:c + 1], pb.ap[rows, 128 * hh:128 * hh + 128], ALU.mult, ALU.add),
                            t, st, egt))
                    pb.free = ns
                    st = ns
                for hh in range(2):
                    rows = slice(64 * hh, 64 * hh + 64)
                    pb = mmps.take()
                    for a_ in range(8):
                        cc = slice(128 * a_, 128 * a_ + 128)
                        pe.op(lambda e, cc=cc, a_=a_, hh=hh, pb=pb: e.matmul(pb.ap[:, cc], vt[:, a_, 128 * hh:128 * hh + 128], at[:, hh, a_, :],
                                                                             start=True, stop=False, skip_group_check=True), att, pb.free)
                        for x in range(2):
                            c = 2 * a_ + x
                            ch = slice(64 * c, 64 * c + 64)
                            t = pe.op(lambda e, ch=ch, c=c, rows=rows, pb=pb: e.matmul(pb.ap[:, ch], St[rows, c, :], q[rows, ch],
                                                                                       start=False, stop=True, skip_group_check=True), st)
                    f = 4 + 2 * hp + hh
                    oa = act.op(lambda e, f=f, pb=pb: e.copy(O[:, f, :], pb.ap), t)
                    pb.free = [oa]
                    probe(f"ogla{f - 4}", O[:, f, :], oa)
                    tr = Rot([tA, tB])
                    barrier()
                    pb = mmps.take()
                    r_ = mean_square_inv([(O[:, f, :], oa)], 128, tr, rstd, pb)
                    d = dve.op(lambda e, f=f: e.scalar_tensor_tensor(O[:, f, :], O[:, f, :], vec("gla_g"), rstd, ALU.mult, ALU.mult), r_)
                    d2 = dve.op(lambda e, f=f, hh=hh: e.tensor_tensor(O[:, f, :], O[:, f, :], zs[hh], ALU.mult), d, zt[hh])
                    res.append([d2])
            return res

        otk = otk + gla()
        barrier()
        top[0] = base_g
        probe("o", O, otk)
        ox = []
        for k in range(8):
            r = split((XH[0][:, k, :], XH[1][:, k, :]), O[:, k, :], otk[k])
            ox.append((XH[0][:, k, :], XH[1][:, k, :], r))
        bt = barrier()
        rt = [dma(sp, X1[:, k, :], spill[:, k, :], bt, sp_t, lane=lane8[k]) for k in range(8)]
        xa = []
        tmp = Rot([sb([128, T]) for _ in range(2)])
        rstd, mu = sb([128, T]), sb([128, T])
        al = [dve.op(lambda e, k=k: e.tensor_scalar(X1[:, k, :], X1[:, k, :], ALPHA, None, ALU.mult), rt[k]) for k in range(8)]
        for ft in range(8):
            def ev(ps, t):
                d = dve.op(lambda e: e.scalar_tensor_tensor(X1[:, ft, :], ps, gt_a(ft), X1[:, ft, :], ALU.mult, ALU.add), t, al[ft], md2)
                xa.append([d])
                return [d]
            product("w_o", ft, ox, ev)
        x1 = layer_norm(X1, xa, "ln1_g", "ln1_b", tmp, mu, rstd)
        probe("ln1", X1, x1)
        if dump is not None and "ln1" in dump:
            barrier()
        HX2 = modulate(X1, x1, sc_f, sh_f)
        mtk = [h[2] for h in HX2]
        al = [[dve.op(lambda e, k=k: e.tensor_scalar(X1[:, k, :], X1[:, k, :], ALPHA, None, ALU.mult), mtk[k])] for k in range(8)]
        barrier()
        top[0] = mark
        acc = ffn(X1, al, "w_up2", "w_down2", HX2, None, True, gt_f)
        probe("preln2", X1, acc)
        barrier()
        top[0] = mark
        tmp = Rot([sb([128, T]) for _ in range(2)])
        rstd, mu = sb([128, T]), sb([128, T])
        xo = layer_norm(X1, acc, "ln2_g", "ln2_b", tmp, mu, rstd)
        st = [dma(sp, out[:, k, :], X1[:, k, :], xo[k], lane=lane8[k]) for k in range(8)]
        assert w_at[2] == len(plan)
        sp.op(None, st, dumps, sp_t)
        queues = (pe, act, dve, pool, sp)
        for q in queues:
            q.mark()
        for q in queues:
            q.number()
        print("sbuf", high[0], "sems", sem_n[0], [len(q.ops) for q in queues]) if dump is not None else None
        block = ctx.enter_context(nc.Block())
        block.tensor(lambda e: pe.emit(e))
        block.scalar(lambda e: act.emit(e))
        block.vector(lambda e: dve.emit(e))
        block.gpsimd(lambda e: pool.emit(e))
        block.sync(lambda e: sp.emit(e))


def layouts(i):
    f = lambda a: np.ascontiguousarray(a)
    a = {k: np.asarray(v) for k, v in i.items()}

    def wp(w):
        k, n = w.shape
        return f(w.reshape(k // 128, 128, n // 128, 128).transpose(2, 1, 0, 3))

    def cols(v):
        v = v.reshape(-1, 128)
        return v.T

    d = {"xT": f(a["x"][0].T.reshape(8, 128, T).transpose(1, 0, 2))}
    d["w_in"] = wp(a["w_in"][0])
    d["w_gate"] = f(np.concatenate([wp(a["w_gate"][0, b]) for b in range(4)]))
    r = 0
    for b, n in enumerate((512, 256, 512, 512)):
        d[f"w_br{b}"] = wp(a["w_branch"][0, r:r + n])
        r += n
    d["w_glu"] = wp(a["s5_w_glu"][0])
    d["w_out"] = wp(a["w_out"][0])
    d["w_up"] = wp(a["w_up"][0])
    d["w_down"] = wp(a["w_down"][0])
    w2 = a["w_in_2"][0]
    z = lambda n: np.zeros((1024, n), np.float32)
    small = np.concatenate([w2[:, 2048:2052], z(28), w2[:, 2052:2056], z(28), w2[:, 3592:3608], z(48)], axis=1)
    d["w_in2"] = wp(np.concatenate([w2[:, 0:2048], w2[:, 2056:3592], small], axis=1))
    d["w_o"] = wp(a["w_o_2"][0])
    d["w_up2"] = wp(a["ffn_w_up_2"][0])
    d["w_down2"] = wp(a["ffn_w_down_2"][0])
    d["w_ada"] = f(a["w_ada_2"][0].reshape(8, 128, 6144))
    d["pool_w"] = f(a["pool_w"][0].transpose(1, 0, 2))
    d["rel_bias"] = f(np.concatenate([a["rel_bias"], np.zeros((96, 12), np.float32)]))
    st = lambda v: v.reshape(16, 128, 16)
    bc = [st(a["s5_b_re"][0]), st(a["s5_b_im"][0]), st(a["s5_c_re"][0].transpose(0, 2, 1)), st(a["s5_c_im"][0].transpose(0, 2, 1))]
    d["s5bc"] = f(np.stack(bc).transpose(2, 0, 1, 3).reshape(128, 4, 256))
    d["gate2"] = f(np.concatenate([np.zeros((64, 256), np.float32), a["gla_w_gate2_2"][0], np.zeros((48, 256), np.float32)]))
    rep = lambda v: np.broadcast_to(v.reshape(1, -1), (128, v.size))
    v = {"attn_g": cols(a["attn_norm_g"]), "ffn_g": cols(a["ffn_norm_g"]), "fin_g": cols(a["final_norm_g"]),
         "ln0_g": cols(a["ln0_g_2"]), "ln0_b": cols(a["ln0_b_2"]), "ln1_g": cols(a["ln1_g_2"]), "ln1_b": cols(a["ln1_b_2"]),
         "ln2_g": cols(a["ln2_g_2"]), "ln2_b": cols(a["ln2_b_2"]), "pool_s": cols(a["pool_scale"]), "s5_d": cols(a["s5_d"]),
         "c": cols(a["c_2"]), "b_ada": cols(a["b_ada_2"]),
         "conv": a["dn_conv_2"][0].reshape(48, 128).T, "dn_g": cols(a["dn_norm_g_2"]), "gla_bg": cols(a["gla_b_gate_2"]),
         "gla_g": cols(a["gla_norm_g_2"]), "fconv": a["ffn_conv_2"][0].reshape(132, 128).T, "fconv_b": cols(a["ffn_conv_b_2"]),
         "alog": rep(a["dn_a_log_2"]), "dtb": rep(a["dn_dt_bias_2"]),
         "a_re": cols(a["s5_a_re"]), "a_im": cols(a["s5_a_im"]), "ldt": cols(np.repeat(a["s5_log_dt"][0], 64))}
    d["vecs"] = f(np.concatenate([v[n] for n in VCOLS], axis=1))
    for k, c in shape_constants().items():
        d["c_" + k] = c
    return d


def kernel(**inputs):
    import concourse.bacc as bacc
    from concourse.bass_utils import run_bass_kernel_spmd

    arrays = layouts(inputs)
    nc = bacc.Bacc("TRN2", target_bir_lowering=False, num_devices=1)
    A = {k: nc.dram_tensor("in_" + k, v.shape, F32, kind="ExternalInput").ap() for k, v in arrays.items()}
    out = nc.dram_tensor("out_0", (128, 8, T), F32, kind="ExternalOutput").ap()
    scr = nc.dram_tensor("scr", (3, T, 264), F32, kind="Internal").ap()
    spill = nc.dram_tensor("spill", (128, 8, T), F32, kind="Internal").ap()
    bsc = nc.dram_tensor("bsc", (4, 3, 384), F32, kind="Internal").ap()
    build(nc, A, out, scr, spill, bsc)
    r = run_bass_kernel_spmd(nc, [{"in_" + k: v for k, v in arrays.items()}], core_ids=[0])
    o = r.results[0]["out_0"]
    return np.ascontiguousarray(o.transpose(1, 0, 2).reshape(1024, T).T).reshape(1, T, 1024)
```

```python
import math

import numpy as np

import concourse.bass as bass
from concourse import mybir
from concourse.alu_op_type import AluOpType as ALU

F32 = mybir.dt.float32
F32R = mybir.dt.float32r
I32 = mybir.dt.int32
ACT = mybir.ActivationFunctionType
AXX = mybir.AxisListType.X

T = 1024
NEG = -1.0e30
EPS = 1e-6
ALPHA = 2.0 ** 0.25
MAGIC = 12582912.0
FFN_CUT = (6, 6, 5, 5)
DILS = (1, 4, 16)
HN_ = (0, 2, 1, 3)

VCOLS = {}
_at = 0
for _n, _w in (("attn_g", 8), ("ffn_g", 8), ("fin_g", 8), ("ln0_g", 8), ("ln0_b", 8), ("ln1_g", 8), ("ln1_b", 8),
               ("ln2_g", 8), ("ln2_b", 8), ("pool_s", 4), ("s5_d", 4), ("c", 8), ("b_ada", 48), ("conv", 48),
               ("dn_g", 1), ("gla_bg", 2), ("gla_g", 1), ("fconv", 132), ("fconv_b", 44), ("alog", 4), ("dtb", 4),
               ("a_re", 16), ("a_im", 16), ("ldt", 16)):
    VCOLS[_n] = (_at, _w)
    _at += _w
NV = _at


def t5_buckets(dil):
    dist = np.arange(129) * dil
    df = np.maximum(dist, 1).astype(np.float32)
    large = 16 + (np.log(df / np.float32(16)) / np.float32(math.log(2048 / 16)) * np.float32(16)).astype(np.int32)
    large = np.minimum(large, 31)
    return np.where(dist < 16, dist, large)


def shape_constants():
    c = {}
    i = np.arange(128)
    c["ident"] = np.eye(128, dtype=np.float32)
    c["upper"] = (i[:, None] <= i[None, :]).astype(np.float32)
    c["negU"] = -(i[:, None] >= i[None, :]).astype(np.float32)
    c["mS"] = np.where(i[:, None] > i[None, :], 0.0, NEG).astype(np.float32)
    c["mT"] = np.where(i[:, None] <= i[None, :], 0.0, NEG).astype(np.float32)
    lev = np.zeros((7, 128, 128), np.float32)
    for l in range(7):
        s = 1 << l
        lev[l] = ((i[:, None] // s) % 2 == 1) & ((i[None, :] // s) == (i[:, None] // s) - 1)
    c["lev"] = np.ascontiguousarray(lev.transpose(1, 0, 2)).reshape(128, 896)
    c["mG"] = ((i[:, None] <= i[None, :]) & (i[:, None] // 64 == i[None, :] // 64)).astype(np.float32)
    c["scanm"] = np.broadcast_to((np.arange(T) % 64 != 0).astype(np.float32), (128, T))
    c["tpos"] = np.broadcast_to(np.arange(T, dtype=np.float32), (128, T))
    cnt = np.zeros((128, 4, 16), np.float32)
    for g, w in enumerate((2, 4, 8, 16)):
        cnt[:, g, :] = np.float32(1.0) / np.minimum(np.arange(16) + 1, w).astype(np.float32)
    c["cnt"] = cnt.reshape(128, 64)
    hot = np.zeros((32, 3, 384), np.float32)
    pen = np.full((128, 3, 384), NEG, np.float32)
    for g, d in enumerate(DILS):
        b = t5_buckets(d)
        for dist in range(129):
            hot[b[dist], g, dist + 127] = 1.0
            pen[:, g, dist + 127] = 0.0
    c["hot"] = np.concatenate([hot.reshape(32, 1152), np.zeros((96, 1152), np.float32)])
    c["pen"] = pen.reshape(128, 1152)[0:4]
    blk = np.where(i[:, None] // 64 == i[None, :] // 64, 0.0, NEG).astype(np.float32)
    c["blk"] = blk
    return {k: np.ascontiguousarray(v) for k, v in c.items()}


CONST_SHAPES = {k: v.shape for k, v in shape_constants().items()}


class Tok:
    __slots__ = ("q", "sig", "val", "sem")

    def __init__(self, q):
        self.q, self.sig, self.val, self.sem = q, False, 0, None


def points(w):
    if w is None:
        return []
    if isinstance(w, Tok):
        return [w]
    return [t for x in w for t in points(x)]


class Lane:

    def __init__(self, sem):
        self.sem, self.n = sem, 0

    def next(self):
        self.n += 16
        return self.sem, self.n


class Noted:

    def activation(self, *a, **k):
        return lambda e: e.activation(*a, **k)

    def affine_select(self, *a, **k):
        return lambda e: e.affine_select(*a, **k)

    def copy(self, *a, **k):
        return lambda e: e.copy(*a, **k)

    def dma_start(self, *a, **k):
        return lambda e: e.dma_start(*a, **k)

    def matmul(self, *a, **k):
        return lambda e: e.matmul(*a, **k)

    def memset(self, *a, **k):
        return lambda e: e.memset(*a, **k)

    def mul(self, *a, **k):
        return lambda e: e.mul(*a, **k)

    def preload_act_table_set(self, *a, **k):
        return lambda e: e.preload_act_table_set(*a, **k)

    def reciprocal(self, *a, **k):
        return lambda e: e.reciprocal(*a, **k)

    def scalar_tensor_tensor(self, *a, **k):
        return lambda e: e.scalar_tensor_tensor(*a, **k)

    def tensor_copy(self, *a, **k):
        return lambda e: e.tensor_copy(*a, **k)

    def tensor_reduce(self, *a, **k):
        return lambda e: e.tensor_reduce(*a, **k)

    def tensor_scalar(self, *a, **k):
        return lambda e: e.tensor_scalar(*a, **k)

    def tensor_tensor(self, *a, **k):
        return lambda e: e.tensor_tensor(*a, **k)

    def tensor_tensor_scan(self, *a, **k):
        return lambda e: e.tensor_tensor_scan(*a, **k)

    def transpose(self, *a, **k):
        return lambda e: e.transpose(*a, **k)


NOTED = Noted()


class Queue:

    def __init__(self, name, sem):
        self.name, self.sem, self.ops, self.extra, self.last = name, sem, [], [], None

    def op(self, fn, *waits):
        t = Tok(self)
        flat = points(self.extra) + points(waits)
        self.extra = []
        call = fn(NOTED) if fn is not None else None
        self.ops.append((t, flat, call, None))
        self.last = t
        return t

    def dma(self, sem, val, fn, *waits):
        t = self.op(fn, *waits)
        t.sem, t.val = sem, val
        tt, w, f, _ = self.ops.pop()
        self.ops.append((tt, w, f, sem))
        return t

    def mark(self):
        for _, waits, _, _ in self.ops:
            for w in waits:
                w.sig = True

    def number(self):
        n = 0
        for t, _, _, dsem in self.ops:
            if dsem is None and t.sig:
                n += 1
                t.sem, t.val = self.sem, n

    def emit(self, eng):
        seen = {}
        for t, waits, fn, dsem in self.ops:
            need = {}
            for w in waits:
                k = id(w.sem)
                if k not in need or need[k][1] < w.val:
                    need[k] = (w.sem, w.val)
            for k, (sem, val) in need.items():
                if seen.get(k, 0) < val:
                    eng.wait_ge(sem, val)
                    seen[k] = val
            if fn is None:
                continue
            ins = fn(eng)
            if dsem is not None:
                ins.then_inc(dsem, 16)
            elif t.sig:
                ins.then_inc(t.sem, 1)


class Buf:

    def __init__(self, ap):
        self.ap, self.free = ap, []


class Rot:
    def __init__(self, aps):
        self.bufs, self.n = [a if isinstance(a, Buf) else Buf(a) for a in aps], 0

    def take(self):
        b = self.bufs[self.n % len(self.bufs)]
        self.n += 1
        return b


def weight_plan():
    plan = []

    def tiles(name, fts, kt, k0=0):
        for ft in fts:
            plan.append((name, ft, k0, kt))

    def merge(b, kt):
        for ft in range(8):
            plan.append(("w_gate", b * 8 + ft, 0, 8))
            plan.append((f"w_br{b}", ft, 0, kt))

    tiles("w_in", range(34, 38), 8)
    tiles("w_glu", [x for i in range(4) for x in (i, i + 4)], 4)
    merge(3, 4)
    tiles("w_in", range(0, 4), 8)
    merge(0, 4)
    for g in range(3):
        tiles("w_in", [4 + 2 * g, 5 + 2 * g, 10 + 2 * g, 11 + 2 * g, 16 + 2 * g, 17 + 2 * g], 8)
    merge(1, 2)
    for h in range(4):
        tiles("w_in", [30 + h, 22 + h, 26 + h], 8)
    merge(2, 4)
    tiles("w_out", range(8), 8)
    k0 = 0
    for n in FFN_CUT:
        tiles("w_up", [x for i in range(k0, k0 + n) for x in (i, i + 22)], 8)
        tiles("w_down", range(8), n, k0)
        k0 += n
    tiles("w_in2", [28], 8)
    for hp in range(2):
        for h in (2 * hp, 2 * hp + 1):
            tiles("w_in2", [h, 4 + h, 8 + h, 12 + h], 8)
    for hp in range(2):
        tiles("w_in2", [16 + hp, 18 + hp], 8)
        tiles("w_in2", [20 + 2 * hp, 21 + 2 * hp, 24 + 2 * hp, 25 + 2 * hp], 8)
    tiles("w_o", range(8), 8)
    k0 = 0
    for n in FFN_CUT:
        tiles("w_up2", [x for i in range(k0, k0 + n) for x in (i, i + 22)], 8)
        tiles("w_down2", range(8), n, k0)
        k0 += n
    return plan


def build(nc, A, out, scr, spill, bsc, dump=None):
    from contextlib import ExitStack
    ctx = ExitStack()
    with ctx:
        sem_n = [0]

        def new_sem():
            sem_n[0] += 1
            return ctx.enter_context(nc.semaphore(f"s{sem_n[0]}"))

        pe, act, dve, pool, sp = (Queue(n, new_sem()) for n in ("pe", "act", "dve", "pool", "sp"))

        top = [(nc.sbuf_base + 63) // 64 * 64]
        high = [0]
        names = [0]

        def sb(shape, dt=F32):
            n = 4
            for s in shape[1:]:
                n *= s
            names[0] += 1
            h = nc.alloc_sbuf_tensor_at(f"t{names[0]}", list(shape), dt, offset=top[0])
            top[0] += (n + 63) // 64 * 64
            high[0] = max(high[0], top[0])
            return h[tuple(slice(None) for _ in shape)]

        PS = ctx.enter_context(nc.psum_tensor("PS", [128, 8, 512], F32))
        banks = [PS[:, i, :] for i in range(8)]
        pairs = [PS[:, 2 * i:2 * i + 2, :].rearrange("p a b -> p (a b)") for i in range(4)]

        dumps = []

        phase = [[]]
        open_dma = []

        def dma(q, o, i, *waits, lane=None):
            sem, val = lane.next() if lane else (new_sem(), 16)
            return q.dma(sem, val, lambda e: e.dma_start(o, i), phase[0], *waits)

        def lanes(n):
            return [Lane(new_sem()) for _ in range(n)]

        def barrier():
            toks = [q.last for q in (pe, act, dve, pool) if q.last is not None] + open_dma
            for q in (pe, act, dve, pool):
                q.extra = q.extra + toks
            phase[0] = list(toks)
            del open_dma[:]
            return toks

        def probe(name, ap, *waits):
            if dump is not None and name in dump:
                t = dma(sp, dump[name], ap, *waits)
                dumps.append(t)
                open_dma.append(t)

        V = sb([128, NV])
        v_tok = dma(sp, V, A["vecs"])

        def vec(name, i=0, n=1):
            a = VCOLS[name][0]
            return V[:, a + i:a + i + n]

        C = {}
        c_tok = {}

        def const(name):
            C[name] = sb(list(CONST_SHAPES[name]))
            c_tok[name] = dma(sp, C[name], A["c_" + name])
            return C[name], c_tok[name]

        ident, id_tok = const("ident")
        mod = sb([128, 48])
        cond = sb([128, 8])
        comb = sb([128, 64])
        md2 = []
        alane = lanes(3)
        ones = sb([128, 128])
        epsc = sb([128, 1])
        o_tok = dve.op(lambda e: e.memset(ones, 1.0))
        e_tok = dve.op(lambda e: e.memset(epsc, EPS))

        plan = weight_plan()
        RAW, SPL, AHEAD = 3, 3, 2
        raws = [sb([128, 8, 128]) for _ in range(RAW)]
        whis = [sb([128, 8, 128], F32R) for _ in range(SPL)]
        wlos = [sb([128, 8, 128], F32R) for _ in range(SPL)]
        raw_sem = [new_sem() for _ in range(RAW)]
        raw_free = [[] for _ in range(RAW)]
        spl_free = [[] for _ in range(SPL)]
        w_dma, w_ready, w_at = {}, {}, [0, 0, 0]

        def w_load(i):
            name, ft, k0, kt = plan[i]
            s = i % RAW
            src = A[name][ft, :, k0:k0 + kt, :]
            w_dma[i] = sp.dma(raw_sem[s], 16 * (i // RAW + 1), lambda e: e.dma_start(raws[s][:, 0:kt, :], src), raw_free[s])

        def w_split(i):
            name, ft, k0, kt = plan[i]
            s, r = i % SPL, i % RAW
            if i == 0:
                for n in range(RAW):
                    w_load(n)
            a = act.op(lambda e: e.copy(whis[s][:, 0:kt, :], raws[r][:, 0:kt, :]), w_dma[i], spl_free[s])
            d = dve.op(lambda e: e.tensor_tensor(wlos[s][:, 0:kt, :], raws[r][:, 0:kt, :],
                                                 whis[s][:, 0:kt, :].bitcast(F32), ALU.subtract), a, w_dma[i], spl_free[s])
            raw_free[r] = [a, d]
            if i + RAW < len(plan):
                w_load(i + RAW)
            w_ready[i] = [a, d]

        def w_next(name, ft, k0=0):
            i = w_at[2]
            assert plan[i][:3] == (name, ft, k0), (plan[i], name, ft, k0)
            w_at[2] += 1
            while w_at[1] <= min(i + AHEAD, len(plan) - 1):
                w_split(w_at[1])
                w_at[1] += 1
            return i

        pbufs = [Buf(p) for p in pairs]
        mmps = Rot(pbufs[0:3])

        def product(name, ft, xs, evac, k0=0):
            i = w_next(name, ft, k0)
            s, kt = i % SPL, plan[i][3]
            assert kt == len(xs)
            b = mmps.take()
            ps = b.ap
            t = None
            for k in range(kt):
                hi, lo, rdy = xs[k]
                steps = [(whis, hi), (whis, lo), (wlos, hi)]
                for n, (w, x) in enumerate(steps):
                    for h in range(2):
                        def f(e, w=w, x=x, h=h, k=k, n=n):
                            return e.matmul(ps[:, h * 512:(h + 1) * 512], w[s][:, k, :], x[:, h * 512:(h + 1) * 512],
                                            start=(k == 0 and n == 0), stop=(k == kt - 1 and n == 2))
                        t = pe.op(f, (b.free + w_ready[i]) if k == 0 and n == 0 else None, rdy if n == 0 else None)
            spl_free[s] = [t]
            b.free = evac(ps, t)
            return b.free

        def split(dst, src, *waits):
            a = act.op(lambda e: e.copy(dst[0], src), *waits)
            d = dve.op(lambda e: e.tensor_tensor(dst[1], src, dst[0].bitcast(F32), ALU.subtract), a, *waits)
            return [a, d]

        def ones_sum(tiles, ps, free):
            t, n = None, len(tiles)
            out_t = []
            for k, (x, r) in enumerate(tiles):
                for h in range(2):
                    t = pe.op(lambda e, x=x, h=h, k=k: e.matmul(ps[:, h * 512:(h + 1) * 512], ones, x[:, h * 512:(h + 1) * 512],
                                                              start=(k == 0), stop=(k == n - 1)), free if k == 0 else None, r, o_tok)
                out_t.append(t)
            return out_t

        def inv_root(src, n, dst, *waits):
            act.op(lambda e: e.preload_act_table_set("natural_log_exp_and_others"))
            a = act.op(lambda e: e.activation(dst, src, ACT.Ln, scale=1.0 / n, bias=epsc), e_tok, *waits)
            return a, act.op(lambda e: e.activation(dst, dst, ACT.Exp, scale=-0.5), a)

        def square_sum(acc, tmps, *free):
            state = dict(n=0, late=None, last=None, free=[list(free) for _ in tmps])

            def late():
                if state["late"] is not None:
                    i, a = state["late"]
                    state["last"] = dve.op(lambda e: e.tensor_tensor(acc, acc, tmps[i], ALU.add), a, state["last"])
                    state["free"][i] = [state["last"]]
                    state["late"] = None
                return state["last"]

            def add(x, *rdy):
                late()
                if state["n"] == 0:
                    state["last"] = act.op(lambda e: e.activation(acc, x, ACT.Square), rdy, free)
                else:
                    i = state["n"] % len(tmps)
                    state["late"] = (i, act.op(lambda e: e.activation(tmps[i], x, ACT.Square), rdy, state["free"][i]))
                state["n"] += 1
            return add, late

        def plain_sum(acc, *free):
            state = dict(last=None, first=None)

            def add(x, rdy, col=None):
                if col is not None:
                    if state["last"] is None:
                        state["last"] = dve.op(lambda e: e.tensor_scalar(acc, x, col, None, ALU.mult), rdy, free, v_tok)
                    else:
                        state["last"] = dve.op(lambda e: e.scalar_tensor_tensor(acc, x, col, acc, ALU.mult, ALU.add), rdy, state["last"])
                elif state["first"] is None:
                    state["first"] = (x, rdy)
                elif state["last"] is None:
                    x0, r0 = state["first"]
                    state["last"] = dve.op(lambda e: e.tensor_tensor(acc, x0, x, ALU.add), r0, rdy, free)
                else:
                    state["last"] = dve.op(lambda e: e.tensor_tensor(acc, acc, x, ALU.add), rdy, state["last"])
                return state["last"]
            return add

        def split_scaled(dst, src, col, *waits):
            a = act.op(lambda e: e.activation(dst[0], src, ACT.Identity, scale=col), *waits)
            d = dve.op(lambda e: e.scalar_tensor_tensor(dst[1], src, col, dst[0].bitcast(F32), ALU.mult, ALU.subtract), a, *waits)
            return [a, d]

        def mean_square_inv(tiles, n, tmp, dst, ps_buf, dst_free=None):
            sq = []
            ps = ps_buf.ap
            toks = []
            for k, (x, r) in enumerate(tiles):
                b = tmp.take()
                a = act.op(lambda e, b=b, x=x: e.activation(b.ap, x, ACT.Square), r, b.free)
                for h in range(2):
                    t = pe.op(lambda e, b=b, h=h, k=k: e.matmul(ps[:, h * 512:(h + 1) * 512], ones, b.ap[:, h * 512:(h + 1) * 512],
                                                                start=(k == 0), stop=(k == len(tiles) - 1)), a, ps_buf.free if k == 0 else None, o_tok)
                b.free = [t]
            a, x = inv_root(ps, n, dst, t, dst_free)
            ps_buf.free = [a]
            return x

        def rms_split(X, rdy, gname, dst, tmp, rstd):
            pb = mmps.take()
            r = mean_square_inv([(X[:, k, :], rdy[k]) for k in range(8)], T, tmp, rstd, pb)
            res = []
            for k in range(8):
                b = tmp.take()
                d = dve.op(lambda e, b=b, k=k: e.scalar_tensor_tensor(b.ap, X[:, k, :], vec(gname, k), rstd, ALU.mult, ALU.mult),
                           r, b.free, v_tok)
                rr = split((dst[0][:, k, :], dst[1][:, k, :]), b.ap, d)
                b.free = rr
                res.append(rr)
            return res

        def centred(X, sums, mu, tmp, rstd, col=None, first=None):
            pb = mmps.take()
            t = ones_sum([sums], pb.ap, pb.free)[-1]
            m = dve.op(lambda e: e.tensor_scalar(mu, pb.ap, 1.0 / T, None, ALU.mult), t)
            pb.free = [m]
            if col is None:
                xc = [dve.op(lambda e, k=k: e.tensor_tensor(X[:, k, :], X[:, k, :], mu, ALU.subtract), m) for k in range(8)]
            else:
                xc = [dve.op(lambda e, k=k: e.scalar_tensor_tensor(X[:, k, :], X[:, k, :], vec(col, k), mu, ALU.mult, ALU.subtract), m)
                      for k in range(8)]
            pb = mmps.take()
            if first is None:
                r = mean_square_inv([(X[:, k, :], [xc[k]]) for k in range(8)], T, tmp, rstd, pb)
            else:
                ps = pb.ap
                sq = dve.op(lambda e: e.tensor_tensor(mu, first[0], first[0], ALU.mult), first[1], xc)
                for k in range(8):
                    b = tmp.take()
                    a = act.op(lambda e, b=b, k=k: e.activation(b.ap, X[:, k, :], ACT.Square), xc[k], b.free)
                    b.free = [ones_part(b.ap, ps, k == 0, k == 7, a, pb.free)]
                w = dve.op(lambda e: e.tensor_tensor(rstd, ps, mu, ALU.mult), pe.last, sq)
                pb.free = [w]
                r = inv_root(rstd, T, rstd, w)[1]
                r = dve.op(lambda e: e.tensor_tensor(rstd, rstd, first[0], ALU.mult), r)
            return [dve.op(lambda e, k=k: e.tensor_tensor(X[:, k, :], X[:, k, :], rstd, ALU.mult), r) for k in range(8)]

        def ones_part(x, ps, start, stop, *waits):
            for h in range(2):
                t = pe.op(lambda e, h=h: e.matmul(ps[:, h * 512:(h + 1) * 512], ones, x[:, h * 512:(h + 1) * 512], start=start, stop=stop),
                          waits, o_tok)
            return t

        def transposes(src, dst_evac, n, ready, ps_buf):
            t = None
            for j in range(n):
                t = pe.op(lambda e, j=j: e.transpose(ps_buf.ap[:, j * 128:(j + 1) * 128], src[:, j * 128:(j + 1) * 128], ident),
                          ready if j == 0 else None, ps_buf.free if j == 0 else None, id_tok)
            ps_buf.free = dst_evac(ps_buf.ap, t)
            return ps_buf.free

        base0 = top[0]
        XH = (sb([128, 8, T], F32R), sb([128, 8, T], F32R))
        base_x = top[0]

        def bias_rows():
            hot, h_t = const("hot")
            pen, p_t = const("pen")
            rb = sb([128, 12])
            rb_t = dma(sp, rb, A["rel_bias"])
            wr = []
            brow = sb([4, 3, 384])
            for g in range(3):
                b = mmps.take()
                t = pe.op(lambda e, b=b, g=g: e.matmul(b.ap[0:4, 0:384], rb[:, 4 * g:4 * g + 4], hot[:, 384 * g:384 * g + 384],
                                                       start=True, stop=True), h_t, rb_t, b.free)
                d = dve.op(lambda e, b=b, g=g: e.tensor_tensor(brow[:, g, :], b.ap[0:4, 0:384], pen[:, 384 * g:384 * g + 384], ALU.add), t, p_t)
                b.free = [d]
                wr.append(d)
            bs_t = dma(sp, bsc, brow, wr)
            return bs_t

        X = sb([128, 8, T])
        tmp = Rot([sb([128, T]) for _ in range(2)])
        rstd = sb([128, T])
        lane8 = lanes(8)
        x_tok = [[dma(sp, X[:, k, :], A["xT"][:, k, :], lane=lane8[k])] for k in range(8)]
        bs_t = bias_rows()
        xn = rms_split(X, x_tok, "attn_g", XH, tmp, rstd)
        XN = [(XH[0][:, k, :], XH[1][:, k, :], xn[k]) for k in range(8)]
        top[0] = base_x

        cs_t = act.op(lambda e: e.activation(cond, vec("c", 0, 8), ACT.Silu), v_tok)
        m_addr = top[0]
        merged = sb([128, 8, T])
        m_tok = [None] * 8
        y_addr = top[0]
        Y = (sb([128, 4, T], F32R), sb([128, 4, T], F32R))
        base_y = top[0]
        first_merge = [True]

        def conditioning(j0):
            adr = [sb([128, T]) for _ in range(3)]
            ada = [sb([128, T]) for _ in range(2)]
            lds, use = {}, {}

            def load(i):
                j, k = j0 + i // 8, i % 8
                lds[i] = dma(sp, adr[i % 3], A["w_ada"][k, :, j * T:(j + 1) * T], use.get(i - 3), lane=alane[i % 3])

            for i in range(3):
                load(i)
            d = None
            for i in range(16):
                yield
                j, k, a, x = j0 + i // 8, i % 8, ada[i // 8], adr[i % 3]
                if k == 0:
                    d = dve.op(lambda e: e.tensor_scalar(a, x, cond[:, 0:1], None, ALU.mult), lds[i], cs_t)
                else:
                    d = dve.op(lambda e: e.scalar_tensor_tensor(a, x, cond[:, k:k + 1], a, ALU.mult, ALU.add), lds[i], d)
                use[i] = [d]
                if i + 3 < 16:
                    load(i + 3)
                if k == 7:
                    if i == 7:
                        yield
                    pb = pbufs[3]
                    for f in range(8):
                        t = pe.op(lambda e: e.matmul(pb.ap[:, f:f + 1], a[:, f * 128:(f + 1) * 128], ones[:, 0:1], start=True, stop=True),
                                  d, pb.free, o_tok)
                    v = dve.op(lambda e: e.tensor_tensor(mod[:, 8 * j:8 * j + 8], pb.ap[:, 0:8], vec("b_ada", 8 * j, 8), ALU.add), t, v_tok)
                    if j in (1, 2, 4, 5):
                        v = dve.op(lambda e: e.tensor_scalar(mod[:, 8 * j:8 * j + 8], mod[:, 8 * j:8 * j + 8], 1.0, None, ALU.add), v)
                    pb.free = [v]
                    md2.append(v)

        def merge(b, kt, ytok, beside=None, done=None):
            barrier()
            mark = top[0]
            sg = Rot([sb([128, T]) for _ in range(2)])
            side = beside() if beside else iter(())
            ys = [(Y[0][:, k, :], Y[1][:, k, :], ytok[k]) for k in range(kt)]
            for ft in range(8):
                g = sg.take()

                def gate(ps, t):
                    return [act.op(lambda e: e.activation(g.ap, ps, ACT.Sigmoid), t, g.free)]

                gt = product("w_gate", b * 8 + ft, XN, gate)

                def br(ps, t):
                    if first_merge[0]:
                        d = dve.op(lambda e: e.tensor_tensor(merged[:, ft, :], ps, g.ap, ALU.mult), t, gt)
                        g.free = [d]
                        m_tok[ft] = [d]
                        return [d]
                    d = dve.op(lambda e: e.tensor_tensor(g.ap, ps, g.ap, ALU.mult), t, gt)
                    d2 = dve.op(lambda e: e.tensor_tensor(merged[:, ft, :], merged[:, ft, :], g.ap, ALU.add), d, m_tok[ft])
                    g.free = [d2]
                    m_tok[ft] = [d2]
                    return [d]

                next(side, None)
                product(f"w_br{b}", ft, ys, br)
                next(side, None)
                if done:
                    done(ft, m_tok[ft])
            for _ in side:
                pass
            first_merge[0] = False
            if not done:
                barrier()
                top[0] = mark

        def s5():
            U = sb([128, 4, T])
            sgl_at = top[0]
            ut = []

            def u_tile(i):
                ut.append(product("w_in", 34 + i, XN, lambda ps, t: [act.op(lambda e: e.copy(U[:, i, :], ps), t)]))

            BC = sb([128, 4, 16, 16])
            bct = dma(sp, BC.rearrange("p a b c -> p a (b c)"), A["s5bc"])
            cpos = sb([128, 128])
            cp_tok = dma(sp, cpos, A["c_tpos"][:, 0:128])
            u_tile(0)
            u_tile(1)
            W = [sb([128, 16]) for _ in range(14)]
            WI = sb([128, 16], I32)
            last = [v_tok]

            def d(fn):
                last[0] = dve.op(fn, last[0])
                return last[0]

            def ts(o, i, s1, s2, op0, op1=None):
                if s2 is None:
                    return d(lambda e: e.tensor_scalar(o, i, s1, None, op0))
                return d(lambda e: e.tensor_scalar(o, i, s1, s2, op0, op1))

            def tt(o, a, b, op):
                return d(lambda e: e.tensor_tensor(o, a, b, op))

            def stt(o, a, s, b, op0, op1):
                return d(lambda e: e.scalar_tensor_tensor(o, a, s, b, op0, op1))

            def exact_exp(o, x, k, r, q):
                ts(r, x, -87.5, 88.9, ALU.max, ALU.min)
                ts(k, r, 1.4426950408889634, MAGIC, ALU.mult, ALU.add)
                ts(k, k, MAGIC, None, ALU.subtract)
                stt(r, k, -0.693359375, r, ALU.mult, ALU.add)
                stt(r, k, 2.12194440054690583e-4, r, ALU.mult, ALU.add)
                ts(q, r, 1.0 / 5040, 1.0 / 720, ALU.mult, ALU.add)
                for cf in (1.0 / 120, 1.0 / 24, 1.0 / 6, 0.5, 1.0, 1.0):
                    tt(q, q, r, ALU.mult)
                    ts(q, q, cf, None, ALU.add)
                ts(k, k, 126.0, 8388608.0, ALU.add, ALU.mult)
                d(lambda e: e.tensor_copy(WI, k))
                stt(o, q, 2.0, WI.bitcast(F32), ALU.mult, ALU.mult)
                ts(k, x, -87.3, None, ALU.is_ge)
                tt(o, o, k, ALU.mult)

            ar, ai = vec("a_re", 0, 16), vec("a_im", 0, 16)
            dt_, mag, th, t1, t2, t3, co, si, cr, ci, tau, t4, nr, ni = W
            exact_exp(dt_, vec("ldt", 0, 16), t1, t2, t3)
            tt(t4, ar, dt_, ALU.mult)
            exact_exp(mag, t4, t1, t2, t3)
            tt(th, ai, dt_, ALU.mult)
            ts(t1, th, 1.0 / (2 * math.pi), MAGIC, ALU.mult, ALU.add)
            ts(t1, t1, MAGIC, None, ALU.subtract)
            c1 = 6.28125
            c2 = float(np.float32(np.round((2 * math.pi - c1) * 2 ** 18) / 2 ** 18))
            c3 = 2 * math.pi - c1 - c2
            stt(th, t1, -c1, th, ALU.mult, ALU.add)
            stt(th, t1, -c2, th, ALU.mult, ALU.add)
            stt(th, t1, -c3, th, ALU.mult, ALU.add)
            ts(tau, th, 1.0 / (2 * math.pi), None, ALU.mult)
            ts(t1, th, 0.25, None, ALU.mult)
            tt(t2, t1, t1, ALU.mult)
            ts(t3, t2, 1.0 / 362880, -1.0 / 5040, ALU.mult, ALU.add)
            for cf in (1.0 / 120, -1.0 / 6, 1.0):
                tt(t3, t3, t2, ALU.mult)
                ts(t3, t3, cf, None, ALU.add)
            tt(si, t3, t1, ALU.mult)
            ts(t3, t2, -1.0 / 3628800, 1.0 / 40320, ALU.mult, ALU.add)
            for cf in (-1.0 / 720, 1.0 / 24, -0.5, 1.0):
                tt(t3, t3, t2, ALU.mult)
                ts(t3, t3, cf, None, ALU.add)
            d(lambda e: e.tensor_copy(co, t3))
            for _ in range(2):
                tt(t1, si, si, ALU.mult)
                stt(si, si, 2.0, co, ALU.mult, ALU.mult)
                ts(co, t1, -2.0, 1.0, ALU.mult, ALU.add)
            tt(nr, mag, co, ALU.mult)
            ts(nr, nr, -1.0, None, ALU.add)
            tt(ni, mag, si, ALU.mult)
            tt(t1, ar, ar, ALU.mult)
            tt(t2, ai, ai, ALU.mult)
            tt(t1, t1, t2, ALU.add)
            d(lambda e: e.reciprocal(t1, t1))
            tt(cr, nr, ar, ALU.mult)
            tt(t2, ni, ai, ALU.mult)
            tt(cr, cr, t2, ALU.add)
            tt(cr, cr, t1, ALU.mult)
            tt(ci, ni, ar, ALU.mult)
            tt(t2, nr, ai, ALU.mult)
            tt(ci, ci, t2, ALU.subtract)
            tt(ci, ci, t1, ALU.mult)
            
            PR, PI = sb([128, 9, 16]), sb([128, 9, 16])
            Br, Bi = sb([128, 16, 16]), sb([128, 16, 16])
            keep = top[0]
            top[0] = m_addr
            q1 = sb([128, 4, 16])
            q2 = sb([128, 16, 16])
            top[0] = keep
            d(lambda e: e.memset(PR[:, 0, :], 1.0))
            d(lambda e: e.memset(PI[:, 0, :], 0.0))
            tt(PR[:, 1, :], mag, co, ALU.mult)
            tt(PI[:, 1, :], mag, si, ALU.mult)
            for m in (1, 2, 4):
                a, o = slice(1, m + 1), slice(m + 1, 2 * m + 1)
                bro = lambda x: x[:, m:m + 1, :].to_broadcast([128, m, 16])
                tt(PR[:, o, :], PR[:, a, :], bro(PR), ALU.mult)
                tt(q1[:, 0:m, :], PI[:, a, :], bro(PI), ALU.mult)
                tt(PR[:, o, :], PR[:, o, :], q1[:, 0:m, :], ALU.subtract)
                tt(PI[:, o, :], PR[:, a, :], bro(PI), ALU.mult)
                tt(q1[:, 0:m, :], PI[:, a, :], bro(PR), ALU.mult)
                tt(PI[:, o, :], PI[:, o, :], q1[:, 0:m, :], ALU.add)
            for _ in range(3):
                tt(mag, mag, mag, ALU.mult)
            ts(tau, tau, 8.0, None, ALU.mult)
            ts(t1, tau, MAGIC, MAGIC, ALU.add, ALU.subtract)
            tt(tau, tau, t1, ALU.subtract)
            b3 = lambda x: x.unsqueeze(2).to_broadcast([128, 16, 16])
            last[0] = [last[0], bct]
            tt(Br, BC[:, 0, :, :], b3(cr), ALU.mult)
            tt(q2, BC[:, 1, :, :], b3(ci), ALU.mult)
            tt(Br, Br, q2, ALU.subtract)
            tt(Bi, BC[:, 1, :, :], b3(cr), ALU.mult)
            tt(q2, BC[:, 0, :, :], b3(ci), ALU.mult)
            tt(Bi, Bi, q2, ALU.add)
            u_tile(2)
            u_tile(3)
            keep = top[0]
            top[0] = m_addr
            CLr, CLi = sb([128, 16, 9, 16]), sb([128, 16, 9, 16])
            M = sb([128, 32, 128])
            big_at = top[0]
            tmp = sb([128, 8, 9, 16])
            Ks = sb([16, 32, 128])
            assert top[0] <= base_y
            mz = pool.op(lambda e: e.memset(M, 0.0), xn)
            trp = Rot([pbufs[0], pbufs[1]])
            pA, pB = pbufs[2], pbufs[3]
            flat4 = lambda x: x.rearrange("p a b c -> p (a b c)")

            kt = []
            for hf in range(2):
                ii = slice(8 * hf, 8 * hf + 8)
                full = [128, 8, 9, 16]
                pr = PR[:, :, ii].rearrange("p k i -> p i k").unsqueeze(3).to_broadcast(full)
                pi = PI[:, :, ii].rearrange("p k i -> p i k").unsqueeze(3).to_broadcast(full)
                c_r = BC[:, 2, ii, :].unsqueeze(2).to_broadcast(full)
                c_i = BC[:, 3, ii, :].unsqueeze(2).to_broadcast(full)
                x, y = CLr[:, ii, :, :], CLi[:, ii, :, :]
                tt(x, pr, c_r, ALU.mult)
                tt(tmp, pi, c_i, ALU.mult)
                tt(flat4(x), flat4(x), flat4(tmp), ALU.subtract)
                tt(y, pr, c_i, ALU.mult)
                tt(tmp, pi, c_r, ALU.mult)
                stt(flat4(y), flat4(y), -1.0, flat4(tmp), ALU.mult, ALU.subtract)
                t = None
                for n in range(8):
                    i = 8 * hf + n
                    for gl in range(2):
                        rows = slice(64 * gl, 64 * gl + 64)
                        pb = (pA, pB)[gl]
                        for m, (w, x) in enumerate(((Br, CLr), (Bi, CLi))):
                            t = pe.op(lambda e: e.matmul(pb.ap[0:16, 128 * n:128 * n + 128], w[rows, i, :],
                                                         x[rows, i, 0:8, :].rearrange("p a b -> p (a b)"), start=(m == 0), stop=(m == 1)),
                                      last[0], pb.free)
                for gl in range(2):
                    pb = (pA, pB)[gl]
                    g = slice(16 * hf + gl, 16 * hf + 16, 2)
                    pb.free = [act.op(lambda e: e.copy(Ks[:, g, :], pb.ap[0:16, :].rearrange("p (a b) -> p a b", a=8)), t)]
                    kt += pb.free
            mt = [dma(sp, M[16 * q:16 * q + 16, :, 16 * q:128], Ks[:, :, 0:128 - 16 * q], kt, mz) for q in range(8)]
            open_dma.extend(mt)
            barrier()
            top[0] = big_at
            Ug, WT = sb([128, 16, 128]), [sb([128, 8, 128]) for _ in range(2)]
            work_at = top[0]
            work = [sb([128, 1024]) for _ in range(3)]
            assert top[0] <= base_y
            top[0] = keep
            work += [sb([128, 1024]) for _ in range(2)]
            H = [sb([128, 8, 128]) for _ in range(2)]
            yt = []
            hz = [dve.op(lambda e: e.memset(H[n][:, :, 0:1], 0.0)) for n in range(2)]
            v8 = lambda x: x.rearrange("p (a b) -> p a b", a=8)
            for hf in range(2):
                barrier()
                ii = slice(8 * hf, 8 * hf + 8)
                full = [128, 8, 8, 16]
                wr, wi, wt, a0, a1 = work
                v4 = lambda x: x.rearrange("p (a b c) -> p a b c", a=8, b=8)
                pr = PR[:, 7::-1, ii].rearrange("p k i -> p i k").unsqueeze(3).to_broadcast(full)
                pi = PI[:, 7::-1, ii].rearrange("p k i -> p i k").unsqueeze(3).to_broadcast(full)
                b_r = Br[:, ii, :].unsqueeze(2).to_broadcast(full)
                b_i = Bi[:, ii, :].unsqueeze(2).to_broadcast(full)
                w0 = last[0]
                tt(v4(wr), pr, b_r, ALU.mult)
                tt(v4(wt), pi, b_i, ALU.mult)
                xr = tt(wr, wr, wt, ALU.subtract)
                tt(v4(wi), pr, b_i, ALU.mult)
                tt(v4(wt), pi, b_r, ALU.mult)
                xi = tt(wi, wi, wt, ALU.add)
                ug = []
                for fl in range(2):
                    f = 2 * hf + fl
                    dst = (a0, a1)[fl]
                    pb = trp.take()
                    for q in range(8):
                        t = pe.op(lambda e: e.transpose(pb.ap[:, 128 * q:128 * q + 128], U[:, f, q::8], ident), ut[f], pb.free, id_tok)
                    c = act.op(lambda e: e.copy(dst.rearrange("p (g s c) -> p g s c", g=8, s=8),
                                                pb.ap.rearrange("p (s g c) -> p g s c", g=8, s=8)), t)
                    pb.free = [c]
                    pb = trp.take()
                    for q in range(8):
                        t = pe.op(lambda e: e.transpose(pb.ap[:, 128 * q:128 * q + 128], dst[:, 128 * q:128 * q + 128], ident), c, pb.free)
                    ug.append(act.op(lambda e: e.copy(Ug[:, 8 * fl:8 * fl + 8, :], v8(pb.ap)), t))
                    pb.free = [ug[-1]]
                wt_t = []
                for n, (w, x) in enumerate(((wr, xr), (wi, xi))):
                    pb = trp.take()
                    for q in range(8):
                        t = pe.op(lambda e: e.transpose(pb.ap[:, 128 * q:128 * q + 128], w[:, 128 * q:128 * q + 128], ident), x, pb.free)
                    wt_t.append(act.op(lambda e: e.copy(WT[n], v8(pb.ap)), t))
                    pb.free = [wt_t[-1]]
                bu = []
                for n, pb in enumerate((pA, pB)):
                    for q in range(8):
                        for gl in range(2):
                            t = pe.op(lambda e: e.matmul(pb.ap[64 * gl:64 * gl + 64, 128 * q:128 * q + 128], WT[n][:, q, 64 * gl:64 * gl + 64],
                                                         Ug[:, 2 * q + gl, :], start=True, stop=True), wt_t[n], ug, pb.free)
                    bu.append(t)
                S, Cc, P, Q, R = work
                busy = [bu[-1], wt_t, ug]
                q = dve.op(lambda e: e.tensor_tensor(v8(P), tau[:, ii].unsqueeze(2).to_broadcast([128, 8, 128]),
                                                     cpos.unsqueeze(1).to_broadcast([128, 8, 128]), ALU.mult), wt_t, ug, cp_tok, last[0])
                k1 = dve.op(lambda e: e.tensor_scalar(Q, P, MAGIC, MAGIC, ALU.add, ALU.subtract), q)
                k2 = dve.op(lambda e: e.tensor_tensor(Q, P, Q, ALU.subtract), k1)
                s_t = act.op(lambda e: e.activation(S, Q, ACT.Sin, scale=2 * math.pi), k2)
                k3 = dve.op(lambda e: e.tensor_scalar(P, P, 0.25, None, ALU.add), k2)
                k4 = dve.op(lambda e: e.tensor_scalar(R, P, MAGIC, MAGIC, ALU.add, ALU.subtract), k3)
                k5 = dve.op(lambda e: e.tensor_tensor(R, P, R, ALU.subtract), k4)
                c_t = act.op(lambda e: e.activation(Cc, R, ACT.Sin, scale=2 * math.pi), k5)
                br, bi = pA.ap, pB.ap
                a1_ = dve.op(lambda e: e.tensor_tensor(P, Cc, br, ALU.mult), bu, c_t, s_t)
                a2_ = dve.op(lambda e: e.tensor_tensor(R, S, bi, ALU.mult), c_t)
                a3_ = dve.op(lambda e: e.tensor_tensor(P, P, R, ALU.add), a1_, a2_)
                a4_ = dve.op(lambda e: e.tensor_tensor(Q, Cc, bi, ALU.mult), s_t)
                a5_ = dve.op(lambda e: e.tensor_tensor(R, S, br, ALU.mult), a3_)
                a6_ = dve.op(lambda e: e.tensor_tensor(Q, Q, R, ALU.subtract), a4_, a5_)
                pA.free = pB.free = [a5_]
                gs = []
                for n in range(8):
                    rb = mag[:, 8 * hf + n:8 * hf + n + 1].to_broadcast([128, 128])
                    for x, w in ((P, a3_), (Q, a6_)):
                        gs.append(dve.op(lambda e: e.tensor_tensor_scan(v8(x)[:, n, :], rb, v8(x)[:, n, :], 0.0, ALU.mult, ALU.add), w))
                b1 = dve.op(lambda e: e.tensor_tensor(R, S, Q, ALU.mult), gs)
                b2 = dve.op(lambda e: e.tensor_tensor(S, S, P, ALU.mult), b1)
                b3_ = dve.op(lambda e: e.tensor_tensor(P, Cc, P, ALU.mult), b2)
                b4 = dve.op(lambda e: e.tensor_tensor(Q, Cc, Q, ALU.mult), b1)
                b5 = dve.op(lambda e: e.tensor_tensor(H[0][:, :, 1:128], v8(P)[:, :, 0:127], v8(R)[:, :, 0:127], ALU.subtract), b3_)
                b6 = dve.op(lambda e: e.tensor_tensor(H[1][:, :, 1:128], v8(Q)[:, :, 0:127], v8(S)[:, :, 0:127], ALU.add), b4, b2)
                for fl in range(2):
                    f = 2 * hf + fl
                    dst = work[fl]
                    pb = (pA, pB)[fl]
                    for j in range(4):
                        for gl in range(2):
                            rows = slice(64 * gl, 64 * gl + 64)
                            n = 4 * fl + j
                            i = 8 * hf + n
                            o = pb.ap[:, 512 * gl + 128 * j:512 * gl + 128 * j + 128]
                            pe.op(lambda e: e.matmul(o, Ug[:, 2 * n + gl, :], M[:, 2 * i + gl, :], start=True, stop=False, skip_group_check=True),
                                  ug, pb.free)
                            for m, (w, x) in enumerate(((H[0], CLr), (H[1], CLi))):
                                t = pe.op(lambda e: e.matmul(o, w[rows, n, :], x[rows, i, 1:9, :].rearrange("p a b -> p (a b)"),
                                                             start=False, stop=(m == 1), skip_group_check=True), b5, b6, hz)
                    cp = [act.op(lambda e: e.copy(dst.rearrange("p (t j g c) -> p g t j c", t=8, j=4, g=2)[:, gl, :, :, :],
                                                  pb.ap.rearrange("p (g j t c) -> p g t j c", g=2, j=4, t=8)[:, gl, :, :, :]), t, b6)
                          for gl in range(2)]
                    pb.free = cp
                    pt = trp.take()
                    for q in range(8):
                        t = pe.op(lambda e: e.transpose(pt.ap[:, 128 * q:128 * q + 128], dst[:, 128 * q:128 * q + 128], ident), cp, pt.free)
                    uv = U[:, f, :].rearrange("p (c t) -> p t c", t=8)
                    y1 = dve.op(lambda e: e.scalar_tensor_tensor(uv, uv, vec("s5_d", f), v8(pt.ap), ALU.mult, ALU.add), t)
                    pt.free = [y1]
                    yt.append(y1)
            barrier()
            top[0] = sgl_at
            sgl = Rot([sb([128, T]) for _ in range(2)])
            yr = []
            for f in range(4):
                y2 = act.op(lambda e, f=f: e.activation(U[:, f, :], U[:, f, :], ACT.Gelu_apprx_tanh), yt[f])
                yr.append(y2)
            gx = []
            for f in range(4):
                r = split((Y[0][:, f, :], Y[1][:, f, :]), U[:, f, :], yr[f])
                gx.append((Y[0][:, f, :], Y[1][:, f, :], r))
            res = []
            outs = []
            for f in range(4):
                g = sgl.take()

                hold = {}

                def lin(ps, t):
                    hold["d"] = dve.op(lambda e, f=f: e.tensor_copy(U[:, f, :], ps), t)
                    return [hold["d"]]

                product("w_glu", f, gx, lin)

                def sig(ps, t):
                    a = act.op(lambda e: e.activation(g.ap, ps, ACT.Sigmoid), t, g.free)
                    dd = dve.op(lambda e, f=f: e.tensor_tensor(U[:, f, :], U[:, f, :], g.ap, ALU.mult), a, hold["d"])
                    g.free = [dd]
                    outs.append(dd)
                    return [a]

                lastmm = product("w_glu", f + 4, gx, sig)
            barrier()
            probe("s5", U, outs)
            for f in range(4):
                res.append(split((Y[0][:, f, :], Y[1][:, f, :]), U[:, f, :], outs[f]))
            return res

        mark = top[0]
        open_dma.append(bs_t)
        yt = s5()
        barrier()
        top[0] = mark
        merge(3, 4, yt, lambda: conditioning(0))

        def pool_branch():
            PADW = 16
            cnt, cn_t = const("cnt")
            pw = sb([128, 4, 128])
            pw_t = dma(sp, pw, A["pool_w"])
            res = []
            bufs = [sb([128, PADW + T]) for _ in range(3)]
            z = [dve.op(lambda e, b=b: e.memset(b[:, 0:PADW], 0.0)) for b in bufs]
            tail = []
            for g in range(4):
                w = (2, 4, 8, 16)[g]
                u, s, s2 = bufs
                ut = product("w_in", g, XN, lambda ps, t: [act.op(lambda e: e.copy(u[:, PADW:], ps), t, tail)])
                src, dst, lt, step = u, s, ut, 1
                while step < w:
                    sh = step
                    lt = [dve.op(lambda e, src=src, dst=dst, sh=sh: e.tensor_tensor(
                        dst[:, PADW:], src[:, PADW:], src[:, PADW - sh:PADW + T - sh], ALU.add), lt, z, tail)]
                    src, dst = dst, (s2 if dst is s else s)
                    step *= 2
                m1 = dve.op(lambda e, src=src: e.tensor_tensor(dst[:, PADW:PADW + 16], src[:, PADW:PADW + 16],
                                                               cnt[:, 16 * g:16 * g + 16], ALU.mult), lt, cn_t)
                m2 = dve.op(lambda e, src=src: e.tensor_scalar(dst[:, PADW + 16:], src[:, PADW + 16:], 1.0 / w, None, ALU.mult), lt)
                m3 = dve.op(lambda e: e.tensor_tensor(dst[:, PADW:], dst[:, PADW:], u[:, PADW:], ALU.subtract), m1, m2)
                b = mmps.take()
                for h in range(2):
                    t = pe.op(lambda e, h=h, b=b, dst=dst: e.matmul(b.ap[:, h * 512:(h + 1) * 512], pw[:, g, :],
                                                                    dst[:, PADW + h * 512:PADW + (h + 1) * 512], start=True, stop=True),
                              m3, b.free, pw_t)
                y = act.op(lambda e, b=b, src=src: e.activation(src[:, PADW:], b.ap, ACT.Identity, scale=vec("pool_s", g)), t, m3)
                b.free = [y]
                r = split((Y[0][:, g, :], Y[1][:, g, :]), src[:, PADW:], y)
                tail = r
                res.append(r)
            return res

        barrier()
        yt = pool_branch()
        probe("pool0", Y[0].bitcast(F32), yt)
        barrier()
        top[0] = mark
        merge(0, 4, yt, lambda: conditioning(2))

        def dil_branch():
            blkm, bk_t = const("blk")
            bias = sb([128, 4, 256])
            QK = sb([128, 4, T])
            Vf = sb([128, 2, T])
            Vt = sb([128, 8, 256])
            sbuf_s = Rot([sb([128, 4, 256]) for _ in range(3)])
            pT = Rot([sb([128, 4, 2, 128]) for _ in range(2)])
            stat = Rot([sb([128, 8]) for _ in range(3)])
            ot = Rot([sb([128, 264]) for _ in range(4)])
            last_pe = []
            stores = []
            blane, olane = lanes(4), [lanes(2) for _ in range(4)]
            sc_ps, tr_ps, ou_ps = Rot([pbufs[3], pbufs[0]]), Rot([pbufs[1]]), Rot([pbufs[2]])
            for g in range(3):
                dil = DILS[g]
                L = T // dil
                bl = []
                for n, h in enumerate(HN_):
                    src = bass.AP(tensor=bsc.tensor, offset=bsc.offset + (h * 3 + g) * 384, ap=[[1, 128], [1, 256]])
                    bl.append(dma(sp, bias[:, n, :], src, bs_t, last_pe, lane=blane[n]))
                qk_t = []
                for n, ft in enumerate((4 + 2 * g, 5 + 2 * g, 10 + 2 * g, 11 + 2 * g)):
                    def ev(ps, t, n=n):
                        o = QK[:, n, :].rearrange("p (r l) -> p l r", r=dil)
                        i = ps.rearrange("p (l r) -> p l r", r=dil)
                        return [act.op(lambda e: e.copy(o, i), t, last_pe)]
                    qk_t += product("w_in", ft, XN, ev)
                vt_t = []
                for n, ft in enumerate((16 + 2 * g, 17 + 2 * g)):
                    def ev(ps, t, n=n):
                        o = Vf[:, n, :].rearrange("p (r l) -> p l r", r=dil)
                        i = ps.rearrange("p (l r) -> p l r", r=dil)
                        return [act.op(lambda e: e.copy(o, i), t, last_pe)]
                    vv = product("w_in", ft, XN, ev)
                    pb = mmps.take()

                    def ev2(ps, t, n=n):
                        return [dve.op(lambda e: e.tensor_copy(Vt[:, :, 128 * n:128 * n + 128],
                                                               ps.rearrange("p (b f) -> p b f", b=8)), t, last_pe)]
                    vt_t += transposes(Vf[:, n, :], ev2, 8, vv, pb)
                def block_scores(u):
                    blk = u["blk"]
                    full = (g == 0 and blk > 0) or (g == 1 and blk % 2 == 1)
                    W = 256 if full else 128
                    pb = sc_ps.take()
                    s4 = pb.ap.rearrange("p (h c) -> p h c", h=4)
                    k0 = (blk - 1) * 128 if full else blk * 128
                    for n, h in enumerate(HN_):
                        rows = slice(64 * (h % 2), 64 * (h % 2) + 64)
                        t = pe.op(lambda e: e.matmul(s4[:, n, 256 - W:256], QK[rows, h // 2, blk * 128:blk * 128 + 128],
                                                     QK[rows, 2 + h // 2, k0:k0 + W], start=True, stop=True), pb.free, qk_t)
                    S = sbuf_s.take()
                    cs = slice(256 - W, 256)
                    bv = bias[:, :, ::-1]
                    d = dve.op(lambda e: e.scalar_tensor_tensor(S.ap[:, :, cs], s4[:, :, cs], 0.125, bv[:, :, cs], ALU.mult, ALU.add),
                               t, S.free, bl)
                    pb.free = [d]
                    if g == 2:
                        d = dve.op(lambda e: e.tensor_tensor(S.ap[:, :, cs], S.ap[:, :, cs],
                                                             blkm.unsqueeze(1).to_broadcast([128, 4, 128]), ALU.add), d, bk_t)
                    st = stat.take()
                    O = ot.take()
                    d2 = dve.op(lambda e: e.tensor_reduce(O.ap[:, 256:260], S.ap[:, :, cs], AXX, ALU.max), d, O.free)
                    d3 = dve.op(lambda e: e.tensor_scalar(st.ap[:, 0:4], O.ap[:, 256:260], -1.0, None, ALU.mult), d2, st.free)
                    ex = []
                    for h in range(4):
                        ex.append(act.op(lambda e: e.activation(S.ap[:, h, cs], S.ap[:, h, cs], ACT.Exp, bias=st.ap[:, h:h + 1],
                                                                accum_out=O.ap[:, 260 + h:261 + h]), d3, O.free))
                    st.free = [ex[-1]]
                    u.update(W=W, k0=k0, S=S, O=O, ex=ex, d2=d2)

                def block_values(u):
                    blk, W, k0, S, O, ex, d2 = (u[n] for n in ("blk", "W", "k0", "S", "O", "ex", "d2"))
                    tb = tr_ps.take()
                    nk = W // 128
                    tv = tb.ap.rearrange("p (h k q) -> p h k q", h=4, k=2)
                    for h in range(4):
                        for k in range(nk):
                            c0 = 256 - W + 128 * k
                            t = pe.op(lambda e: e.transpose(tv[:, h, k, :], S.ap[:, h, c0:c0 + 128], ident), ex[h], tb.free)
                    S.free = [t]
                    p = pT.take()
                    pc = act.op(lambda e: e.copy(p.ap[:, :, 0:nk, :], tv[:, :, 0:nk, :]), t, p.free)
                    tb.free = [pc]
                    u.update(p=p, pc=pc)

                def block_out(u):
                    blk, W, k0, O, ex, d2, p, pc = (u[n] for n in ("blk", "W", "k0", "O", "ex", "d2", "p", "pc"))
                    nk = W // 128
                    ob = ou_ps.take()
                    for n, h in enumerate(HN_):
                        for k in range(nk):
                            t = pe.op(lambda e: e.matmul(ob.ap[:, 64 * h:64 * h + 64], p.ap[:, n, k, :],
                                                         Vt[:, k0 // 128 + k, 64 * h:64 * h + 64],
                                                         start=(k == 0), stop=(k == nk - 1)), pc, vt_t, ob.free)
                    p.free = [t]
                    oc = dve.op(lambda e: e.tensor_copy(O.ap[:, 0:256], ob.ap[:, 0:256]), t, O.free)
                    ob.free = [oc]
                    v = scr[g].rearrange("(l r) c -> r l c", r=dil)
                    if g == 2:
                        dd = [dma(sp, v[2 * blk + x], O.ap[64 * x:64 * x + 64, :], oc, ex, d2, lane=olane[blk % 4][x]) for x in range(2)]
                    else:
                        nb = 8 // dil
                        dst = v[blk // nb, (blk % nb) * 128:(blk % nb) * 128 + 128, :]
                        dd = [dma(sp, dst, O.ap, oc, ex, d2, lane=olane[blk % 4][0])]
                    O.free = dd
                    stores.extend(dd)
                    return t

                units = [dict(blk=b) for b in range(8)]
                for i in range(11):
                    if i < 8:
                        block_scores(units[i])
                    if 0 <= i - 2 < 8:
                        block_values(units[i - 2])
                    if 0 <= i - 3 < 8:
                        t = block_out(units[i - 3])
                last_pe = [t]
            return stores

        def dil_combine(stores):
            R = sb([128, 3, 8, 264])
            rt = [dma(sp, R[:, g, :, :], scr[g].rearrange("(a p) c -> p a c", p=128), stores) for g in range(3)]
            M = sb([128, 8, 4])
            E = sb([128, 3, 8, 4])
            D = sb([128, 8, 4])
            D2 = sb([128, 8, 4])
            m = [R[:, g, :, 256:260] for g in range(3)]
            dn = [R[:, g, :, 260:264] for g in range(3)]
            a = dve.op(lambda e: e.tensor_tensor(M, m[0], m[1], ALU.max), rt)
            a = dve.op(lambda e: e.tensor_tensor(M, M, m[2], ALU.max), a)
            x = []
            for g in range(3):
                s = dve.op(lambda e, g=g: e.tensor_tensor(E[:, g, :, :], m[g], M, ALU.subtract), a)
                x.append(act.op(lambda e, g=g: e.activation(E[:, g, :, :], E[:, g, :, :], ACT.Exp), s))
            d = dve.op(lambda e: e.tensor_tensor(D, E[:, 0, :, :], dn[0], ALU.mult), x)
            for g in (1, 2):
                d1 = dve.op(lambda e, g=g: e.tensor_tensor(D2, E[:, g, :, :], dn[g], ALU.mult), d)
                d = dve.op(lambda e: e.tensor_tensor(D, D, D2, ALU.add), d1)
            d = dve.op(lambda e: e.reciprocal(D, D), d)
            o = []
            for g in range(3):
                f = dve.op(lambda e, g=g: e.tensor_tensor(E[:, g, :, :], E[:, g, :, :], D, ALU.mult), d)
                for h in range(4):
                    v = R[:, g, :, 64 * h:64 * h + 64]
                    o.append(dve.op(lambda e, g=g, v=v, h=h: e.tensor_tensor(
                        v, v, E[:, g, :, HN_[h]:HN_[h] + 1].to_broadcast([128, 8, 64]), ALU.mult), f))
            y = R[:, 0, :, 0:256]
            s1 = dve.op(lambda e: e.tensor_tensor(y, y, R[:, 1, :, 0:256], ALU.add), o)
            s2 = dve.op(lambda e: e.tensor_tensor(y, y, R[:, 2, :, 0:256], ALU.add), s1)
            probe("dil", R[:, 0, :, 0:256], s2)
            res = []
            yc = sb([128, T])
            yc_free = []
            for f in range(2):
                pb = mmps.take()
                for a_ in range(8):
                    t = pe.op(lambda e, a_=a_, f=f, pb=pb: e.transpose(pb.ap[:, a_ * 128:(a_ + 1) * 128],
                                                                       R[:, 0, a_, 128 * f:128 * f + 128], ident), s2, pb.free)
                c = dve.op(lambda e, pb=pb: e.tensor_copy(yc, pb.ap), t, yc_free)
                pb.free = [c]
                r = split((Y[0][:, f, :], Y[1][:, f, :]), yc, c)
                yc_free = r
                res.append(r)
            return res

        barrier()
        top[0] = y_addr
        st = dil_branch()
        barrier()
        top[0] = mark
        yt = dil_combine(st)
        barrier()
        top[0] = mark
        merge(1, 2, yt, lambda: conditioning(4))

        def sb_branch():
            negU, nu_t = const("negU")
            negO = sb([128, 128])
            no_t = dve.op(lambda e: e.memset(negO, -1.0))
            qT, kT, vf = sb([128, T]), sb([128, T]), sb([128, T])
            Vt = sb([128, 8, 128])
            wk = Rot([(sb([128, 512]), sb([128, 512])) for _ in range(5)])
            acc = sb([128, 512])
            zp = Rot(banks[2:6])
            op = Rot(banks[6:8])
            prp = Rot([pairs[0]])
            res = []
            prev = []
            acc_t = [None]
            nonlocal mmps
            keep = mmps
            mmps = prp

            def scores(u):
                kb, cs, qs, ds = u["kb"], u["cs"], u["qs"], u["ds"]
                z = u["z"] = zp.take()
                w = u["w"] = wk.take()
                t1, t2 = w.ap
                zt = pe.op(lambda e: e.matmul(z.ap[:, cs], kT[:, kb * 128:kb * 128 + 128], qT[:, qs], start=True, stop=True),
                           u["rdy"], z.free)
                x = act.op(lambda e: e.activation(t1[:, cs], z.ap[:, cs], ACT.Abs), zt, w.free)
                x = act.op(lambda e: e.activation(t1[:, cs], t1[:, cs], ACT.Exp, scale=-1.0), x)
                x = act.op(lambda e: e.activation(t1[:, cs], t1[:, cs], ACT.Ln, bias=1.0), x)
                u["x"] = x
                s = dve.op(lambda e: e.scalar_tensor_tensor(t2[:, cs], z.ap[:, cs], 0.0, t1[:, cs], ALU.max, ALU.add), x, w.free)
                if ds is not None:
                    s = pool.op(lambda e: e.affine_select(out=t2[:, ds], in_=t2[:, ds], pattern=[[1, 128]], compare_op=ALU.is_gt,
                                                          fill=0.0, base=0, channel_multiplier=-1), s)
                u["s"] = s

            def weights(u):
                cs, ds, z, s = u["cs"], u["ds"], u["z"], u["s"]
                t1, t2 = u["w"].ap
                if u["first"]:
                    acc_t[0] = dve.op(lambda e: e.memset(acc, 0.0), acc_t[0])
                pe.op(lambda e: e.matmul(z.ap[:, cs], negU, t2[:, cs], start=False, stop=True, skip_group_check=True), s, nu_t)
                m2 = pe.op(lambda e: e.matmul(z.ap[:, cs], negO, acc[:, cs], start=False, stop=True, skip_group_check=True), acc_t[0], no_t)
                acc_t[0] = dve.op(lambda e: e.tensor_tensor(acc[:, cs], acc[:, cs], t2[:, cs], ALU.add), m2, s, acc_t[0])
                y = act.op(lambda e: e.activation(t1[:, cs], z.ap[:, cs], ACT.Exp), m2, s)
                z.free = [y]
                if ds is not None:
                    y = pool.op(lambda e: e.affine_select(out=t1[:, ds], in_=t1[:, ds], pattern=[[1, 128]], compare_op=ALU.is_gt,
                                                          fill=0.0, base=0, channel_multiplier=-1), y)
                u["y"], u["a"] = y, acc_t[0]

            def values(u):
                kb, cs, t1 = u["kb"], u["cs"], u["w"].ap[0]
                if u["first"]:
                    u["o"]["b"] = op.take()
                ob = u["o"]["b"]
                t = pe.op(lambda e: e.matmul(ob.ap[:, cs], Vt[:, kb, :], t1[:, cs], start=u["first"], stop=(kb == 0), skip_group_check=True),
                          u["y"], u["rdy"], ob.free)
                u["w"].free = [t, u["a"]]
                u["t"] = t
                if kb == 0:
                    h, qs = u["h"], slice(u["qc"] * 512, u["qc"] * 512 + 512)
                    r = split((Y[0][:, h, qs], Y[1][:, h, qs]), ob.ap, t)
                    ob.free = r
                    u["o"]["r"].extend(r)

            act.op(lambda e: e.preload_act_table_set("natural_log_exp_and_others"))

            def v_tile(h, free):
                return product("w_in", 30 + h, XN, lambda ps, t: [act.op(lambda e: e.copy(vf, ps), t, free)])

            nv_t = v_tile(0, None)
            for h in range(4):
                v_t = nv_t
                q_t = product("w_in", 22 + h, XN, lambda ps, t: [act.op(lambda e: e.mul(qT, ps, 128.0 ** -0.5), t, prev)])
                k_t = product("w_in", 26 + h, XN, lambda ps, t: [dve.op(lambda e: e.tensor_copy(kT, ps), t, prev)])
                vt_t = transposes(vf, lambda ps, t: [dve.op(lambda e: e.tensor_copy(Vt.rearrange("p a b -> p (a b)"), ps), t, prev)],
                                  8, v_t, prp.take())
                units = []
                r = []
                for qc in range(2):
                    nk = 4 * qc + 4
                    o = {"r": r}
                    for kb in range(nk - 1, -1, -1):
                        off = max(0, kb - 4 * qc) * 128
                        units.append(dict(h=h, qc=qc, kb=kb, cs=slice(off, 512), qs=slice(qc * 512 + off, qc * 512 + 512),
                                          ds=slice(off, off + 128) if kb >= 4 * qc else None, first=(kb == nk - 1), o=o,
                                          rdy=[q_t, k_t, vt_t]))
                n = len(units)
                for i in range(n + 3):
                    if i == n and h < 3:
                        nv_t = v_tile(h + 1, vt_t)
                    if i < n:
                        scores(units[i])
                    if 0 <= i - 2 < n:
                        weights(units[i - 2])
                    if 0 <= i - 3 < n:
                        values(units[i - 3])
                prev = [units[-1]["t"], units[-1]["a"]]
                res.append(r)
            mmps = keep
            return res

        barrier()
        yt = sb_branch()
        probe("sb0", Y[0].bitcast(F32), yt)
        barrier()
        for b_ in mmps.bufs:
            b_.free = []
        top[0] = mark
        keep = top[0]
        top[0] += 2 * 4 * T
        WX = (sb([128, 4, T], F32R), sb([128, 4, T], F32R))
        top[0] = keep
        mx = []

        def early(ft, ready):
            if ft < 4:
                r = split((WX[0][:, ft, :], WX[1][:, ft, :]), merged[:, ft, :], ready)
                mx.append((WX[0][:, ft, :], WX[1][:, ft, :], r))

        merge(2, 4, yt, done=early)
        merge_end = [pe.last]
        probe("merged", merged, m_tok)

        for k in range(4):
            r = split((Y[0][:, k, :], Y[1][:, k, :]), merged[:, 4 + k, :], m_tok[4 + k], merge_end)
            mx.append((Y[0][:, k, :], Y[1][:, k, :], r))
        X2 = merged
        keep, xls = top[0], []
        for n in range(2):
            top[0] = base0 + (8 * n + 7) * 4 * T
            xls.append(sb([128, T]))
        top[0] = keep
        xl = Rot(xls)
        for b_ in xl.bufs:
            b_.free = merge_end
        top[0] = base_y
        sq_acc = sb([128, T])
        sq_add, sq_last = square_sum(sq_acc, [sb([128, T])], m_tok)
        x2_tok, hn = [None] * 8, [None] * 8
        xlane = lanes(2)
        for ft in range(8):
            b = xl.take()
            ld = dma(sp, b.ap, A["xT"][:, ft, :], b.free, lane=xlane[ft % 2])

            def ev(ps, t):
                d = dve.op(lambda e: e.tensor_tensor(X2[:, ft, :], ps, b.ap, ALU.add), t, ld, mx[ft][2])
                b.free = [d]
                x2_tok[ft] = [d]
                sq_add(X2[:, ft, :], d)
                hn[ft] = split_scaled((XH[0][:, ft, :], XH[1][:, ft, :]), X2[:, ft, :], vec("ffn_g", ft), d, merge_end, v_tok)
                return [d]
            product("w_out", ft, mx, ev)
        probe("x2", X2, x2_tok)
        top[0] = y_addr

        def ffn(Xacc, rdy, wu, wd, hx, conv, out_scale, rstd, root, tail):
            H = (sb([128, 6, T], F32R), sb([128, 6, T], F32R))
            PADW = 2
            sg = Rot([sb([128, T + PADW]) for _ in range(2)])
            cb = Rot([sb([128, T]) for _ in range(2)]) if conv else None
            uv = Rot([sb([128, T]) for _ in range(2)])
            acc_t = list(rdy)
            zt = None
            if conv:
                zt = [dve.op(lambda e, b=b: e.memset(b.ap[:, 0:PADW], 0.0)) for b in sg.bufs]
            h_free = []
            k0 = 0
            for n in FFN_CUT:
                hs = []
                for i in range(n):
                    u = uv.take()
                    got = {}

                    def conved(ps, t, ft, dst, dfree):
                        raw = sg.take()
                        a = act.op(lambda e: e.copy(raw.ap[:, PADW:], ps), t, raw.free, zt)
                        w = [vec("fconv", 44 * j + ft) for j in range(3)]
                        x = dve.op(lambda e: e.tensor_scalar(dst, raw.ap[:, 2:], w[2], vec("fconv_b", ft), ALU.mult, ALU.add), a, dfree, v_tok)
                        x = dve.op(lambda e: e.scalar_tensor_tensor(dst, raw.ap[:, 1:T + 1], w[1], dst, ALU.mult, ALU.add), x)
                        x = dve.op(lambda e: e.scalar_tensor_tensor(dst, raw.ap[:, 0:T], w[0], dst, ALU.mult, ALU.add), x)
                        raw.free = [x]
                        return a, x

                    if conv:
                        gb, vb = cb.bufs

                        def gate(ps, t):
                            a, x = conved(ps, t, k0 + i, gb.ap, gb.free)
                            got["g"] = act.op(lambda e: e.activation(gb.ap, gb.ap, ACT.Silu), x)
                            return [a]

                        def val(ps, t):
                            a, x = conved(ps, t, 22 + k0 + i, vb.ap, vb.free)
                            got["v"] = dve.op(lambda e: e.tensor_tensor(u.ap, gb.ap, vb.ap, ALU.mult), x, got["g"], u.free)
                            gb.free = vb.free = [got["v"]]
                            return [a]
                    else:
                        s = sg.take()

                        def gate(ps, t):
                            m = dve.op(lambda e: e.tensor_tensor(s.ap[:, 0:T], ps, rstd, ALU.mult), t, s.free, root())
                            got["g"] = act.op(lambda e: e.activation(s.ap[:, 0:T], s.ap[:, 0:T], ACT.Silu), m)
                            return [m]

                        def val(ps, t):
                            m = dve.op(lambda e: e.tensor_tensor(u.ap, ps, rstd, ALU.mult), t, u.free)
                            got["v"] = dve.op(lambda e: e.tensor_tensor(u.ap, u.ap, s.ap[:, 0:T], ALU.mult), m, got["g"])
                            s.free = [got["v"]]
                            return [m]

                    product(wu, k0 + i, hx, gate)
                    product(wu, 22 + k0 + i, hx, val)
                    r = split((H[0][:, i, :], H[1][:, i, :]), u.ap, got["v"], h_free)
                    u.free = r
                    hs.append((H[0][:, i, :], H[1][:, i, :], r))
                finish = tail(sg.bufs, uv.bufs) if k0 + n == 22 else None
                for ft in range(8):
                    def ev(ps, t):
                        if out_scale is None:
                            d = dve.op(lambda e: e.tensor_tensor(Xacc[:, ft, :], ps, Xacc[:, ft, :], ALU.add), t, acc_t[ft])
                        else:
                            d = dve.op(lambda e: e.scalar_tensor_tensor(Xacc[:, ft, :], ps, out_scale(ft), Xacc[:, ft, :], ALU.mult, ALU.add),
                                       t, acc_t[ft])
                        acc_t[ft] = [d]
                        if finish:
                            finish(ft, d)
                        return [d]
                    product(wd, ft, hs, ev, k0)
                h_free = [pe.last]
                k0 += n
            return acc_t

        mark = top[0]
        HN = [(XH[0][:, k, :], XH[1][:, k, :], hn[k]) for k in range(8)]
        rstd1 = sb([128, T])
        root_tok = []

        def root():
            if not root_tok:
                pb = mmps.take()
                t = ones_sum([(sq_acc, sq_last())], pb.ap, pb.free)[-1]
                a, x = inv_root(pb.ap, T, rstd1, t)
                pb.free = [a]
                root_tok.append(x)
            return root_tok

        tails = {}

        def tail1(sgb, uvb):
            sa, st_ = sgb[0].ap[:, 0:T], sgb[1].ap[:, 0:T]
            add, last = square_sum(sa, [st_], sgb[0].free, sgb[1].free)
            padd = plain_sum(uvb[0].ap, uvb[0].free)
            tails[1] = dict(sq=sa, last=last, sum=uvb[0].ap)

            def finish(ft, d):
                add(X2[:, ft, :], d)
                tails[1]["tok"] = padd(X2[:, ft, :], d, vec("fin_g", ft))
            return finish

        def tail2(sgb, uvb):
            padd = plain_sum(uvb[0].ap, uvb[0].free)
            tails[2] = dict(sum=uvb[0].ap)

            def finish(ft, d):
                tails[2]["tok"] = padd(X1[:, ft, :], d)
            return finish

        acc = ffn(X2, [None] * 8, "w_up", "w_down", HN, False, None, rstd1, root, tail1)
        probe("x3", X2, acc)
        if dump is not None and "x3" in dump:
            barrier()
        top[0] = mark

        sh_a, sc_a, gt_a, sh_f, sc_f, gt_f = (lambda k, o=o, n=1: mod[:, o + k:o + k + n] for o in (0, 8, 16, 24, 32, 40))
        cmb = []
        for n, (g, o, sc, sh) in enumerate((("ln0_g", "ln0_b", sc_a, sh_a), ("ln1_g", "ln1_b", sc_f, sh_f))):
            gs, bs, ga, ba = (comb[:, 32 * n + 8 * j:32 * n + 8 * j + 8] for j in range(4))
            c1 = dve.op(lambda e: e.tensor_tensor(gs, vec(g, 0, 8), sc(0, n=8), ALU.mult), md2, v_tok)
            c2 = dve.op(lambda e: e.tensor_tensor(bs, vec(o, 0, 8), sc(0, n=8), ALU.mult))
            c3 = dve.op(lambda e: e.tensor_tensor(bs, bs, sh(0, n=8), ALU.add), c2)
            c4 = dve.op(lambda e: e.tensor_scalar(ga, vec(g, 0, 8), ALPHA, None, ALU.mult))
            c5 = dve.op(lambda e: e.tensor_scalar(ba, vec(o, 0, 8), ALPHA, None, ALU.mult))
            cmb.append((gs, bs, ga, ba, [c1, c3, c4, c5]))

        def modulated(X, ready, c, tmp):
            gs, bs, _, _, tok = cmb[c]
            res = []
            for k in range(8):
                b = tmp.take()
                h = act.op(lambda e: e.activation(b.ap, X[:, k, :], ACT.Identity, scale=gs[:, k:k + 1], bias=bs[:, k:k + 1]), ready[k], tok, b.free)
                b.free = split((XH[0][:, k, :], XH[1][:, k, :]), b.ap, h)
                res.append((XH[0][:, k, :], XH[1][:, k, :], b.free))
            return res

        def residual(X, ready, c):
            _, _, ga, ba, tok = cmb[c]
            return [[act.op(lambda e, k=k: e.activation(X[:, k, :], X[:, k, :], ACT.Identity, scale=ga[:, k:k + 1], bias=ba[:, k:k + 1]), ready[k], tok)]
                    for k in range(8)]

        sm = sb([128, T])
        rstd = sb([128, T])
        keep = top[0]
        tmp = Rot([sb([128, T]) for _ in range(3)])
        rfin, mu = sb([128, T]), sb([128, T])
        t1 = tails[1]
        pb = mmps.take()
        t = ones_sum([(t1["sq"], t1["last"]())], pb.ap, pb.free)[-1]
        a, fin = inv_root(pb.ap, T, rfin, t)
        pb.free = [a]
        xc = centred(X2, (t1["sum"], t1["tok"]), mu, tmp, rstd, "fin_g", (rfin, fin))
        HX = modulated(X2, xc, 0, tmp)
        smt = product("w_in2", 28, HX, lambda ps, t: [act.op(lambda e: e.copy(sm, ps), t)])
        x1 = residual(X2, [h[2] for h in HX], 0)
        sp_t = [dma(sp, spill[:, k, :], X2[:, k, :], x1[k], lane=lane8[k]) for k in range(8)]
        barrier()
        top[0] = keep
        X1 = X2
        O = X1

        upper, up_t = const("upper")
        base_g = top[0]

        def delta():
            mS, ms_t = const("mS")
            mT, mt_t = const("mT")
            lev, lv_t = const("lev")
            abt = sb([128, 8, 8])
            pb = mmps.take()

            def ev(ps, t):
                v = ps.rearrange("p (a c) -> p a c", a=8)
                return [dve.op(lambda e: e.tensor_copy(abt[:, :, 0:4], v[:, :, 0:4]), t),
                        dve.op(lambda e: e.tensor_copy(abt[:, :, 4:8], v[:, :, 32:36]), t)]
            at_ = transposes(sm, ev, 8, smt, pb)
            beta, la, t1, t2 = (sb([128, 8, 4]) for _ in range(4))
            na = sb([128, 4])
            bet = act.op(lambda e: e.activation(beta, abt[:, :, 4:8], ACT.Sigmoid), at_)
            nat = act.op(lambda e: e.activation(na, vec("alog", 0, 4), ACT.Exp), v_tok)
            x = dve.op(lambda e: e.tensor_tensor(la, abt[:, :, 0:4], vec("dtb", 0, 4).unsqueeze(1).to_broadcast([128, 8, 4]), ALU.add), at_, v_tok)
            x1_ = act.op(lambda e: e.activation(t1, la, ACT.Abs), x)
            x1_ = act.op(lambda e: e.activation(t1, t1, ACT.Exp, scale=-1.0), x1_)
            x1_ = act.op(lambda e: e.activation(t1, t1, ACT.Ln, bias=1.0), x1_)
            x2_ = dve.op(lambda e: e.scalar_tensor_tensor(la, la, 0.0, t1, ALU.max, ALU.add), x1_, x)
            x3_ = dve.op(lambda e: e.tensor_scalar(na, na, -1.0, None, ALU.mult), nat)
            lat = dve.op(lambda e: e.tensor_tensor(la, la, na.unsqueeze(1).to_broadcast([128, 8, 4]), ALU.mult), x2_, x3_)
            pb = mmps.take()
            t = pe.op(lambda e, pb=pb: e.matmul(pb.ap[:, 0:32], upper, la.rearrange("p a b -> p (a b)"), start=True, stop=True), lat, up_t, pb.free)
            G, nG, eG, kl = (sb([128, 8, 4]) for _ in range(4))
            fl = lambda z: z.rearrange("p a b -> p (a b)")
            g1 = dve.op(lambda e, pb=pb: e.tensor_copy(fl(G), pb.ap[:, 0:32]), t)
            g2 = dve.op(lambda e, pb=pb: e.tensor_scalar(fl(nG), pb.ap[:, 0:32], -1.0, None, ALU.mult), t)
            pb.free = [g1, g2]
            pb = mmps.take()
            t = pe.op(lambda e, pb=pb: e.matmul(pb.ap[:, 0:32], ones, la.rearrange("p a b -> p (a b)"), start=True, stop=True), lat, pb.free)
            gl = sb([128, 8, 4])
            glt = act.op(lambda e, pb=pb: e.activation(fl(gl), pb.ap[:, 0:32], ACT.Exp), t)
            klt = dve.op(lambda e, pb=pb: e.tensor_tensor(fl(kl), pb.ap[:, 0:32], fl(G), ALU.subtract), t, g1, glt)
            pb.free = [glt, klt]
            klt = act.op(lambda e: e.activation(fl(kl), fl(kl), ACT.Exp), klt)
            egt = act.op(lambda e: e.activation(fl(eG), fl(G), ACT.Exp), g1)
            nbt = dve.op(lambda e: e.scalar_tensor_tensor(fl(eG), fl(eG), -1.0, fl(beta), ALU.mult, ALU.mult), egt, bet)
            small = [g1, g2, glt, klt, nbt, bet, lat]
            base_d = top[0]
            res = []
            for hp in range(2):
                barrier()
                top[0] = base_d
                FT = [[sb([128, T]) for _ in range(3)] for _ in range(2)]
                KT, VT = [[sb([128, 8, 128]) for _ in range(2)] for _ in range(2)]
                ovl = top[0]
                raw = Rot([sb([128, T + 3]) for _ in range(2)])
                tmpR = Rot([sb([128, T]) for _ in range(2)])
                zt = [dve.op(lambda e, b=b: e.memset(b.ap[:, 0:3], 0.0)) for b in raw.bufs]
                f_tok, k_tok, v2_tok = [], [], []
                for hh in range(2):
                    h = 2 * hp + hh
                    toks = []
                    for part in range(3):
                        dst = FT[hh][part]
                        r = raw.take()
                        ft = 4 * part + h
                        pt = product("w_in2", ft, HX, lambda ps, t: [act.op(lambda e: e.copy(r.ap[:, 3:], ps), t, r.free, zt)])
                        w = [vec("conv", 12 * j + ft) for j in range(4)]
                        x = dve.op(lambda e: e.tensor_scalar(dst, r.ap[:, 3:], w[3], None, ALU.mult), pt, v_tok)
                        for j in range(3):
                            x = dve.op(lambda e, j=j: e.scalar_tensor_tensor(dst, r.ap[:, j:j + T], w[j], dst, ALU.mult, ALU.add), x)
                        r.free = [x]
                        x = act.op(lambda e: e.activation(dst, dst, ACT.Silu), x)
                        if part < 2:
                            b = tmpR.take()
                            sq = act.op(lambda e, b=b, dst=dst: e.activation(b.ap, dst, ACT.Square), x, b.free)
                            pb = mmps.take()
                            t = ones_sum([(b.ap, sq)], pb.ap, pb.free)[-1]
                            a, d = inv_root(pb.ap, 1, b.ap, t)
                            pb.free = [a]
                            sc = 128.0 ** -0.5 if part == 0 else 1.0
                            x = dve.op(lambda e, b=b, dst=dst, sc=sc: e.scalar_tensor_tensor(dst, dst, sc, b.ap, ALU.mult, ALU.mult), d)
                            b.free = [x]
                        toks.append(x)
                    f_tok.append(toks)
                    pb = mmps.take()

                    def evk(ps, t):
                        return [act.op(lambda e, c=c: e.activation(KT[hh][:, c, :], ps[:, c * 128:(c + 1) * 128], ACT.Identity,
                                                                   scale=kl[:, c, h:h + 1]), t, klt) for c in range(8)][-1:]
                    k_tok.append(transposes(FT[hh][1], evk, 8, toks[1], pb))
                    pb = mmps.take()

                    def evv(ps, t):
                        return [dve.op(lambda e, c=c: e.tensor_scalar(VT[hh][:, c, :], ps[:, c * 128:(c + 1) * 128], beta[:, c, h:h + 1],
                                                                      None, ALU.mult), t, bet) for c in range(8)][-1:]
                    v2_tok.append(transposes(FT[hh][2], evv, 8, toks[2], pb))
                    zdst = FT[hh][2]
                    zz = product("w_in2", 12 + h, HX, lambda ps, t: [act.op(lambda e: e.activation(zdst, ps, ACT.Silu), t, v2_tok[hh], k_tok[hh])])
                    f_tok[hh].append(zz)
                barrier()
                top[0] = ovl
                for q in (act, dve):
                    q.extra = q.extra + sp_t
                Z = O[:, 4:6, :].rearrange("p a (b c) -> p (a b) c", b=2)
                AT = O[:, 6:8, :].rearrange("p a (b c) -> p (a b) c", b=2)
                units = [[(2 * b + x, hh) for x in range(2) for hh in range(2)] for b in range(4)]
                WB = [dict(M=sb([128, 512]), Tm=sb([128, 512]), Y=sb([128, 512]), Ml=sb([128, 512])) for _ in range(2)]
                rot = Rot(banks[0:8])
                u_tok = []

                def prep(b, wb):
                    us = units[b]
                    Mm, Tm, Yy, Ml = wb["M"], wb["Tm"], wb["Y"], wb["Ml"]
                    Zb, ATb = Z[:, b, :], AT[:, b, :]
                    fr = wb.get("free", [])
                    sl = [slice(128 * n, 128 * n + 128) for n in range(4)]
                    lb = [dve.op(lambda e, n=n, c=c, hh=hh: e.tensor_scalar(Ml[:, sl[n]], ones, la[:, c, 2 * hp + hh:2 * hp + hh + 1], None, ALU.mult),
                                 fr, lat, o_tok) for n, (c, hh) in enumerate(us)]
                    bg, ba, bq = rot.take(), rot.take(), rot.take()
                    for n in range(4):
                        tg = pe.op(lambda e, n=n: e.matmul(bg.ap[:, sl[n]], Ml[:, sl[n]], upper, start=True, stop=True), lb, bg.free, up_t)
                    yield
                    for n, (c, hh) in enumerate(us):
                        kx, qx = FT[hh][1], FT[hh][0]
                        cc = slice(128 * c, 128 * c + 128)
                        ta = pe.op(lambda e, n=n, kx=kx, cc=cc: e.matmul(ba.ap[:, sl[n]], kx[:, cc], kx[:, cc], start=True, stop=True), ba.free)
                        tq = pe.op(lambda e, n=n, kx=kx, qx=qx, cc=cc: e.matmul(bq.ap[:, sl[n]], kx[:, cc], qx[:, cc], start=True, stop=True), bq.free)
                    m3 = mS.unsqueeze(1).to_broadcast([128, 4, 128])
                    m4 = mT.unsqueeze(1).to_broadcast([128, 4, 128])
                    v3 = lambda z: z.rearrange("p (n c) -> p n c", n=4)
                    d1 = dve.op(lambda e: e.scalar_tensor_tensor(v3(Tm), v3(bg.ap), -1.0, m3, ALU.mult, ALU.add), tg, fr, ms_t)
                    d2 = dve.op(lambda e: e.tensor_tensor(v3(Yy), v3(bg.ap), m4, ALU.add), tg, fr, mt_t)
                    bg.free = [d2]
                    e1 = [act.op(lambda e, n=n, c=c, hh=hh: e.activation(Tm[:, sl[n]], Tm[:, sl[n]], ACT.Exp, bias=G[:, c, 2 * hp + hh:2 * hp + hh + 1]),
                                 d1, g1) for n, (c, hh) in enumerate(us)]
                    e2 = [act.op(lambda e, n=n, c=c, hh=hh: e.activation(Yy[:, sl[n]], Yy[:, sl[n]], ACT.Exp, bias=nG[:, c, 2 * hp + hh:2 * hp + hh + 1]),
                                 d2, g2) for n, (c, hh) in enumerate(us)]
                    yield
                    ms = [dve.op(lambda e, n=n, c=c, hh=hh: e.scalar_tensor_tensor(Mm[:, sl[n]], ba.ap[:, sl[n]], beta[:, c, 2 * hp + hh:2 * hp + hh + 1],
                                                                                  Tm[:, sl[n]], ALU.mult, ALU.mult), ta, e1, fr)
                          for n, (c, hh) in enumerate(us)]
                    ba.free = [ms[-1]]
                    at = dve.op(lambda e: e.tensor_tensor(ATb, bq.ap, Yy, ALU.mult), tq, e2)
                    bq.free = [at]
                    i3 = ident.unsqueeze(1).to_broadcast([128, 4, 128])

                    def lmask(l, w):
                        m = lev[:, 128 * l:128 * l + 128].unsqueeze(1).to_broadcast([128, 4, 128])
                        return dve.op(lambda e: e.tensor_tensor(v3(Ml), v3(Mm), m, ALU.mult), w, ms, lv_t)
                    ml = lmask(0, tg)
                    bt = rot.take()
                    for n in range(4):
                        tt_ = pe.op(lambda e, n=n: e.transpose(bt.ap[:, sl[n]], Ml[:, sl[n]], ident), ml, bt.free)
                    zt_ = dve.op(lambda e: e.scalar_tensor_tensor(v3(Zb), v3(bt.ap), -1.0, i3, ALU.mult, ALU.add), tt_)
                    bt.free = [zt_]
                    tm_ = dve.op(lambda e: e.scalar_tensor_tensor(v3(Tm), v3(Ml), -1.0, i3, ALU.mult, ALU.add), ml, ms)
                    yield
                    for l in range(1, 7):
                        ml = lmask(l, [tt_, tm_])
                        b1 = rot.take()
                        for n in range(4):
                            ty = pe.op(lambda e, n=n: e.matmul(b1.ap[:, sl[n]], Ml[:, sl[n]], Zb[:, sl[n]], start=True, stop=True), ml, zt_, b1.free)
                        ye = act.op(lambda e: e.copy(Yy, b1.ap), ty, at)
                        b1.free = [ye]
                        yield
                        b2, b3 = rot.take(), rot.take()
                        for n in range(4):
                            tx = pe.op(lambda e, n=n: e.matmul(b2.ap[:, sl[n]], Tm[:, sl[n]], Yy[:, sl[n]], start=True, stop=True), ye, tm_, b2.free)
                        if l < 6:
                            for n in range(4):
                                tt_ = pe.op(lambda e, n=n: e.matmul(b3.ap[:, sl[n]], Yy[:, sl[n]], Tm[:, sl[n]], start=True, stop=True), b3.free)
                        zt_ = dve.op(lambda e: e.tensor_tensor(Zb, Zb, b2.ap, ALU.subtract), tx, ty)
                        b2.free = [zt_]
                        if l < 6:
                            tm_ = dve.op(lambda e: e.tensor_tensor(Tm, Tm, b3.ap, ALU.subtract), tt_, tx)
                            b3.free = [tm_]
                        else:
                            tt_ = tx
                        yield
                    wb["free"] = [zt_, tx]
                    u_tok.append([zt_, at])

                for b in (0, 2):
                    gens = [prep(b, WB[0]), prep(b + 1, WB[1])]
                    live = True
                    while live:
                        live = False
                        for gnr in gens:
                            try:
                                next(gnr)
                                live = True
                            except StopIteration:
                                pass
                barrier()
                ex = WB[1]["M"]
                qd_t = []
                ex_free = []
                lbuf = WB[0]["Ml"]
                for hh in range(2):
                    for c4 in range(2):
                        lb = [dve.op(lambda e, n=n, hh=hh, c4=c4: e.tensor_scalar(lbuf[:, 128 * n:128 * n + 128], ones,
                                                                               la[:, 4 * c4 + n, 2 * hp + hh:2 * hp + hh + 1], None, ALU.mult), ex_free)
                              for n in range(4)]
                        bg = rot.take()
                        for n in range(4):
                            tg = pe.op(lambda e, n=n, bg=bg: e.matmul(bg.ap[:, 128 * n:128 * n + 128], lbuf[:, 128 * n:128 * n + 128], upper,
                                                                      start=True, stop=True), lb, bg.free)
                        a = act.op(lambda e, bg=bg: e.activation(ex, bg.ap, ACT.Exp), tg, ex_free)
                        bg.free = [a]
                        q = FT[hh][0][:, 512 * c4:512 * c4 + 512]
                        d = dve.op(lambda e, q=q: e.tensor_tensor(q, q, ex, ALU.mult), a)
                        ex_free = [d, tg]
                        qd_t.append(d)
                cut = lambda w, n: w[:, 128 * n:128 * n + 128]
                S = [[cut(WB[1]["Tm"], 2 * x + y) for y in range(2)] for x in range(2)]
                rb_ = [cut(WB[0]["Y"], x) for x in range(2)]
                vn = [[cut(WB[1]["Y"], 2 * x + y) for y in range(2)] for x in range(2)]
                s_tok = [None, None]
                o_last = [None, None]
                vn_free = [[[], []], [[], []]]
                s_read = [[[], []], [[], []]]
                rb_free = [[], []]
                oe = [[], []]
                for c in range(8):
                    for hh in range(2):
                        h = 2 * hp + hh
                        cc = slice(128 * c, 128 * c + 128)
                        b, n = c // 2, 2 * (c % 2) + hh
                        un = slice(128 * n, 128 * n + 128)
                        So, Sn = S[hh][c % 2], S[hh][(c + 1) % 2]
                        vb = VT[hh][:, c, :]
                        if c > 0:
                            p1 = rot.take()
                            t = pe.op(lambda e, p1=p1, hh=hh, cc=cc, So=So: e.matmul(p1.ap[:, 0:128], FT[hh][1][:, cc], So, start=True, stop=True),
                                      p1.free, s_tok[hh])
                            d = dve.op(lambda e, p1=p1, hh=hh, c=c, h=h, vb=vb: e.scalar_tensor_tensor(
                                rb_[hh], p1.ap[:, 0:128], eG[:, c, h:h + 1], vb, ALU.mult, ALU.add), t, rb_free[hh])
                            p1.free = [d]
                            rx = rb_[hh]
                        else:
                            d, rx = None, vb
                        p2 = rot.take()
                        t = pe.op(lambda e, p2=p2, b=b, un=un, rx=rx: e.matmul(p2.ap[:, 0:128], Z[:, b, un], rx, start=True, stop=True), p2.free, d)
                        rb_free[hh] = [t]
                        vx = vn[hh][c % 2]
                        va = act.op(lambda e, p2=p2, vx=vx: e.copy(vx, p2.ap[:, 0:128]), t, vn_free[hh][c % 2])
                        p2.free = [va]
                        p4 = rot.take()
                        if c > 0:
                            pe.op(lambda e, p4=p4, So=So, hh=hh, cc=cc: e.matmul(p4.ap[:, 0:128], So, FT[hh][0][:, cc], start=True, stop=False),
                                  p4.free, qd_t)
                        to = pe.op(lambda e, p4=p4, vx=vx, b=b, un=un, c=c: e.matmul(p4.ap[:, 0:128], vx, AT[:, b, un], start=(c == 0), stop=True),
                                   va, p4.free)
                        oa = act.op(lambda e, p4=p4, h=h, cc=cc: e.copy(O[:, h, cc], p4.ap[:, 0:128]), to)
                        p4.free = [oa]
                        s_read[hh][c % 2] = [to]
                        oe[hh] = [oa]
                        tl = to
                        if c < 7:
                            p3 = rot.take()
                            t3 = pe.op(lambda e, p3=p3, hh=hh, c=c, vx=vx: e.matmul(p3.ap[:, 0:128], KT[hh][:, c, :], vx, start=True, stop=True), p3.free, va)
                            tl = t3
                            if c == 0:
                                s_tok[hh] = dve.op(lambda e, p3=p3, Sn=Sn: e.tensor_copy(Sn, p3.ap[:, 0:128]), t3, s_read[hh][(c + 1) % 2])
                            else:
                                s_tok[hh] = dve.op(lambda e, p3=p3, Sn=Sn, So=So, c=c, h=h: e.scalar_tensor_tensor(
                                    Sn, So, gl[:, c, h:h + 1], p3.ap[:, 0:128], ALU.mult, ALU.add), t3, s_read[hh][(c + 1) % 2], s_tok[hh])
                            p3.free = [s_tok[hh]]
                        vn_free[hh][c % 2] = [tl]
                barrier()
                for b_ in mmps.bufs:
                    b_.free = []
                top[0] = ovl
                tmpR = Rot([sb([128, T]) for _ in range(2)])
                for hh in range(2):
                    h = 2 * hp + hh
                    pb = mmps.take()
                    probe(f"odn{h}", O[:, h, :], oe[hh])
                    r = mean_square_inv([(O[:, h, :], None)], 128, tmpR, rstd, pb, res[-1] if res else None)
                    d = dve.op(lambda e, h=h: e.scalar_tensor_tensor(O[:, h, :], O[:, h, :], vec("dn_g"), rstd, ALU.mult, ALU.mult), r)
                    d2 = dve.op(lambda e, h=h, hh=hh: e.tensor_tensor(O[:, h, :], O[:, h, :], FT[hh][2], ALU.mult), d)
                    res.append([d2])
            return res

        o_tok = [o_tok] if not isinstance(o_tok, list) else o_tok
        otk = delta()
        barrier()
        top[0] = base_g

        def gla():
            mG, mg_t = const("mG")
            scanm, sc_t = const("scanm")
            g2 = sb([128, 256])
            g2_t = dma(sp, g2, A["gate2"])
            base = top[0]
            res = []
            for hp in range(2):
                barrier()
                top[0] = base
                q, k, bb, tA, tB = (sb([128, T]) for _ in range(5))
                kdt = sb([128, 8, 128])
                vt = sb([128, 8, 256])
                zs = [sb([128, T]) for _ in range(2)]
                bl = sb([128, 16])
                egl = sb([128, 16])
                St = sb([128, 16, 128])
                at = sb([128, 2, 8, 128])
                pb = mmps.take()
                for h in range(2):
                    t = pe.op(lambda e, h=h, pb=pb: e.matmul(pb.ap[:, 512 * h:512 * h + 512], g2[:, 128 * hp:128 * hp + 128],
                                                             sm[:, 512 * h:512 * h + 512], start=True, stop=True), g2_t, smt, pb.free)
                a = act.op(lambda e, pb=pb: e.activation(tA, pb.ap, ACT.Identity, bias=vec("gla_bg", hp)), t, v_tok)
                pb.free = [a]
                x = act.op(lambda e: e.activation(tB, tA, ACT.Abs), a)
                x = act.op(lambda e: e.activation(tB, tB, ACT.Exp, scale=-1.0), x)
                x = act.op(lambda e: e.activation(tB, tB, ACT.Ln, bias=1.0), x)
                d = dve.op(lambda e: e.scalar_tensor_tensor(tA, tA, 0.0, tB, ALU.min, ALU.subtract), x)
                d = dve.op(lambda e: e.tensor_scalar(tA, tA, 1.0 / 16, None, ALU.mult), d)
                bt = dve.op(lambda e: e.tensor_tensor_scan(bb, scanm, tA, 0.0, ALU.mult, ALU.add), d, sc_t)
                b3 = bb.rearrange("p (c t) -> p c t", t=64)
                blt = dve.op(lambda e: e.tensor_copy(bl.unsqueeze(2), b3[:, :, 63:64]), bt)
                egt = act.op(lambda e: e.activation(egl, bl, ACT.Exp), blt)
                qt = product("w_in2", 16 + hp, HX, lambda ps, t: [act.op(lambda e: e.mul(q, ps, 0.125), t)])
                kt = product("w_in2", 18 + hp, HX, lambda ps, t: [act.op(lambda e: e.copy(k, ps), t)])
                e1 = act.op(lambda e: e.activation(tA, bb, ACT.Exp), bt)
                qd = dve.op(lambda e: e.tensor_tensor(q, q, tA, ALU.mult), e1, qt)
                d = dve.op(lambda e: e.tensor_tensor(tB.rearrange("p (c t) -> p c t", t=64), bl.unsqueeze(2).to_broadcast([128, 16, 64]),
                                                     b3, ALU.subtract), blt)
                e2 = act.op(lambda e: e.activation(tB, tB, ACT.Exp), d)
                kd = dve.op(lambda e: e.tensor_tensor(tB, tB, k, ALU.mult), e2, kt)
                pb = mmps.take()
                kdT = transposes(tB, lambda ps, t: [dve.op(lambda e: e.tensor_copy(kdt.rearrange("p a b -> p (a b)"), ps), t)], 8, kd, pb)
                e3 = act.op(lambda e: e.activation(tA, bb, ACT.Exp, scale=-1.0), qd)
                kn = dve.op(lambda e: e.tensor_tensor(k, k, tA, ALU.mult), e3, kd)
                vtk = []
                for hh in range(2):
                    vv = product("w_in2", 20 + 2 * hp + hh, HX, lambda ps, t: [act.op(lambda e: e.copy(bb, ps), t, e3, vtk)])
                    pb = mmps.take()
                    vtk = transposes(bb, lambda ps, t: [dve.op(lambda e: e.tensor_copy(
                        vt[:, :, 128 * hh:128 * hh + 128], ps.rearrange("p (a b) -> p a b", a=8)), t)], 8, vv, pb)
                zt = []
                for hh in range(2):
                    zt.append(product("w_in2", 24 + 2 * hp + hh, HX, lambda ps, t: [act.op(lambda e: e.activation(zs[hh], ps, ACT.Silu), t)]))
                att = []
                for hh in range(2):
                    rows = slice(64 * hh, 64 * hh + 64)
                    pb = mmps.take()
                    for a_ in range(8):
                        cc = slice(128 * a_, 128 * a_ + 128)
                        t = pe.op(lambda e, cc=cc, rows=rows, pb=pb: e.matmul(pb.ap[:, cc], k[rows, cc], q[rows, cc], start=True, stop=True),
                                  kn, qd, pb.free)
                    d = dve.op(lambda e, hh=hh, pb=pb: e.tensor_tensor(at[:, hh, :, :], pb.ap.rearrange("p (a b) -> p a b", a=8),
                                                                       mG.unsqueeze(1).to_broadcast([128, 8, 128]), ALU.mult), t, mg_t)
                    pb.free = [d]
                    att.append(d)
                st = [dve.op(lambda e: e.memset(St[:, 0, :], 0.0))]
                for c in range(15):
                    a_, r = c // 2, slice(64 * (c % 2), 64 * (c % 2) + 64)
                    pb = mmps.take()
                    t = pe.op(lambda e, a_=a_, r=r, pb=pb: e.matmul(pb.ap[:, 0:256], kdt[r, a_, :], vt[r, a_, :], start=True, stop=True),
                              kdT, vtk, pb.free)
                    ns = []
                    for hh in range(2):
                        rows = slice(64 * hh, 64 * hh + 64)
                        ns.append(dve.op(lambda e, c=c, rows=rows, hh=hh, pb=pb: e.scalar_tensor_tensor(
                            St[rows, c + 1, :], St[rows, c, :], egl[rows, c:c + 1], pb.ap[rows, 128 * hh:128 * hh + 128], ALU.mult, ALU.add),
                            t, st, egt))
                    pb.free = ns
                    st = ns
                for hh in range(2):
                    rows = slice(64 * hh, 64 * hh + 64)
                    pb = mmps.take()
                    for a_ in range(8):
                        cc = slice(128 * a_, 128 * a_ + 128)
                        pe.op(lambda e, cc=cc, a_=a_, hh=hh, pb=pb: e.matmul(pb.ap[:, cc], vt[:, a_, 128 * hh:128 * hh + 128], at[:, hh, a_, :],
                                                                             start=True, stop=False, skip_group_check=True), att, pb.free)
                        for x in range(2):
                            c = 2 * a_ + x
                            ch = slice(64 * c, 64 * c + 64)
                            t = pe.op(lambda e, ch=ch, c=c, rows=rows, pb=pb: e.matmul(pb.ap[:, ch], St[rows, c, :], q[rows, ch],
                                                                                       start=False, stop=True, skip_group_check=True), st)
                    f = 4 + 2 * hp + hh
                    oa = act.op(lambda e, f=f, pb=pb: e.copy(O[:, f, :], pb.ap), t)
                    pb.free = [oa]
                    probe(f"ogla{f - 4}", O[:, f, :], oa)
                    tr = Rot([tA, tB])
                    barrier()
                    pb = mmps.take()
                    r_ = mean_square_inv([(O[:, f, :], oa)], 128, tr, rstd, pb)
                    d = dve.op(lambda e, f=f: e.scalar_tensor_tensor(O[:, f, :], O[:, f, :], vec("gla_g"), rstd, ALU.mult, ALU.mult), r_)
                    d2 = dve.op(lambda e, f=f, hh=hh: e.tensor_tensor(O[:, f, :], O[:, f, :], zs[hh], ALU.mult), d, zt[hh])
                    res.append([d2])
            return res

        otk = otk + gla()
        barrier()
        top[0] = base_g
        probe("o", O, otk)
        ox = []
        for k in range(8):
            r = split((XH[0][:, k, :], XH[1][:, k, :]), O[:, k, :], otk[k])
            ox.append((XH[0][:, k, :], XH[1][:, k, :], r))
        bt = barrier()
        rt = [dma(sp, X1[:, k, :], spill[:, k, :], bt, sp_t, lane=lane8[k]) for k in range(8)]
        xa = []
        tmp = Rot([sb([128, T]) for _ in range(3)])
        mu, sum1 = sb([128, T]), sb([128, T])
        add1 = plain_sum(sum1)
        for ft in range(8):
            def ev(ps, t):
                d = dve.op(lambda e: e.scalar_tensor_tensor(X1[:, ft, :], ps, gt_a(ft), X1[:, ft, :], ALU.mult, ALU.add), t, rt[ft], md2)
                xa.append(add1(X1[:, ft, :], d))
                return [d]
            product("w_o", ft, ox, ev)
        xc = centred(X1, (sum1, xa[-1]), mu, tmp, rstd)
        HX2 = modulated(X1, xc, 1, tmp)
        al = residual(X1, [h[2] for h in HX2], 1)
        top[0] = mark
        acc = ffn(X1, al, "w_up2", "w_down2", HX2, True, gt_f, None, None, tail2)
        probe("preln2", X1, acc)
        if dump is not None and "preln2" in dump:
            barrier()
        top[0] = mark
        tmp = Rot([sb([128, T]) for _ in range(2)])
        rstd, mu = sb([128, T]), sb([128, T])
        xc = centred(X1, (tails[2]["sum"], tails[2]["tok"]), mu, tmp, rstd)
        xo = [act.op(lambda e, k=k: e.activation(X1[:, k, :], X1[:, k, :], ACT.Identity, scale=vec("ln2_g", k), bias=vec("ln2_b", k)), xc[k], v_tok)
              for k in range(8)]
        st = [dma(sp, out[:, k, :], X1[:, k, :], xo[k], lane=lane8[k]) for k in range(8)]
        assert w_at[2] == len(plan)
        sp.op(None, st, dumps, sp_t)
        queues = (pe, act, dve, pool, sp)
        for q in queues:
            q.mark()
        for q in queues:
            q.number()
        print("sbuf", high[0], "sems", sem_n[0], [len(q.ops) for q in queues]) if dump is not None else None
        block = ctx.enter_context(nc.Block())
        block.tensor(lambda e: pe.emit(e))
        block.scalar(lambda e: act.emit(e))
        block.vector(lambda e: dve.emit(e))
        block.gpsimd(lambda e: pool.emit(e))
        block.sync(lambda e: sp.emit(e))


def layouts(i):
    f = lambda a: np.ascontiguousarray(a)
    a = {k: np.asarray(v) for k, v in i.items()}

    def wp(w):
        k, n = w.shape
        return f(w.reshape(k // 128, 128, n // 128, 128).transpose(2, 1, 0, 3))

    def cols(v):
        v = v.reshape(-1, 128)
        return v.T

    d = {"xT": f(a["x"][0].T.reshape(8, 128, T).transpose(1, 0, 2))}
    d["w_in"] = wp(a["w_in"][0])
    d["w_gate"] = f(np.concatenate([wp(a["w_gate"][0, b]) for b in range(4)]))
    r = 0
    for b, n in enumerate((512, 256, 512, 512)):
        d[f"w_br{b}"] = wp(a["w_branch"][0, r:r + n])
        r += n
    d["w_glu"] = wp(a["s5_w_glu"][0])
    d["w_out"] = wp(a["w_out"][0])
    d["w_up"] = wp(a["w_up"][0])
    d["w_down"] = wp(a["w_down"][0])
    w2 = a["w_in_2"][0]
    z = lambda n: np.zeros((1024, n), np.float32)
    small = np.concatenate([w2[:, 2048:2052], z(28), w2[:, 2052:2056], z(28), w2[:, 3592:3608], z(48)], axis=1)
    d["w_in2"] = wp(np.concatenate([w2[:, 0:2048], w2[:, 2056:3592], small], axis=1))
    d["w_o"] = wp(a["w_o_2"][0])
    d["w_up2"] = wp(a["ffn_w_up_2"][0])
    d["w_down2"] = wp(a["ffn_w_down_2"][0])
    d["w_ada"] = f(a["w_ada_2"][0].reshape(8, 128, 6144))
    d["pool_w"] = f(a["pool_w"][0].transpose(1, 0, 2))
    d["rel_bias"] = f(np.concatenate([a["rel_bias"], np.zeros((96, 12), np.float32)]))
    st = lambda v: v.reshape(16, 128, 16)
    bc = [st(a["s5_b_re"][0]), st(a["s5_b_im"][0]), st(a["s5_c_re"][0].transpose(0, 2, 1)), st(a["s5_c_im"][0].transpose(0, 2, 1))]
    d["s5bc"] = f(np.stack(bc).transpose(2, 0, 1, 3).reshape(128, 4, 256))
    d["gate2"] = f(np.concatenate([np.zeros((64, 256), np.float32), a["gla_w_gate2_2"][0], np.zeros((48, 256), np.float32)]))
    rep = lambda v: np.broadcast_to(v.reshape(1, -1), (128, v.size))
    v = {"attn_g": cols(a["attn_norm_g"]), "ffn_g": cols(a["ffn_norm_g"]), "fin_g": cols(a["final_norm_g"]),
         "ln0_g": cols(a["ln0_g_2"]), "ln0_b": cols(a["ln0_b_2"]), "ln1_g": cols(a["ln1_g_2"]), "ln1_b": cols(a["ln1_b_2"]),
         "ln2_g": cols(a["ln2_g_2"]), "ln2_b": cols(a["ln2_b_2"]), "pool_s": cols(a["pool_scale"]), "s5_d": cols(a["s5_d"]),
         "c": cols(a["c_2"]), "b_ada": cols(a["b_ada_2"]),
         "conv": a["dn_conv_2"][0].reshape(48, 128).T, "dn_g": cols(a["dn_norm_g_2"]), "gla_bg": cols(a["gla_b_gate_2"]),
         "gla_g": cols(a["gla_norm_g_2"]), "fconv": a["ffn_conv_2"][0].reshape(132, 128).T, "fconv_b": cols(a["ffn_conv_b_2"]),
         "alog": rep(a["dn_a_log_2"]), "dtb": rep(a["dn_dt_bias_2"]),
         "a_re": cols(a["s5_a_re"]), "a_im": cols(a["s5_a_im"]), "ldt": cols(np.repeat(a["s5_log_dt"][0], 64))}
    d["vecs"] = f(np.concatenate([v[n] for n in VCOLS], axis=1))
    for k, c in shape_constants().items():
        d["c_" + k] = c
    return d


def kernel(**inputs):
    import concourse.bacc as bacc
    from concourse.bass_utils import run_bass_kernel_spmd

    arrays = layouts(inputs)
    nc = bacc.Bacc("TRN2", target_bir_lowering=False, num_devices=1)
    A = {k: nc.dram_tensor("in_" + k, v.shape, F32, kind="ExternalInput").ap() for k, v in arrays.items()}
    out = nc.dram_tensor("out_0", (128, 8, T), F32, kind="ExternalOutput").ap()
    scr = nc.dram_tensor("scr", (3, T, 264), F32, kind="Internal").ap()
    spill = nc.dram_tensor("spill", (128, 8, T), F32, kind="Internal").ap()
    bsc = nc.dram_tensor("bsc", (4, 3, 384), F32, kind="Internal").ap()
    build(nc, A, out, scr, spill, bsc)
    r = run_bass_kernel_spmd(nc, [{"in_" + k: v for k, v in arrays.items()}], core_ids=[0])
    o = r.results[0]["out_0"]
    return np.ascontiguousarray(o.transpose(1, 0, 2).reshape(1024, T).T).reshape(1, T, 1024)
```

```python
import math

import numpy as np

import concourse.bass as bass
from concourse import mybir
from concourse.alu_op_type import AluOpType as ALU

F32 = mybir.dt.float32
F32R = mybir.dt.float32r
I32 = mybir.dt.int32
ACT = mybir.ActivationFunctionType
AXX = mybir.AxisListType.X

T = 1024
NEG = -1.0e30
EPS = 1e-6
ALPHA = 2.0 ** 0.25
MAGIC = 12582912.0
FFN_CUT = (6, 6, 5, 5)
DILS = (1, 4, 16)
HN_ = (0, 2, 1, 3)

VCOLS = {}
_at = 0
for _n, _w in (("attn_g", 8), ("ffn_g", 8), ("fin_g", 8), ("ln0_g", 8), ("ln0_b", 8), ("ln1_g", 8), ("ln1_b", 8),
               ("ln2_g", 8), ("ln2_b", 8), ("pool_s", 4), ("s5_d", 4), ("c", 8), ("b_ada", 48), ("conv", 48),
               ("dn_g", 1), ("gla_bg", 2), ("gla_g", 1), ("fconv", 132), ("fconv_b", 44), ("alog", 4), ("dtb", 4),
               ("a_re", 16), ("a_im", 16), ("ldt", 16)):
    VCOLS[_n] = (_at, _w)
    _at += _w
NV = _at


def t5_buckets(dil):
    dist = np.arange(129) * dil
    df = np.maximum(dist, 1).astype(np.float32)
    large = 16 + (np.log(df / np.float32(16)) / np.float32(math.log(2048 / 16)) * np.float32(16)).astype(np.int32)
    large = np.minimum(large, 31)
    return np.where(dist < 16, dist, large)


def shape_constants():
    c = {}
    i = np.arange(128)
    c["ident"] = np.eye(128, dtype=np.float32)
    c["upper"] = (i[:, None] <= i[None, :]).astype(np.float32)
    c["negU"] = -(i[:, None] >= i[None, :]).astype(np.float32)
    c["mS"] = np.where(i[:, None] > i[None, :], 0.0, NEG).astype(np.float32)
    c["mT"] = np.where(i[:, None] <= i[None, :], 0.0, NEG).astype(np.float32)
    lev = np.zeros((7, 128, 128), np.float32)
    for l in range(7):
        s = 1 << l
        lev[l] = ((i[:, None] // s) % 2 == 1) & ((i[None, :] // s) == (i[:, None] // s) - 1)
    c["lev"] = np.ascontiguousarray(lev.transpose(1, 0, 2)).reshape(128, 896)
    c["mG"] = ((i[:, None] <= i[None, :]) & (i[:, None] // 64 == i[None, :] // 64)).astype(np.float32)
    c["scanm"] = np.broadcast_to((np.arange(T) % 64 != 0).astype(np.float32), (128, T))
    c["tpos"] = np.broadcast_to(np.arange(T, dtype=np.float32), (128, T))
    cnt = np.zeros((128, 4, 16), np.float32)
    for g, w in enumerate((2, 4, 8, 16)):
        cnt[:, g, :] = np.float32(1.0) / np.minimum(np.arange(16) + 1, w).astype(np.float32)
    c["cnt"] = cnt.reshape(128, 64)
    hot = np.zeros((32, 3, 384), np.float32)
    pen = np.full((128, 3, 384), NEG, np.float32)
    for g, d in enumerate(DILS):
        b = t5_buckets(d)
        for dist in range(129):
            hot[b[dist], g, dist + 127] = 1.0
            pen[:, g, dist + 127] = 0.0
    c["hot"] = np.concatenate([hot.reshape(32, 1152), np.zeros((96, 1152), np.float32)])
    c["pen"] = pen.reshape(128, 1152)[0:4]
    blk = np.where(i[:, None] // 64 == i[None, :] // 64, 0.0, NEG).astype(np.float32)
    c["blk"] = blk
    return {k: np.ascontiguousarray(v) for k, v in c.items()}


CONST_SHAPES = {k: v.shape for k, v in shape_constants().items()}


class Tok:
    __slots__ = ("q", "sig", "val", "sem")

    def __init__(self, q):
        self.q, self.sig, self.val, self.sem = q, False, 0, None


def points(w):
    if w is None:
        return []
    if isinstance(w, Tok):
        return [w]
    return [t for x in w for t in points(x)]


class Lane:

    def __init__(self, sem):
        self.sem, self.n = sem, 0

    def next(self):
        self.n += 16
        return self.sem, self.n


class Noted:

    def activation(self, *a, **k):
        return lambda e: e.activation(*a, **k)

    def affine_select(self, *a, **k):
        return lambda e: e.affine_select(*a, **k)

    def copy(self, *a, **k):
        return lambda e: e.copy(*a, **k)

    def dma_start(self, *a, **k):
        return lambda e: e.dma_start(*a, **k)

    def matmul(self, *a, **k):
        return lambda e: e.matmul(*a, **k)

    def memset(self, *a, **k):
        return lambda e: e.memset(*a, **k)

    def mul(self, *a, **k):
        return lambda e: e.mul(*a, **k)

    def preload_act_table_set(self, *a, **k):
        return lambda e: e.preload_act_table_set(*a, **k)

    def reciprocal(self, *a, **k):
        return lambda e: e.reciprocal(*a, **k)

    def scalar_tensor_tensor(self, *a, **k):
        return lambda e: e.scalar_tensor_tensor(*a, **k)

    def tensor_copy(self, *a, **k):
        return lambda e: e.tensor_copy(*a, **k)

    def tensor_reduce(self, *a, **k):
        return lambda e: e.tensor_reduce(*a, **k)

    def tensor_scalar(self, *a, **k):
        return lambda e: e.tensor_scalar(*a, **k)

    def tensor_tensor(self, *a, **k):
        return lambda e: e.tensor_tensor(*a, **k)

    def tensor_tensor_scan(self, *a, **k):
        return lambda e: e.tensor_tensor_scan(*a, **k)

    def transpose(self, *a, **k):
        return lambda e: e.transpose(*a, **k)


NOTED = Noted()


class Queue:

    def __init__(self, name, sem):
        self.name, self.sem, self.ops, self.extra, self.last = name, sem, [], [], None

    def op(self, fn, *waits):
        t = Tok(self)
        flat = points(self.extra) + points(waits)
        self.extra = []
        call = fn(NOTED) if fn is not None else None
        self.ops.append((t, flat, call, None))
        self.last = t
        return t

    def dma(self, sem, val, fn, *waits):
        t = self.op(fn, *waits)
        t.sem, t.val = sem, val
        tt, w, f, _ = self.ops.pop()
        self.ops.append((tt, w, f, sem))
        return t

    def mark(self):
        for _, waits, _, _ in self.ops:
            for w in waits:
                w.sig = True

    def number(self):
        n = 0
        for t, _, _, dsem in self.ops:
            if dsem is None and t.sig:
                n += 1
                t.sem, t.val = self.sem, n

    def emit(self, eng):
        seen = {}
        for t, waits, fn, dsem in self.ops:
            need = {}
            for w in waits:
                k = id(w.sem)
                if k not in need or need[k][1] < w.val:
                    need[k] = (w.sem, w.val)
            for k, (sem, val) in need.items():
                if seen.get(k, 0) < val:
                    eng.wait_ge(sem, val)
                    seen[k] = val
            if fn is None:
                continue
            ins = fn(eng)
            if dsem is not None:
                ins.then_inc(dsem, 16)
            elif t.sig:
                ins.then_inc(t.sem, 1)


class Buf:

    def __init__(self, ap):
        self.ap, self.free = ap, []


class Rot:
    def __init__(self, aps):
        self.bufs, self.n = [a if isinstance(a, Buf) else Buf(a) for a in aps], 0

    def take(self):
        b = self.bufs[self.n % len(self.bufs)]
        self.n += 1
        return b


def weight_plan():
    plan = []

    def tiles(name, fts, kt, k0=0):
        for ft in fts:
            plan.append((name, ft, k0, kt))

    def merge(b, kt, beside=()):
        for ft in range(9):
            if ft < 8 and (b, ft) != (3, 0):
                plan.append(("w_gate", b * 8 + ft, 0, 8))
            if ft == 1:
                plan.extend(("w_in", x, 0, 8) for x in beside)
            if ft:
                plan.append((f"w_br{b}", ft - 1, 0, kt))

    tiles("w_in", range(34, 38), 8)
    tiles("w_gate", [24], 8)
    tiles("w_glu", [x for i in range(4) for x in (i, i + 4)], 4)
    merge(3, 4)
    tiles("w_in", range(0, 4), 8)
    merge(0, 4)
    tiles("w_in", [4, 5], 8)
    for g in range(3):
        tiles("w_in", [10 + 2 * g, 11 + 2 * g, 16 + 2 * g, 17 + 2 * g] + ([6 + 2 * g, 7 + 2 * g] if g < 2 else []), 8)
    merge(1, 2, (22, 26, 30))
    for h in range(1, 4):
        tiles("w_in", [22 + h, 26 + h, 30 + h], 8)
    merge(2, 4)
    tiles("w_out", range(8), 8)
    k0 = 0
    for n in FFN_CUT:
        tiles("w_up", [x for i in range(k0, k0 + n) for x in (i, i + 22)], 8)
        tiles("w_down", range(8), n, k0)
        k0 += n
    tiles("w_in2", [28], 8)
    for hp in range(2):
        for h in (2 * hp, 2 * hp + 1):
            tiles("w_in2", [h, 4 + h, 8 + h, 12 + h], 8)
    for hp in range(2):
        tiles("w_in2", [16 + hp, 18 + hp], 8)
        tiles("w_in2", [20 + 2 * hp, 21 + 2 * hp, 24 + 2 * hp, 25 + 2 * hp], 8)
    tiles("w_o", range(8), 8)
    k0 = 0
    for n in FFN_CUT:
        tiles("w_up2", [x for i in range(k0, k0 + n) for x in (i, i + 22)], 8)
        tiles("w_down2", range(8), n, k0)
        k0 += n
    return plan


def build(nc, A, out, scr, spill, bsc, dump=None):
    from contextlib import ExitStack
    ctx = ExitStack()
    with ctx:
        sem_n = [0]

        def new_sem():
            sem_n[0] += 1
            return ctx.enter_context(nc.semaphore(f"s{sem_n[0]}"))

        pe, act, dve, pool, sp = (Queue(n, new_sem()) for n in ("pe", "act", "dve", "pool", "sp"))

        top = [(nc.sbuf_base + 63) // 64 * 64]
        high = [0]
        names = [0]

        def sb(shape, dt=F32):
            n = 4
            for s in shape[1:]:
                n *= s
            names[0] += 1
            h = nc.alloc_sbuf_tensor_at(f"t{names[0]}", list(shape), dt, offset=top[0])
            top[0] += (n + 63) // 64 * 64
            high[0] = max(high[0], top[0])
            return h[tuple(slice(None) for _ in shape)]

        PS = ctx.enter_context(nc.psum_tensor("PS", [128, 8, 512], F32))
        banks = [PS[:, i, :] for i in range(8)]
        pairs = [PS[:, 2 * i:2 * i + 2, :].rearrange("p a b -> p (a b)") for i in range(4)]

        dumps = []

        def at_address(addr, shape, dt=F32):
            keep = top[0]
            top[0] = addr
            x = sb(shape, dt)
            top[0] = keep
            return x

        phase = [[]]
        open_dma = []

        def dma(q, o, i, *waits, lane=None):
            sem, val = lane.next() if lane else (new_sem(), 16)
            return q.dma(sem, val, lambda e: e.dma_start(o, i), phase[0], *waits)

        def lanes(n):
            return [Lane(new_sem()) for _ in range(n)]

        def barrier(hold=(pe, act, dve, pool)):
            toks = [q.last for q in (pe, act, dve, pool) if q.last is not None] + open_dma
            for q in hold:
                q.extra = q.extra + toks
            phase[0] = list(toks)
            del open_dma[:]
            return toks

        def probe(name, ap, *waits):
            if dump is not None and name in dump:
                t = dma(sp, dump[name], ap, *waits)
                dumps.append(t)
                open_dma.append(t)

        V = sb([128, NV])
        v_tok = dma(sp, V, A["vecs"])

        def vec(name, i=0, n=1):
            a = VCOLS[name][0]
            return V[:, a + i:a + i + n]

        C = {}
        c_tok = {}

        def const(name):
            C[name] = sb(list(CONST_SHAPES[name]))
            c_tok[name] = dma(sp, C[name], A["c_" + name])
            return C[name], c_tok[name]

        ident, id_tok = const("ident")
        mod = sb([128, 48])
        cond = sb([128, 8])
        comb = sb([128, 64])
        md2 = []
        alane = lanes(3)
        ones = sb([128, 128])
        epsc = sb([128, 1])
        o_tok = dve.op(lambda e: e.memset(ones, 1.0))
        e_tok = dve.op(lambda e: e.memset(epsc, EPS))

        plan = weight_plan()
        RAW, SPL, AHEAD = 3, 3, 2
        raws = [sb([128, 8, 128]) for _ in range(RAW)]
        whis = [sb([128, 8, 128], F32R) for _ in range(SPL)]
        wlos = [sb([128, 8, 128], F32R) for _ in range(SPL)]
        raw_sem = [new_sem() for _ in range(RAW)]
        raw_free = [[] for _ in range(RAW)]
        spl_free = [[] for _ in range(SPL)]
        w_dma, w_ready, w_at = {}, {}, [0, 0, 0]

        def w_load(i):
            name, ft, k0, kt = plan[i]
            s = i % RAW
            src = A[name][ft, :, k0:k0 + kt, :]
            w_dma[i] = sp.dma(raw_sem[s], 16 * (i // RAW + 1), lambda e: e.dma_start(raws[s][:, 0:kt, :], src), raw_free[s])

        def w_split(i):
            name, ft, k0, kt = plan[i]
            s, r = i % SPL, i % RAW
            if i == 0:
                for n in range(RAW):
                    w_load(n)
            a = act.op(lambda e: e.copy(whis[s][:, 0:kt, :], raws[r][:, 0:kt, :]), w_dma[i], spl_free[s])
            d = dve.op(lambda e: e.tensor_tensor(wlos[s][:, 0:kt, :], raws[r][:, 0:kt, :],
                                                 whis[s][:, 0:kt, :].bitcast(F32), ALU.subtract), a, w_dma[i], spl_free[s])
            raw_free[r] = [a, d]
            if i + RAW < len(plan):
                w_load(i + RAW)
            w_ready[i] = [a, d]

        def w_next(name, ft, k0=0):
            i = w_at[2]
            assert plan[i][:3] == (name, ft, k0), (plan[i], name, ft, k0)
            w_at[2] += 1
            while w_at[1] <= min(i + AHEAD, len(plan) - 1):
                w_split(w_at[1])
                w_at[1] += 1
            return i

        pbufs = [Buf(p) for p in pairs]
        mmps = Rot(pbufs[0:3])

        def product_steps(name, ft, xs, evac, k0=0, order=None):
            i = w_next(name, ft, k0)
            s, kt = i % SPL, plan[i][3]
            assert kt == len(xs)
            b = mmps.take()
            ps = b.ap
            t = None
            for at, k in enumerate(order or range(kt)):
                hi, lo, rdy = xs[k]
                steps = [(whis, hi), (whis, lo), (wlos, hi)]
                for n, (w, x) in enumerate(steps):
                    for h in range(2):
                        def f(e, w=w, x=x, h=h, k=k, n=n):
                            return e.matmul(ps[:, h * 512:(h + 1) * 512], w[s][:, k, :], x[:, h * 512:(h + 1) * 512],
                                            start=(at == 0 and n == 0), stop=(at == kt - 1 and n == 2))
                        t = pe.op(f, (b.free + w_ready[i]) if at == 0 and n == 0 else None, rdy if n == 0 else None)
                if at < kt - 1:
                    yield None
            spl_free[s] = [t]
            b.free = evac(ps, t)
            yield b.free

        def product(*args, **kw):
            for r in product_steps(*args, **kw):
                pass
            return r

        def split(dst, src, *waits):
            a = act.op(lambda e: e.copy(dst[0], src), *waits)
            d = dve.op(lambda e: e.tensor_tensor(dst[1], src, dst[0].bitcast(F32), ALU.subtract), a, *waits)
            return [a, d]

        def ones_sum(tiles, ps, free):
            t, n = None, len(tiles)
            out_t = []
            for k, (x, r) in enumerate(tiles):
                for h in range(2):
                    t = pe.op(lambda e, x=x, h=h, k=k: e.matmul(ps[:, h * 512:(h + 1) * 512], ones, x[:, h * 512:(h + 1) * 512],
                                                              start=(k == 0), stop=(k == n - 1)), free if k == 0 else None, r, o_tok)
                out_t.append(t)
            return out_t

        def inv_root(src, n, dst, *waits, tables=True):
            if tables:
                act.op(lambda e: e.preload_act_table_set("natural_log_exp_and_others"))
            a = act.op(lambda e: e.activation(dst, src, ACT.Ln, scale=1.0 / n, bias=epsc), e_tok, *waits)
            return a, act.op(lambda e: e.activation(dst, dst, ACT.Exp, scale=-0.5), a)

        def square_sum(acc, tmps, *free):
            state = dict(n=0, late=None, last=None, free=[list(free) for _ in tmps])

            def late():
                if state["late"] is not None:
                    i, a = state["late"]
                    state["last"] = dve.op(lambda e: e.tensor_tensor(acc, acc, tmps[i], ALU.add), a, state["last"])
                    state["free"][i] = [state["last"]]
                    state["late"] = None
                return state["last"]

            def add(x, *rdy):
                late()
                if state["n"] == 0:
                    state["last"] = act.op(lambda e: e.activation(acc, x, ACT.Square), rdy, free)
                else:
                    i = state["n"] % len(tmps)
                    state["late"] = (i, act.op(lambda e: e.activation(tmps[i], x, ACT.Square), rdy, state["free"][i]))
                state["n"] += 1
            return add, late

        def plain_sum(acc, *free):
            state = dict(last=None, first=None)

            def add(x, rdy, col=None):
                if col is not None:
                    if state["last"] is None:
                        state["last"] = dve.op(lambda e: e.tensor_scalar(acc, x, col, None, ALU.mult), rdy, free, v_tok)
                    else:
                        state["last"] = dve.op(lambda e: e.scalar_tensor_tensor(acc, x, col, acc, ALU.mult, ALU.add), rdy, state["last"])
                elif state["first"] is None:
                    state["first"] = (x, rdy)
                elif state["last"] is None:
                    x0, r0 = state["first"]
                    state["last"] = dve.op(lambda e: e.tensor_tensor(acc, x0, x, ALU.add), r0, rdy, free)
                else:
                    state["last"] = dve.op(lambda e: e.tensor_tensor(acc, acc, x, ALU.add), rdy, state["last"])
                return state["last"]
            return add

        def split_scaled(dst, src, col, *waits):
            a = act.op(lambda e: e.activation(dst[0], src, ACT.Identity, scale=col), *waits)
            d = dve.op(lambda e: e.scalar_tensor_tensor(dst[1], src, col, dst[0].bitcast(F32), ALU.mult, ALU.subtract), a, *waits)
            return [a, d]

        def mean_square_inv(tiles, n, tmp, dst, ps_buf, dst_free=None):
            ps = ps_buf.ap
            t = squares(tiles, tmp, ps, ps_buf.free)
            a, x = inv_root(ps, n, dst, t, dst_free)
            ps_buf.free = [a]
            return x

        def rms_split(X, rdy, gname, dst, tmp, rstd):
            pb = mmps.take()
            r = mean_square_inv([(X[:, k, :], rdy[k]) for k in range(8)], T, tmp, rstd, pb)
            while w_at[1] <= AHEAD:
                w_split(w_at[1])
                w_at[1] += 1
            res = []
            late = None
            for k in range(8):
                b = tmp.take()
                d = dve.op(lambda e, b=b, k=k: e.scalar_tensor_tensor(b.ap, X[:, k, :], vec(gname, k), rstd, ALU.mult, ALU.mult),
                           r, b.free, v_tok)
                late = split_late(late, b, (dst[0][:, k, :], dst[1][:, k, :]), d, res)
            split_late(late, None, None, None, res)
            return res

        def split_late(late, b, dst, ready, res):
            if b is not None:
                a = act.op(lambda e: e.copy(dst[0], b.ap), ready)
            if late is not None:
                b0, d0, a0, r0 = late
                x = dve.op(lambda e: e.tensor_tensor(d0[1], b0.ap, d0[0].bitcast(F32), ALU.subtract), a0, r0)
                b0.free = [a0, x]
                res.append([a0, x])
            return (b, dst, a, ready) if b is not None else None

        def squares(tiles, tmp, ps, free):
            for k, (x, r) in enumerate(tiles):
                b = tmp.take()
                a = act.op(lambda e: e.activation(b.ap, x, ACT.Square), r, b.free)
                b.free = [ones_part(b.ap, ps, k == 0, k == len(tiles) - 1, a, free)]
            return pe.last

        def centred(X, sums, mu, tmp, rstd, col=None, first=None):
            pb = mmps.take()
            t = ones_sum([sums], pb.ap, pb.free)[-1]
            m = dve.op(lambda e: e.tensor_scalar(mu, pb.ap, 1.0 / T, None, ALU.mult), t)
            pb.free = [m]
            if col is None:
                xc = [dve.op(lambda e, k=k: e.tensor_tensor(X[:, k, :], X[:, k, :], mu, ALU.subtract), m) for k in range(8)]
            else:
                xc = [dve.op(lambda e, k=k: e.scalar_tensor_tensor(X[:, k, :], X[:, k, :], vec(col, k), mu, ALU.mult, ALU.subtract), m)
                      for k in range(8)]
            pb = mmps.take()
            if first is None:
                r = mean_square_inv([(X[:, k, :], [xc[k]]) for k in range(8)], T, tmp, rstd, pb)
            else:
                ps = pb.ap
                sq = dve.op(lambda e: e.tensor_tensor(mu, first[0], first[0], ALU.mult), first[1], xc)
                squares([(X[:, k, :], [xc[k]]) for k in range(8)], tmp, ps, pb.free)
                w = dve.op(lambda e: e.tensor_tensor(rstd, ps, mu, ALU.mult), pe.last, sq)
                pb.free = [w]
                r = inv_root(rstd, T, rstd, w)[1]
                r = dve.op(lambda e: e.tensor_tensor(rstd, rstd, first[0], ALU.mult), r)
            return [lambda k=k: dve.op(lambda e: e.tensor_tensor(X[:, k, :], X[:, k, :], rstd, ALU.mult), r) for k in range(8)]

        def ones_part(x, ps, start, stop, *waits):
            for h in range(2):
                t = pe.op(lambda e, h=h: e.matmul(ps[:, h * 512:(h + 1) * 512], ones, x[:, h * 512:(h + 1) * 512], start=start, stop=stop),
                          waits, o_tok)
            return t

        def transposes(src, dst_evac, n, ready, ps_buf):
            t = None
            for j in range(n):
                t = pe.op(lambda e, j=j: e.transpose(ps_buf.ap[:, j * 128:(j + 1) * 128], src[:, j * 128:(j + 1) * 128], ident),
                          ready if j == 0 else None, ps_buf.free if j == 0 else None, id_tok)
            ps_buf.free = dst_evac(ps_buf.ap, t)
            return ps_buf.free

        base0 = top[0]
        XH = (sb([128, 8, T], F32R), sb([128, 8, T], F32R))
        base_x = top[0]

        def bias_rows():
            hot, h_t = const("hot")
            pen, p_t = const("pen")
            rb = sb([128, 12])
            rb_t = dma(sp, rb, A["rel_bias"])
            wr = []
            brow = sb([4, 3, 384])
            for g in range(3):
                b = mmps.take()
                t = pe.op(lambda e, b=b, g=g: e.matmul(b.ap[0:4, 0:384], rb[:, 4 * g:4 * g + 4], hot[:, 384 * g:384 * g + 384],
                                                       start=True, stop=True), h_t, rb_t, b.free)
                d = dve.op(lambda e, b=b, g=g: e.tensor_tensor(brow[:, g, :], b.ap[0:4, 0:384], pen[:, 384 * g:384 * g + 384], ALU.add), t, p_t)
                b.free = [d]
                wr.append(d)
            bs_t = dma(sp, bsc, brow, wr)
            return bs_t

        def s5_prepare():
            keep0 = top[0]
            top[0] = base_x + 16 * 4 * T
            u_at = top[0]
            U = sb([128, 4, T])
            sgl_at = top[0]
            BC = sb([128, 4, 16, 16])
            bct = dma(sp, BC.rearrange("p a b c -> p a (b c)"), A["s5bc"])
            cpos = sb([128, 128])
            cp_tok = dma(sp, cpos, A["c_tpos"][:, 0:128])
            W = [sb([128, 16]) for _ in range(14)]
            WI = sb([128, 16], I32)
            PR, PI = sb([128, 9, 16]), sb([128, 9, 16])
            Br, Bi = sb([128, 16, 16]), sb([128, 16, 16])
            s5_top = top[0]
            top[0] = u_at - 4 * (4 * 16 + 16 * 16)
            q1 = sb([128, 4, 16])
            q2 = sb([128, 16, 16])
            top[0] = keep0
            last = [v_tok]

            def d(fn):
                last[0] = dve.op(fn, last[0])
                return last[0]

            def ts(o, i, s1, s2, op0, op1=None):
                if s2 is None:
                    return d(lambda e: e.tensor_scalar(o, i, s1, None, op0))
                return d(lambda e: e.tensor_scalar(o, i, s1, s2, op0, op1))

            def tt(o, a, b, op):
                return d(lambda e: e.tensor_tensor(o, a, b, op))

            def stt(o, a, s, b, op0, op1):
                return d(lambda e: e.scalar_tensor_tensor(o, a, s, b, op0, op1))

            def exact_exp(o, x, k, r, q):
                ts(r, x, -87.5, 88.9, ALU.max, ALU.min)
                ts(k, r, 1.4426950408889634, MAGIC, ALU.mult, ALU.add)
                ts(k, k, MAGIC, None, ALU.subtract)
                stt(r, k, -0.693359375, r, ALU.mult, ALU.add)
                stt(r, k, 2.12194440054690583e-4, r, ALU.mult, ALU.add)
                ts(q, r, 1.0 / 5040, 1.0 / 720, ALU.mult, ALU.add)
                for cf in (1.0 / 120, 1.0 / 24, 1.0 / 6, 0.5, 1.0, 1.0):
                    tt(q, q, r, ALU.mult)
                    ts(q, q, cf, None, ALU.add)
                ts(k, k, 126.0, 8388608.0, ALU.add, ALU.mult)
                d(lambda e: e.tensor_copy(WI, k))
                stt(o, q, 2.0, WI.bitcast(F32), ALU.mult, ALU.mult)
                ts(k, x, -87.3, None, ALU.is_ge)
                tt(o, o, k, ALU.mult)

            ar, ai = vec("a_re", 0, 16), vec("a_im", 0, 16)
            dt_, mag, th, t1, t2, t3, co, si, cr, ci, tau, t4, nr, ni = W
            exact_exp(dt_, vec("ldt", 0, 16), t1, t2, t3)
            tt(t4, ar, dt_, ALU.mult)
            exact_exp(mag, t4, t1, t2, t3)
            tt(th, ai, dt_, ALU.mult)
            ts(t1, th, 1.0 / (2 * math.pi), MAGIC, ALU.mult, ALU.add)
            ts(t1, t1, MAGIC, None, ALU.subtract)
            c1 = 6.28125
            c2 = float(np.float32(np.round((2 * math.pi - c1) * 2 ** 18) / 2 ** 18))
            c3 = 2 * math.pi - c1 - c2
            stt(th, t1, -c1, th, ALU.mult, ALU.add)
            stt(th, t1, -c2, th, ALU.mult, ALU.add)
            stt(th, t1, -c3, th, ALU.mult, ALU.add)
            ts(tau, th, 1.0 / (2 * math.pi), None, ALU.mult)
            ts(t1, th, 0.25, None, ALU.mult)
            tt(t2, t1, t1, ALU.mult)
            ts(t3, t2, 1.0 / 362880, -1.0 / 5040, ALU.mult, ALU.add)
            for cf in (1.0 / 120, -1.0 / 6, 1.0):
                tt(t3, t3, t2, ALU.mult)
                ts(t3, t3, cf, None, ALU.add)
            tt(si, t3, t1, ALU.mult)
            ts(t3, t2, -1.0 / 3628800, 1.0 / 40320, ALU.mult, ALU.add)
            for cf in (-1.0 / 720, 1.0 / 24, -0.5, 1.0):
                tt(t3, t3, t2, ALU.mult)
                ts(t3, t3, cf, None, ALU.add)
            d(lambda e: e.tensor_copy(co, t3))
            for _ in range(2):
                tt(t1, si, si, ALU.mult)
                stt(si, si, 2.0, co, ALU.mult, ALU.mult)
                ts(co, t1, -2.0, 1.0, ALU.mult, ALU.add)
            tt(nr, mag, co, ALU.mult)
            ts(nr, nr, -1.0, None, ALU.add)
            tt(ni, mag, si, ALU.mult)
            tt(t1, ar, ar, ALU.mult)
            tt(t2, ai, ai, ALU.mult)
            tt(t1, t1, t2, ALU.add)
            d(lambda e: e.reciprocal(t1, t1))
            tt(cr, nr, ar, ALU.mult)
            tt(t2, ni, ai, ALU.mult)
            tt(cr, cr, t2, ALU.add)
            tt(cr, cr, t1, ALU.mult)
            tt(ci, ni, ar, ALU.mult)
            tt(t2, nr, ai, ALU.mult)
            tt(ci, ci, t2, ALU.subtract)
            tt(ci, ci, t1, ALU.mult)
            
            yield None
            d(lambda e: e.memset(PR[:, 0, :], 1.0))
            d(lambda e: e.memset(PI[:, 0, :], 0.0))
            tt(PR[:, 1, :], mag, co, ALU.mult)
            tt(PI[:, 1, :], mag, si, ALU.mult)
            for m in (1, 2, 4):
                a, o = slice(1, m + 1), slice(m + 1, 2 * m + 1)
                bro = lambda x: x[:, m:m + 1, :].to_broadcast([128, m, 16])
                tt(PR[:, o, :], PR[:, a, :], bro(PR), ALU.mult)
                tt(q1[:, 0:m, :], PI[:, a, :], bro(PI), ALU.mult)
                tt(PR[:, o, :], PR[:, o, :], q1[:, 0:m, :], ALU.subtract)
                tt(PI[:, o, :], PR[:, a, :], bro(PI), ALU.mult)
                tt(q1[:, 0:m, :], PI[:, a, :], bro(PR), ALU.mult)
                tt(PI[:, o, :], PI[:, o, :], q1[:, 0:m, :], ALU.add)
            for _ in range(3):
                tt(mag, mag, mag, ALU.mult)
            ts(tau, tau, 8.0, None, ALU.mult)
            ts(t1, tau, MAGIC, MAGIC, ALU.add, ALU.subtract)
            tt(tau, tau, t1, ALU.subtract)
            b3 = lambda x: x.unsqueeze(2).to_broadcast([128, 16, 16])
            last[0] = [last[0], bct]
            tt(Br, BC[:, 0, :, :], b3(cr), ALU.mult)
            tt(q2, BC[:, 1, :, :], b3(ci), ALU.mult)
            tt(Br, Br, q2, ALU.subtract)
            tt(Bi, BC[:, 1, :, :], b3(cr), ALU.mult)
            tt(q2, BC[:, 0, :, :], b3(ci), ALU.mult)
            tt(Bi, Bi, q2, ALU.add)
            r = U, sgl_at, BC, cpos, cp_tok, PR, PI, Br, Bi, mag, tau, tt, stt, last, s5_top
            yield r

        s5_steps = s5_prepare()
        next(s5_steps)
        X = sb([128, 8, T])
        tmp = Rot([sb([128, T]) for _ in range(3)])
        rstd = sb([128, T])
        rows_at = top[0]
        lane8 = lanes(8)
        x_tok = [[dma(sp, X[:, k, :], A["xT"][:, k, :], lane=lane8[k])] for k in range(8)]
        xn = rms_split(X, x_tok, "attn_g", XH, tmp, rstd)
        s5_pre = next(s5_steps)
        XN = [(XH[0][:, k, :], XH[1][:, k, :], xn[k]) for k in range(8)]
        top[0] = base_x

        cs_t = act.op(lambda e: e.activation(cond, vec("c", 0, 8), ACT.Silu), v_tok)
        m_addr = top[0]
        merged = sb([128, 8, T])
        m_tok = [None] * 8
        y_addr = top[0]
        Y = (sb([128, 4, T], F32R), sb([128, 4, T], F32R))
        base_y = top[0]
        first_merge = [True]

        def conditioning(j0):
            adr = [sb([128, T]) for _ in range(3)]
            ada = [sb([128, T]) for _ in range(2)]
            lds, use = {}, {}

            def load(i):
                j, k = j0 + i // 8, i % 8
                lds[i] = dma(sp, adr[i % 3], A["w_ada"][k, :, j * T:(j + 1) * T], use.get(i - 3), lane=alane[i % 3])

            load(0)
            load(1)
            d = None
            for i in range(16):
                yield
                if i + 2 < 16:
                    load(i + 2)
                j, k, a, x = j0 + i // 8, i % 8, ada[i // 8], adr[i % 3]
                if k == 0:
                    d = dve.op(lambda e: e.tensor_scalar(a, x, cond[:, 0:1], None, ALU.mult), lds[i], cs_t)
                else:
                    d = dve.op(lambda e: e.scalar_tensor_tensor(a, x, cond[:, k:k + 1], a, ALU.mult, ALU.add), lds[i], d)
                use[i] = [d]
                if k == 7:
                    yield
                    yield
                    pb = pbufs[3]
                    for f in range(8):
                        t = pe.op(lambda e: e.matmul(pb.ap[:, f:f + 1], a[:, f * 128:(f + 1) * 128], ones[:, 0:1], start=True, stop=True),
                                  d, pb.free, o_tok)
                    v = dve.op(lambda e: e.tensor_tensor(mod[:, 8 * j:8 * j + 8], pb.ap[:, 0:8], vec("b_ada", 8 * j, 8), ALU.add), t, v_tok)
                    if j in (1, 2, 4, 5):
                        v = dve.op(lambda e: e.tensor_scalar(mod[:, 8 * j:8 * j + 8], mod[:, 8 * j:8 * j + 8], 1.0, None, ALU.add), v)
                    pb.free = [v]
                    md2.append(v)

        def merge(b, kt, branch, beside=None, done=None, sg_at=None, first=None):
            mark = top[0]
            if sg_at is not None:
                top[0] = sg_at
            sg = Rot([sb([128, T]) for _ in range(2)])
            if sg_at is not None:
                top[0] = mark
            side = iter(())
            ys = None
            def gate_tile(ft):
                g = sg.take()
                gt = product("w_gate", b * 8 + ft, XN, lambda ps, t: [act.op(lambda e: e.activation(g.ap, ps, ACT.Sigmoid), t, g.free)])
                return g, gt

            now = first or gate_tile(0)
            for ft in range(8):
                g, gt = now
                if ft < 7:
                    now = gate_tile(ft + 1)
                if ft == 0:
                    ytok = branch()
                    ys = [(Y[0][:, k, :], Y[1][:, k, :], ytok[k]) for k in range(kt)]
                    if beside:
                        side = beside()

                def br(ps, t):
                    if first_merge[0]:
                        d = dve.op(lambda e: e.tensor_tensor(merged[:, ft, :], ps, g.ap, ALU.mult), t, gt)
                        g.free = [d]
                        m_tok[ft] = [d]
                        return [d]
                    d = dve.op(lambda e: e.tensor_tensor(g.ap, ps, g.ap, ALU.mult), t, gt)
                    d2 = dve.op(lambda e: e.tensor_tensor(merged[:, ft, :], merged[:, ft, :], g.ap, ALU.add), d, m_tok[ft])
                    g.free = [d2]
                    m_tok[ft] = [d2]
                    return [d]

                next(side, None)
                product(f"w_br{b}", ft, ys, br)
                next(side, None)
                next(side, None)
                if done:
                    done(ft, m_tok[ft])
            for _ in side:
                pass
            first_merge[0] = False
            if not done:
                barrier()
                top[0] = mark

        def s5():
            ut = []
            U, sgl_at, BC, cpos, cp_tok, PR, PI, Br, Bi, mag, tau, tt, stt, last, s5_top = s5_pre
            top[0] = s5_top

            def u_tile(i):
                ut.append(product("w_in", 34 + i, XN, lambda ps, t: [act.op(lambda e: e.copy(U[:, i, :], ps), t)]))

            nonlocal mmps
            keep_ps, mmps = mmps, Rot([pbufs[0], pbufs[1]])
            u_tile(0)
            u_tile(1)
            keep, top[0] = top[0], rows_at
            bs_t.append(bias_rows())
            top[0] = keep
            open_dma.extend(bs_t)
            keep = top[0]
            top[0] = m_addr
            CLr, CLi = sb([128, 16, 9, 16]), sb([128, 16, 9, 16])
            M = sb([128, 32, 128])
            big_at = top[0]
            tmp = sb([128, 8, 9, 16])
            Ks = sb([16, 32, 128])
            assert top[0] <= base_y
            mz = pool.op(lambda e: e.memset(M, 0.0), xn, bs_t)
            trp = Rot([pbufs[0], pbufs[1]])
            pA, pB = pbufs[2], pbufs[3]
            flat4 = lambda x: x.rearrange("p a b c -> p (a b c)")
            last[0] = [last[0], bs_t, xn]

            kt = []
            for hf in range(2):
                ii = slice(8 * hf, 8 * hf + 8)
                full = [128, 8, 9, 16]
                pr = PR[:, :, ii].rearrange("p k i -> p i k").unsqueeze(3).to_broadcast(full)
                pi = PI[:, :, ii].rearrange("p k i -> p i k").unsqueeze(3).to_broadcast(full)
                c_r = BC[:, 2, ii, :].unsqueeze(2).to_broadcast(full)
                c_i = BC[:, 3, ii, :].unsqueeze(2).to_broadcast(full)
                x, y = CLr[:, ii, :, :], CLi[:, ii, :, :]
                tt(x, pr, c_r, ALU.mult)
                tt(tmp, pi, c_i, ALU.mult)
                tt(flat4(x), flat4(x), flat4(tmp), ALU.subtract)
                tt(y, pr, c_i, ALU.mult)
                tt(tmp, pi, c_r, ALU.mult)
                stt(flat4(y), flat4(y), -1.0, flat4(tmp), ALU.mult, ALU.subtract)
                t = None
                for n in range(8):
                    i = 8 * hf + n
                    for gl in range(2):
                        rows = slice(64 * gl, 64 * gl + 64)
                        pb = (pA, pB)[gl]
                        for m, (w, x) in enumerate(((Br, CLr), (Bi, CLi))):
                            t = pe.op(lambda e: e.matmul(pb.ap[0:16, 128 * n:128 * n + 128], w[rows, i, :],
                                                         x[rows, i, 0:8, :].rearrange("p a b -> p (a b)"), start=(m == 0), stop=(m == 1)),
                                      last[0], pb.free)
                for gl in range(2):
                    pb = (pA, pB)[gl]
                    g = slice(16 * hf + gl, 16 * hf + 16, 2)
                    pb.free = [act.op(lambda e: e.copy(Ks[:, g, :], pb.ap[0:16, :].rearrange("p (a b) -> p a b", a=8)), t)]
                    kt += pb.free
            mt = [dma(sp, M[16 * q:16 * q + 16, :, 16 * q:128], Ks[:, :, 0:128 - 16 * q], kt, mz) for q in range(8)]
            open_dma.extend(mt)
            u_tile(2)
            Ug = sb([128, 16, 128])
            assert top[0] <= base_y
            top[0] = big_at
            WT = [sb([128, 8, 128]) for _ in range(2)]
            work_at = top[0]
            work = [sb([128, 1024]) for _ in range(3)]
            assert top[0] <= base_y
            top[0] = keep
            work += [sb([128, 1024]) for _ in range(2)]
            H = [sb([128, 8, 128]) for _ in range(2)]
            yt = []
            hz = [dve.op(lambda e: e.memset(H[n][:, :, 0:1], 0.0)) for n in range(2)]
            v8 = lambda x: x.rearrange("p (a b) -> p a b", a=8)
            last[0] = [last[0], mt]
            for hf in range(2):
                if hf:
                    barrier((act, dve, pool))
                ii = slice(8 * hf, 8 * hf + 8)
                full = [128, 8, 8, 16]
                wr, wi, wt, a0, a1 = work
                v4 = lambda x: x.rearrange("p (a b c) -> p a b c", a=8, b=8)
                pr = PR[:, 7::-1, ii].rearrange("p k i -> p i k").unsqueeze(3).to_broadcast(full)
                pi = PI[:, 7::-1, ii].rearrange("p k i -> p i k").unsqueeze(3).to_broadcast(full)
                b_r = Br[:, ii, :].unsqueeze(2).to_broadcast(full)
                b_i = Bi[:, ii, :].unsqueeze(2).to_broadcast(full)
                w0 = last[0]
                tt(v4(wr), pr, b_r, ALU.mult)
                tt(v4(wt), pi, b_i, ALU.mult)
                xr = tt(wr, wr, wt, ALU.subtract)
                tt(v4(wi), pr, b_i, ALU.mult)
                tt(v4(wt), pi, b_r, ALU.mult)
                xi = tt(wi, wi, wt, ALU.add)
                ug = []
                for fl in range(2):
                    f = 2 * hf + fl
                    dst = (a0, a1)[fl]
                    pb = trp.take()
                    for q in range(8):
                        t = pe.op(lambda e: e.transpose(pb.ap[:, 128 * q:128 * q + 128], U[:, f, q::8], ident), ut[f], pb.free, id_tok)
                    c = act.op(lambda e: e.copy(dst.rearrange("p (g s c) -> p g s c", g=8, s=8),
                                                pb.ap.rearrange("p (s g c) -> p g s c", g=8, s=8)), t)
                    pb.free = [c]
                    pb = trp.take()
                    for q in range(8):
                        t = pe.op(lambda e: e.transpose(pb.ap[:, 128 * q:128 * q + 128], dst[:, 128 * q:128 * q + 128], ident), c, pb.free)
                    ug.append(act.op(lambda e: e.copy(Ug[:, 8 * fl:8 * fl + 8, :], v8(pb.ap)), t))
                    pb.free = [ug[-1]]
                wt_t = []
                for n, (w, x) in enumerate(((wr, xr), (wi, xi))):
                    pb = trp.take()
                    for q in range(8):
                        t = pe.op(lambda e: e.transpose(pb.ap[:, 128 * q:128 * q + 128], w[:, 128 * q:128 * q + 128], ident), x, pb.free)
                    wt_t.append(act.op(lambda e: e.copy(WT[n], v8(pb.ap)), t))
                    pb.free = [wt_t[-1]]
                bu = []
                for n, pb in enumerate((pA, pB)):
                    for q in range(8):
                        for gl in range(2):
                            t = pe.op(lambda e: e.matmul(pb.ap[64 * gl:64 * gl + 64, 128 * q:128 * q + 128], WT[n][:, q, 64 * gl:64 * gl + 64],
                                                         Ug[:, 2 * q + gl, :], start=True, stop=True), wt_t[n], ug, pb.free)
                    bu.append(t)
                if hf == 0:
                    u_tile(3)
                else:
                    g = Buf(at_address(sgl_at, [128, T]))
                    early_gate.append((g, product("w_gate", 24, XN, lambda ps, t: [act.op(lambda e: e.activation(g.ap, ps, ACT.Sigmoid), t, last[0])])))
                S, Cc, P, Q, R = work
                busy = [bu[-1], wt_t, ug]
                q = dve.op(lambda e: e.tensor_tensor(v8(P), tau[:, ii].unsqueeze(2).to_broadcast([128, 8, 128]),
                                                     cpos.unsqueeze(1).to_broadcast([128, 8, 128]), ALU.mult), wt_t, ug, cp_tok, last[0])
                k1 = dve.op(lambda e: e.tensor_scalar(Q, P, MAGIC, MAGIC, ALU.add, ALU.subtract), q)
                k2 = dve.op(lambda e: e.tensor_tensor(Q, P, Q, ALU.subtract), k1)
                s_t = act.op(lambda e: e.activation(S, Q, ACT.Sin, scale=2 * math.pi), k2)
                k3 = dve.op(lambda e: e.tensor_scalar(P, P, 0.25, None, ALU.add), k2)
                k4 = dve.op(lambda e: e.tensor_scalar(R, P, MAGIC, MAGIC, ALU.add, ALU.subtract), k3)
                k5 = dve.op(lambda e: e.tensor_tensor(R, P, R, ALU.subtract), k4)
                c_t = act.op(lambda e: e.activation(Cc, R, ACT.Sin, scale=2 * math.pi), k5)
                br, bi = pA.ap, pB.ap
                a1_ = dve.op(lambda e: e.tensor_tensor(P, Cc, br, ALU.mult), bu, c_t, s_t)
                a2_ = dve.op(lambda e: e.tensor_tensor(R, S, bi, ALU.mult), c_t)
                a3_ = dve.op(lambda e: e.tensor_tensor(P, P, R, ALU.add), a1_, a2_)
                a4_ = dve.op(lambda e: e.tensor_tensor(Q, Cc, bi, ALU.mult), s_t)
                a5_ = dve.op(lambda e: e.tensor_tensor(R, S, br, ALU.mult), a3_)
                a6_ = dve.op(lambda e: e.tensor_tensor(Q, Q, R, ALU.subtract), a4_, a5_)
                pA.free = pB.free = [a5_]
                gs = []
                for n in range(8):
                    rb = mag[:, 8 * hf + n:8 * hf + n + 1].to_broadcast([128, 128])
                    for x, w in ((P, a3_), (Q, a6_)):
                        gs.append(dve.op(lambda e: e.tensor_tensor_scan(v8(x)[:, n, :], rb, v8(x)[:, n, :], 0.0, ALU.mult, ALU.add), w))
                b1 = dve.op(lambda e: e.tensor_tensor(R, S, Q, ALU.mult), gs)
                b2 = dve.op(lambda e: e.tensor_tensor(S, S, P, ALU.mult), b1)
                b3_ = dve.op(lambda e: e.tensor_tensor(P, Cc, P, ALU.mult), b2)
                b4 = dve.op(lambda e: e.tensor_tensor(Q, Cc, Q, ALU.mult), b1)
                b5 = dve.op(lambda e: e.tensor_tensor(H[0][:, :, 1:128], v8(P)[:, :, 0:127], v8(R)[:, :, 0:127], ALU.subtract), b3_)
                b6 = dve.op(lambda e: e.tensor_tensor(H[1][:, :, 1:128], v8(Q)[:, :, 0:127], v8(S)[:, :, 0:127], ALU.add), b4, b2)
                for fl in range(2):
                    f = 2 * hf + fl
                    dst = work[fl]
                    pb = (pA, pB)[fl]
                    for j in range(4):
                        for gl in range(2):
                            rows = slice(64 * gl, 64 * gl + 64)
                            n = 4 * fl + j
                            i = 8 * hf + n
                            o = pb.ap[:, 512 * gl + 128 * j:512 * gl + 128 * j + 128]
                            pe.op(lambda e: e.matmul(o, Ug[:, 2 * n + gl, :], M[:, 2 * i + gl, :], start=True, stop=False, skip_group_check=True),
                                  ug, mt, pb.free)
                            for m, (w, x) in enumerate(((H[0], CLr), (H[1], CLi))):
                                t = pe.op(lambda e: e.matmul(o, w[rows, n, :], x[rows, i, 1:9, :].rearrange("p a b -> p (a b)"),
                                                             start=False, stop=(m == 1), skip_group_check=True), b5, b6, hz)
                    cp = [act.op(lambda e: e.copy(dst.rearrange("p (t j g c) -> p g t j c", t=8, j=4, g=2)[:, gl, :, :, :],
                                                  pb.ap.rearrange("p (g j t c) -> p g t j c", g=2, j=4, t=8)[:, gl, :, :, :]), t, b6)
                          for gl in range(2)]
                    pb.free = cp
                    pt = trp.take()
                    for q in range(8):
                        t = pe.op(lambda e: e.transpose(pt.ap[:, 128 * q:128 * q + 128], dst[:, 128 * q:128 * q + 128], ident), cp, pt.free)
                    uv = U[:, f, :].rearrange("p (c t) -> p t c", t=8)
                    y1 = dve.op(lambda e: e.scalar_tensor_tensor(uv, uv, vec("s5_d", f), v8(pt.ap), ALU.mult, ALU.add), t)
                    pt.free = [y1]
                    yt.append(y1)
            barrier()
            mmps = keep_ps
            top[0] = sgl_at + 4 * T
            sgl = Rot([sb([128, T]) for _ in range(2)])
            gx = []
            for f in range(4):
                y2 = act.op(lambda e, f=f: e.activation(U[:, f, :], U[:, f, :], ACT.Gelu_apprx_tanh), yt[f])
                r = split((Y[0][:, f, :], Y[1][:, f, :]), U[:, f, :], y2)
                gx.append((Y[0][:, f, :], Y[1][:, f, :], r))
            res = []
            outs = []
            for f in range(4):
                g = sgl.take()

                hold = {}

                def lin(ps, t):
                    hold["d"] = dve.op(lambda e, f=f: e.tensor_copy(U[:, f, :], ps), t)
                    return [hold["d"]]

                product("w_glu", f, gx, lin)

                def sig(ps, t):
                    a = act.op(lambda e: e.activation(g.ap, ps, ACT.Sigmoid), t, g.free)
                    dd = dve.op(lambda e, f=f: e.tensor_tensor(U[:, f, :], U[:, f, :], g.ap, ALU.mult), a, hold["d"])
                    g.free = [dd]
                    outs.append(dd)
                    return [a]

                lastmm = product("w_glu", f + 4, gx, sig)
            probe("s5", U, outs)
            for f in range(4):
                res.append(split((Y[0][:, f, :], Y[1][:, f, :]), U[:, f, :], outs[f], lastmm, pe.last))
            return res

        mark = top[0]
        bs_t, early_gate = [], []
        yt = s5()
        barrier((act, dve, pool))
        top[0] = mark
        merge(3, 4, lambda: yt, lambda: conditioning(0), sg_at=base_y + 5 * 4 * T, first=early_gate[0])

        def pool_branch():
            PADW = 16
            cnt, cn_t = const("cnt")
            pw = sb([128, 4, 128])
            pw_t = dma(sp, pw, A["pool_w"])
            res = []
            sets = [[sb([128, PADW + T]) for _ in range(3)] for _ in range(2)]
            z = [[dve.op(lambda e: e.memset(b[:, 0:PADW], 0.0)) for b in bufs] for bufs in sets]
            free = [[], []]

            def window(g):
                w = (2, 4, 8, 16)[g]
                u, s, s2 = sets[g % 2]
                zz, fr = z[g % 2], free[g % 2]
                ut = product("w_in", g, XN, lambda ps, t: [act.op(lambda e: e.copy(u[:, PADW:], ps), t, fr)])
                src, dst, lt, step = u, s, ut, 1
                while step < w:
                    lt = [dve.op(lambda e: e.tensor_tensor(dst[:, PADW:], src[:, PADW:], src[:, PADW - step:PADW + T - step], ALU.add), lt, zz, fr)]
                    src, dst = dst, (s2 if dst is s else s)
                    step *= 2
                m1 = dve.op(lambda e: e.tensor_tensor(dst[:, PADW:PADW + 16], src[:, PADW:PADW + 16], cnt[:, 16 * g:16 * g + 16], ALU.mult), lt, cn_t)
                m2 = dve.op(lambda e: e.tensor_scalar(dst[:, PADW + 16:], src[:, PADW + 16:], 1.0 / w, None, ALU.mult), lt)
                m3 = dve.op(lambda e: e.tensor_tensor(dst[:, PADW:], dst[:, PADW:], u[:, PADW:], ALU.subtract), m1, m2)
                return src, dst, m3

            def mixed(g, src, dst, m3):
                b = mmps.take()
                for h in range(2):
                    t = pe.op(lambda e: e.matmul(b.ap[:, h * 512:(h + 1) * 512], pw[:, g, :], dst[:, PADW + h * 512:PADW + (h + 1) * 512],
                                                 start=True, stop=True), m3, b.free, pw_t)
                y = act.op(lambda e: e.activation(src[:, PADW:], b.ap, ACT.Identity, scale=vec("pool_s", g)), t, m3)
                b.free = [y]
                r = split((Y[0][:, g, :], Y[1][:, g, :]), src[:, PADW:], y)
                free[g % 2] = r
                res.append(r)

            held = None
            for g in range(4):
                now = (g,) + window(g)
                if held:
                    mixed(*held)
                held = now
            def rest():
                mixed(*held)
                return res
            return rest

        barrier((act, dve, pool))
        pool_rest = pool_branch()
        pool_top = top[0]

        def pooled():
            r = pool_rest()
            barrier((act, dve, pool))
            top[0] = mark
            return r

        merge(0, 4, pooled, lambda: conditioning(2), sg_at=pool_top)
        top[0] = mark

        def dil_branch():
            blkm, bk_t = const("blk")
            bias = sb([128, 4, 256])
            Qs, K2 = [sb([128, 2, T]) for _ in range(2)], sb([128, 2, T])
            Vf = sb([128, 2, T])
            Vt = sb([128, 8, 256])
            sbuf_s = Rot([sb([128, 4, 256]) for _ in range(3)])
            pT = Rot([sb([128, 4, 2, 128]) for _ in range(2)])
            stat = Rot([sb([128, 8]) for _ in range(3)])
            ot = Rot([sb([128, 264]) for _ in range(4)])
            last_pe = []
            stores = []
            blane, olane = lanes(4), [lanes(2) for _ in range(4)]
            nonlocal mmps
            keep_ps = mmps
            mmps_dense, mmps_side = Rot(pbufs[0:3]), Rot([pbufs[0]])
            mmps = mmps_dense
            sc_ps, tr_ps, ou_ps = Rot([pbufs[3]]), Rot([pbufs[1]]), Rot([pbufs[2]])
            q_read = [[], []]

            def queries(g, free):
                toks = []
                for n, ft in enumerate((4 + 2 * g, 5 + 2 * g)):
                    def ev(ps, t):
                        o = Qs[g % 2][:, n, :].rearrange("p (r l) -> p l r", r=DILS[g])
                        return [act.op(lambda e: e.copy(o, ps.rearrange("p (l r) -> p l r", r=DILS[g])), t, free)]
                    for r in product_steps("w_in", ft, XN, ev):
                        if r:
                            toks.extend(r)
                        yield None
                yield toks
            for g in range(3):
                dil = DILS[g]
                L = T // dil
                bl = []
                for n, h in enumerate(HN_):
                    src = bass.AP(tensor=bsc.tensor, offset=bsc.offset + (h * 3 + g) * 384, ap=[[1, 128], [1, 256]])
                    bl.append(dma(sp, bias[:, n, :], src, bs_t, last_pe, lane=blane[n]))
                Q2 = Qs[g % 2]
                if g == 0:
                    q_t = [x for x in queries(0, []) if x][-1]
                qk_t = list(q_t)
                for n, ft in enumerate((10 + 2 * g, 11 + 2 * g)):
                    def ev(ps, t, n=n):
                        o = K2[:, n, :].rearrange("p (r l) -> p l r", r=dil)
                        i = ps.rearrange("p (l r) -> p l r", r=dil)
                        return [act.op(lambda e: e.copy(o, i), t, last_pe)]
                    qk_t += product("w_in", ft, XN, ev)
                vt_t = []
                for n, ft in enumerate((16 + 2 * g, 17 + 2 * g)):
                    def ev(ps, t, n=n):
                        o = Vf[:, n, :].rearrange("p (r l) -> p l r", r=dil)
                        i = ps.rearrange("p (l r) -> p l r", r=dil)
                        return [act.op(lambda e: e.copy(o, i), t, last_pe)]
                    vv = product("w_in", ft, XN, ev)
                    pb = mmps.take()

                    def ev2(ps, t, n=n):
                        return [dve.op(lambda e: e.tensor_copy(Vt[:, :, 128 * n:128 * n + 128],
                                                               ps.rearrange("p (b f) -> p b f", b=8)), t, last_pe)]
                    vt_t += transposes(Vf[:, n, :], ev2, 8, vv, pb)
                def block_scores(u):
                    blk = u["blk"]
                    full = (g == 0 and blk > 0) or (g == 1 and blk % 2 == 1)
                    W = 256 if full else 128
                    pb = sc_ps.take()
                    s4 = pb.ap.rearrange("p (h c) -> p h c", h=4)
                    k0 = (blk - 1) * 128 if full else blk * 128
                    for n, h in enumerate(HN_):
                        rows = slice(64 * (h % 2), 64 * (h % 2) + 64)
                        t = pe.op(lambda e: e.matmul(s4[:, n, 256 - W:256], Q2[rows, h // 2, blk * 128:blk * 128 + 128],
                                                     K2[rows, h // 2, k0:k0 + W], start=True, stop=True), pb.free, qk_t)
                    S = sbuf_s.take()
                    cs = slice(256 - W, 256)
                    bv = bias[:, :, ::-1]
                    d = dve.op(lambda e: e.scalar_tensor_tensor(S.ap[:, :, cs], s4[:, :, cs], 0.125, bv[:, :, cs], ALU.mult, ALU.add),
                               t, S.free, bl)
                    pb.free = [d]
                    if g == 2:
                        d = dve.op(lambda e: e.tensor_tensor(S.ap[:, :, cs], S.ap[:, :, cs],
                                                             blkm.unsqueeze(1).to_broadcast([128, 4, 128]), ALU.add), d, bk_t)
                    st = stat.take()
                    O = ot.take()
                    d2 = dve.op(lambda e: e.tensor_reduce(O.ap[:, 256:260], S.ap[:, :, cs], AXX, ALU.max), d, O.free)
                    d3 = dve.op(lambda e: e.tensor_scalar(st.ap[:, 0:4], O.ap[:, 256:260], -1.0, None, ALU.mult), d2, st.free)
                    ex = []
                    for h in range(4):
                        ex.append(act.op(lambda e: e.activation(S.ap[:, h, cs], S.ap[:, h, cs], ACT.Exp, bias=st.ap[:, h:h + 1],
                                                                accum_out=O.ap[:, 260 + h:261 + h]), d3, O.free))
                    st.free = [ex[-1]]
                    u.update(W=W, k0=k0, S=S, O=O, ex=ex, d2=d2)

                def block_values(u):
                    blk, W, k0, S, O, ex, d2 = (u[n] for n in ("blk", "W", "k0", "S", "O", "ex", "d2"))
                    tb = tr_ps.take()
                    nk = W // 128
                    tv = tb.ap.rearrange("p (h k q) -> p h k q", h=4, k=2)
                    for h in range(4):
                        for k in range(nk):
                            c0 = 256 - W + 128 * k
                            t = pe.op(lambda e: e.transpose(tv[:, h, k, :], S.ap[:, h, c0:c0 + 128], ident), ex[h], tb.free)
                    S.free = [t]
                    p = pT.take()
                    pc = act.op(lambda e: e.copy(p.ap[:, :, 0:nk, :], tv[:, :, 0:nk, :]), t, p.free)
                    tb.free = [pc]
                    u.update(p=p, pc=pc)

                def block_out(u):
                    blk, W, k0, O, ex, d2, p, pc = (u[n] for n in ("blk", "W", "k0", "O", "ex", "d2", "p", "pc"))
                    nk = W // 128
                    ob = ou_ps.take()
                    for n, h in enumerate(HN_):
                        for k in range(nk):
                            t = pe.op(lambda e: e.matmul(ob.ap[:, 64 * h:64 * h + 64], p.ap[:, n, k, :],
                                                         Vt[:, k0 // 128 + k, 64 * h:64 * h + 64],
                                                         start=(k == 0), stop=(k == nk - 1)), pc, vt_t, ob.free)
                    p.free = [t]
                    oc = dve.op(lambda e: e.tensor_copy(O.ap[:, 0:256], ob.ap[:, 0:256]), t, O.free)
                    ob.free = [oc]
                    v = scr[g].rearrange("(l r) c -> r l c", r=dil)
                    if g == 2:
                        dd = [dma(sp, v[2 * blk + x], O.ap[64 * x:64 * x + 64, :], oc, ex, d2, lane=olane[blk % 4][x]) for x in range(2)]
                    else:
                        nb = 8 // dil
                        dst = v[blk // nb, (blk % nb) * 128:(blk % nb) * 128 + 128, :]
                        dd = [dma(sp, dst, O.ap, oc, ex, d2, lane=olane[blk % 4][0])]
                    O.free = dd
                    stores.extend(dd)
                    return t

                units = [dict(blk=b) for b in range(8)]
                side = queries(g + 1, q_read[(g + 1) % 2]) if g < 2 else iter(())
                mmps = mmps_side
                for i in range(11):
                    if i > 1:
                        q_t = next(side, None) or next(side, None) or q_t
                    if i < 8:
                        block_scores(units[i])
                    if 0 <= i - 2 < 8:
                        block_values(units[i - 2])
                    if 0 <= i - 3 < 8:
                        t = block_out(units[i - 3])
                for x in side:
                    q_t = x or q_t
                mmps = mmps_dense
                last_pe = [t]
                q_read[g % 2] = [t]
            mmps = keep_ps
            return stores

        def dil_load(stores):
            R = sb([128, 3, 8, 264])
            return R, [dma(sp, R[:, g, :, :], scr[g].rearrange("(a p) c -> p a c", p=128), stores) for g in range(3)]

        def dil_combine(back):
            R, rt = back
            M = sb([128, 8, 4])
            E = sb([128, 3, 8, 4])
            D = sb([128, 8, 4])
            D2 = sb([128, 8, 4])
            m = [R[:, g, :, 256:260] for g in range(3)]
            dn = [R[:, g, :, 260:264] for g in range(3)]
            a = dve.op(lambda e: e.tensor_tensor(M, m[0], m[1], ALU.max), rt)
            a = dve.op(lambda e: e.tensor_tensor(M, M, m[2], ALU.max), a)
            x = []
            for g in range(3):
                s = dve.op(lambda e, g=g: e.tensor_tensor(E[:, g, :, :], m[g], M, ALU.subtract), a)
                x.append(act.op(lambda e, g=g: e.activation(E[:, g, :, :], E[:, g, :, :], ACT.Exp), s))
            d = dve.op(lambda e: e.tensor_tensor(D, E[:, 0, :, :], dn[0], ALU.mult), x)
            for g in (1, 2):
                d1 = dve.op(lambda e, g=g: e.tensor_tensor(D2, E[:, g, :, :], dn[g], ALU.mult), d)
                d = dve.op(lambda e: e.tensor_tensor(D, D, D2, ALU.add), d1)
            d = dve.op(lambda e: e.reciprocal(D, D), d)
            o = []
            for g in range(3):
                f = dve.op(lambda e, g=g: e.tensor_tensor(E[:, g, :, :], E[:, g, :, :], D, ALU.mult), d)
                for h in range(4):
                    v = R[:, g, :, 64 * h:64 * h + 64]
                    o.append(dve.op(lambda e, g=g, v=v, h=h: e.tensor_tensor(
                        v, v, E[:, g, :, HN_[h]:HN_[h] + 1].to_broadcast([128, 8, 64]), ALU.mult), f))
            y = R[:, 0, :, 0:256]
            s1 = dve.op(lambda e: e.tensor_tensor(y, y, R[:, 1, :, 0:256], ALU.add), o)
            s2 = dve.op(lambda e: e.tensor_tensor(y, y, R[:, 2, :, 0:256], ALU.add), s1)
            probe("dil", R[:, 0, :, 0:256], s2)
            yc = sb([128, T])

            def by_feature():
                res = []
                yc_free = []
                for f in range(2):
                    pb = mmps.take()
                    for a_ in range(8):
                        t = pe.op(lambda e, a_=a_, f=f, pb=pb: e.transpose(pb.ap[:, a_ * 128:(a_ + 1) * 128],
                                                                           R[:, 0, a_, 128 * f:128 * f + 128], ident), s2, pb.free)
                    c = dve.op(lambda e, pb=pb: e.tensor_copy(yc, pb.ap), t, yc_free)
                    pb.free = [c]
                    r = split((Y[0][:, f, :], Y[1][:, f, :]), yc, c)
                    yc_free = r
                    res.append(r)
                return res

            return by_feature

        barrier()
        top[0] = y_addr
        st = dil_branch()
        barrier((act, dve, pool))
        top[0] = mark

        sb_first = [at_address(y_addr + n * 4 * T, [128, T]) for n in (3, 7, 2)]
        sb_tok = []

        def combined():
            rest = dil_combine(dil_load(st))
            for n, ft in enumerate((22, 26, 30)):
                sb_tok.append(product("w_in", ft, XN, lambda ps, t: [act.op(lambda e: e.mul(sb_first[n], ps, 128.0 ** -0.5 if n == 0 else 1.0), t)]))
            r = rest()
            barrier((act, dve, pool))
            top[0] = mark + 2 * 4 * T
            return r

        top[0] = mark + 2 * 4 * T
        merge(1, 2, combined, lambda: conditioning(4), sg_at=mark)
        top[0] = mark

        def sb_branch():
            negU, nu_t = const("negU")
            negO = sb([128, 128])
            no_t = dve.op(lambda e: e.memset(negO, -1.0))
            rU, rO = sb([128, 128], F32R), sb([128, 128], F32R)
            ru_t = [act.op(lambda e: e.copy(rU, negU), nu_t), act.op(lambda e: e.copy(rO, negO), no_t)]
            vf = sb([128, T])
            qk = [sb_first[0:2], [sb([128, T]) for _ in range(2)]]
            Vt = sb([128, 8, 128])
            places = [(top[0] + 4096 * n, top[0] + 4096 * n + 2048) for n in range(5)]
            wk = Rot([(at_address(x, [128, 512]), at_address(y, [128, 512]), at_address(x, [128, 512], F32R), at_address(y, [128, 512], F32R))
                      for x, y in places])
            top[0] += 5 * 4096
            acc = sb([128, 512])
            zp = Rot(banks[2:5])
            col = Buf(banks[5])
            op = Rot(banks[6:8])
            prp = Rot([pairs[0]])
            res = []
            prev = []
            acc_t = [None]
            nonlocal mmps
            keep_ps = mmps
            mmps = prp

            def scores(u):
                kb, cs, qs, ds = u["kb"], u["cs"], u["qs"], u["ds"]
                z = u["z"] = zp.take()
                w = u["w"] = wk.take()
                t1, t2 = w.ap[0:2]
                qT, kT = qk[u["h"] % 2]
                zt = pe.op(lambda e: e.matmul(z.ap[:, cs], kT[:, kb * 128:kb * 128 + 128], qT[:, qs], start=True, stop=True),
                           u["rdy"], z.free)
                x = act.op(lambda e: e.activation(t1[:, cs], z.ap[:, cs], ACT.Abs), zt, w.free)
                x = act.op(lambda e: e.activation(t1[:, cs], t1[:, cs], ACT.Exp, scale=-1.0), x)
                x = act.op(lambda e: e.activation(t1[:, cs], t1[:, cs], ACT.Ln, bias=1.0), x)
                u["x"] = x
                s = dve.op(lambda e: e.scalar_tensor_tensor(t2[:, cs], z.ap[:, cs], 0.0, t1[:, cs], ALU.max, ALU.add), x, w.free)
                if ds is not None:
                    s = pool.op(lambda e: e.affine_select(out=t2[:, ds], in_=t2[:, ds], pattern=[[1, 128]], compare_op=ALU.is_gt,
                                                          fill=0.0, base=0, channel_multiplier=-1), s)
                u["s"] = s

            def parts(u):
                cs, s = u["cs"], u["s"]
                _, t2, hi, lo = u["w"].ap
                h = act.op(lambda e: e.copy(hi[:, cs], t2[:, cs]), s)
                u["p"] = [h, dve.op(lambda e: e.tensor_tensor(lo[:, cs], t2[:, cs], hi[:, cs].bitcast(F32), ALU.subtract), h, s)]

            def weights(u):
                cs, ds, z = u["cs"], u["ds"], u["z"]
                t1, _, hi, lo = u["w"].ap
                if u["first"]:
                    acc_t[0] = dve.op(lambda e: e.memset(acc, 0.0), acc_t[0])
                pe.op(lambda e: e.matmul(z.ap[:, cs], rU, hi[:, cs], start=False, stop=True, skip_group_check=True), u["p"], ru_t)
                m = pe.op(lambda e: e.matmul(z.ap[:, cs], rU, lo[:, cs], start=False, stop=True, skip_group_check=True))
                m2 = m
                if u["kb"] > 0:
                    pe.op(lambda e: e.matmul(col.ap[:, cs], rO, hi[:, cs], start=True, stop=False), col.free)
                    m2 = pe.op(lambda e: e.matmul(col.ap[:, cs], rO, lo[:, cs], start=False, stop=True))
                if u["first"]:
                    y = act.op(lambda e: e.activation(t1[:, cs], z.ap[:, cs], ACT.Exp), m, m2)
                    z.free = [y]
                else:
                    x = dve.op(lambda e: e.tensor_tensor(t1[:, cs], z.ap[:, cs], acc[:, cs], ALU.add), m, m2, acc_t[0])
                    z.free = [x]
                    y = act.op(lambda e: e.activation(t1[:, cs], t1[:, cs], ACT.Exp), x)
                    acc_t[0] = x
                if u["kb"] > 0:
                    acc_t[0] = dve.op(lambda e: e.tensor_tensor(acc[:, cs], acc[:, cs], col.ap[:, cs], ALU.add), m2, acc_t[0])
                    col.free = [acc_t[0]]
                if ds is not None:
                    y = pool.op(lambda e: e.affine_select(out=t1[:, ds], in_=t1[:, ds], pattern=[[1, 128]], compare_op=ALU.is_gt,
                                                          fill=0.0, base=0, channel_multiplier=-1), y)
                u["y"], u["a"] = y, acc_t[0]

            def values(u):
                kb, cs, t1 = u["kb"], u["cs"], u["w"].ap[0]
                if u["first"]:
                    u["o"]["b"] = op.take()
                ob = u["o"]["b"]
                t = pe.op(lambda e: e.matmul(ob.ap[:, cs], Vt[:, kb, :], t1[:, cs], start=u["first"], stop=(kb == 0), skip_group_check=True),
                          u["y"], u["rdy"], ob.free)
                u["w"].free = [t, u["a"]]
                u["t"] = t
                if kb == 0:
                    h, qs = u["h"], slice(u["qc"] * 512, u["qc"] * 512 + 512)
                    r = split((Y[0][:, h, qs], Y[1][:, h, qs]), ob.ap, t)
                    ob.free = r
                    u["o"]["r"].extend(r)

            act.op(lambda e: e.preload_act_table_set("natural_log_exp_and_others"))

            def qkv(h, free, vfree):
                qT, kT = qk[h % 2]
                for q_t in product_steps("w_in", 22 + h, XN, lambda ps, t: [act.op(lambda e: e.mul(qT, ps, 128.0 ** -0.5), t, free)]):
                    yield None
                for k_t in product_steps("w_in", 26 + h, XN, lambda ps, t: [dve.op(lambda e: e.tensor_copy(kT, ps), t, free)]):
                    yield None
                for v_t in product_steps("w_in", 30 + h, XN, lambda ps, t: [act.op(lambda e: e.copy(vf, ps), t, vfree)]):
                    yield None
                yield q_t, k_t, v_t

            read = [[], []]
            q_t, k_t, v_t = sb_tok
            for h in range(4):
                if h:
                    q_t, k_t, v_t = got
                vt_t = transposes(vf if h else sb_first[2], lambda ps, t: [dve.op(lambda e: e.tensor_copy(Vt.rearrange("p a b -> p (a b)"), ps), t, prev)],
                                  8, v_t, prp.take())
                units = []
                r = []
                for qc in range(2):
                    nk = 4 * qc + 4
                    o = {"r": r}
                    for kb in range(nk - 1, -1, -1):
                        off = max(0, kb - 4 * qc) * 128
                        units.append(dict(h=h, qc=qc, kb=kb, cs=slice(off, 512), qs=slice(qc * 512 + off, qc * 512 + 512),
                                          ds=slice(off, off + 128) if kb >= 4 * qc else None, first=(kb == nk - 1), o=o,
                                          rdy=[q_t, k_t, vt_t]))
                n = len(units)
                got = None
                side = qkv(h + 1, read[(h + 1) % 2], vt_t) if h < 3 else iter(())
                for i in range(n + 3):
                    if i > 0:
                        got = next(side, got) or got
                        got = next(side, got) or got
                    if i < n:
                        scores(units[i])
                    if 0 <= i - 1 < n:
                        parts(units[i - 1])
                    if 0 <= i - 2 < n:
                        weights(units[i - 2])
                    if 0 <= i - 3 < n:
                        values(units[i - 3])
                for x in side:
                    got = x or got
                prev = [units[-1]["t"], units[-1]["a"]]
                read[h % 2] = [units[-1]["t"]]
                res.append(r)
            mmps = keep_ps
            return res

        barrier()
        yt = sb_branch()
        probe("sb0", Y[0].bitcast(F32), yt)
        barrier()
        for b_ in mmps.bufs:
            b_.free = []
        top[0] = mark
        keep = top[0]
        top[0] += 2 * 4 * T
        WX = (sb([128, 4, T], F32R), sb([128, 4, T], F32R))
        top[0] = keep
        mx = []

        def early(ft, ready):
            if ft < 4:
                r = split((WX[0][:, ft, :], WX[1][:, ft, :]), merged[:, ft, :], ready)
                mx.append((WX[0][:, ft, :], WX[1][:, ft, :], r))

        merge(2, 4, lambda: yt, done=early)
        merge_end = [pe.last]
        probe("merged", merged, m_tok)

        for k in range(4):
            r = split((Y[0][:, k, :], Y[1][:, k, :]), merged[:, 4 + k, :], m_tok[4 + k], merge_end)
            mx.append((Y[0][:, k, :], Y[1][:, k, :], r))
        X2 = merged
        keep, xls = top[0], []
        for n in range(2):
            top[0] = base0 + (8 * n + 7) * 4 * T
            xls.append(sb([128, T]))
        top[0] = keep
        xl = Rot(xls)
        for b_ in xl.bufs:
            b_.free = merge_end
        top[0] = base_y
        sq_acc = sb([128, T])
        sq_add, sq_last = square_sum(sq_acc, [sb([128, T])], m_tok)
        x2_tok, hn = [None] * 8, [None] * 8
        xlane = lanes(2)
        for ft in range(8):
            b = xl.take()
            ld = dma(sp, b.ap, A["xT"][:, ft, :], b.free, lane=xlane[ft % 2])

            def ev(ps, t):
                d = dve.op(lambda e: e.tensor_tensor(X2[:, ft, :], ps, b.ap, ALU.add), t, ld, mx[ft][2])
                b.free = [d]
                x2_tok[ft] = [d]
                sq_add(X2[:, ft, :], d)
                hn[ft] = split_scaled((XH[0][:, ft, :], XH[1][:, ft, :]), X2[:, ft, :], vec("ffn_g", ft), d, merge_end, v_tok)
                return [d]
            product("w_out", ft, mx, ev)
        probe("x2", X2, x2_tok)
        top[0] = y_addr

        def ffn(Xacc, rdy, wu, wd, hx, conv, out_scale, rstd, root, tail):
            H = (sb([128, 6, T], F32R), sb([128, 6, T], F32R))
            PADW = 2
            sg = Rot([sb([128, T + PADW]) for _ in range(2)])
            cb = Rot([sb([128, T]) for _ in range(2)]) if conv else None
            uv = Rot([sb([128, T]) for _ in range(2)])
            acc_t = list(rdy)
            zt = None
            if conv:
                zt = [dve.op(lambda e, b=b: e.memset(b.ap[:, 0:PADW], 0.0)) for b in sg.bufs]
            h_free = []
            k0 = 0
            for n in FFN_CUT:
                hs = []
                for i in range(n):
                    u = uv.take()
                    got = {}

                    def conved(ps, t, ft, dst, dfree):
                        raw = sg.take()
                        a = act.op(lambda e: e.copy(raw.ap[:, PADW:], ps), t, raw.free, zt)
                        w = [vec("fconv", 44 * j + ft) for j in range(3)]
                        x = dve.op(lambda e: e.tensor_scalar(dst, raw.ap[:, 2:], w[2], vec("fconv_b", ft), ALU.mult, ALU.add), a, dfree, v_tok)
                        x = dve.op(lambda e: e.scalar_tensor_tensor(dst, raw.ap[:, 1:T + 1], w[1], dst, ALU.mult, ALU.add), x)
                        x = dve.op(lambda e: e.scalar_tensor_tensor(dst, raw.ap[:, 0:T], w[0], dst, ALU.mult, ALU.add), x)
                        raw.free = [x]
                        return a, x

                    if conv:
                        gb, vb = cb.bufs

                        def gate(ps, t):
                            a, x = conved(ps, t, k0 + i, gb.ap, gb.free)
                            got["g"] = act.op(lambda e: e.activation(gb.ap, gb.ap, ACT.Silu), x)
                            return [a]

                        def val(ps, t):
                            a, x = conved(ps, t, 22 + k0 + i, vb.ap, vb.free)
                            got["v"] = dve.op(lambda e: e.tensor_tensor(u.ap, gb.ap, vb.ap, ALU.mult), x, got["g"], u.free)
                            gb.free = vb.free = [got["v"]]
                            return [a]
                    else:
                        s = sg.take()

                        def gate(ps, t):
                            m = dve.op(lambda e: e.tensor_tensor(s.ap[:, 0:T], ps, rstd, ALU.mult), t, s.free, root())
                            got["g"] = act.op(lambda e: e.activation(s.ap[:, 0:T], s.ap[:, 0:T], ACT.Silu), m)
                            return [m]

                        def val(ps, t):
                            m = dve.op(lambda e: e.tensor_tensor(u.ap, ps, rstd, ALU.mult), t, u.free)
                            got["v"] = dve.op(lambda e: e.tensor_tensor(u.ap, u.ap, s.ap[:, 0:T], ALU.mult), m, got["g"])
                            s.free = [got["v"]]
                            return [m]

                    product(wu, k0 + i, hx, gate)
                    product(wu, 22 + k0 + i, hx, val)
                    r = split((H[0][:, i, :], H[1][:, i, :]), u.ap, got["v"], h_free)
                    u.free = r
                    hs.append((H[0][:, i, :], H[1][:, i, :], r))
                finish = tail(sg.bufs, uv.bufs) if k0 + n == 22 else None
                for ft in range(8):
                    def ev(ps, t):
                        if out_scale is None:
                            d = dve.op(lambda e: e.tensor_tensor(Xacc[:, ft, :], ps, Xacc[:, ft, :], ALU.add), t, acc_t[ft])
                        else:
                            d = dve.op(lambda e: e.scalar_tensor_tensor(Xacc[:, ft, :], ps, out_scale(ft), Xacc[:, ft, :], ALU.mult, ALU.add),
                                       t, acc_t[ft])
                        acc_t[ft] = [d]
                        if finish:
                            finish(ft, d)
                        return [d]
                    product(wd, ft, hs, ev, k0)
                h_free = [pe.last]
                k0 += n
            return acc_t

        mark = top[0]
        HN = [(XH[0][:, k, :], XH[1][:, k, :], hn[k]) for k in range(8)]
        rstd1 = sb([128, T])
        root_tok = []

        def root():
            if not root_tok:
                pb = mmps.take()
                t = ones_sum([(sq_acc, sq_last())], pb.ap, pb.free)[-1]
                a, x = inv_root(pb.ap, T, rstd1, t)
                pb.free = [a]
                root_tok.append(x)
            return root_tok

        tails = {}

        def tail1(sgb, uvb):
            sa, st_ = sgb[0].ap[:, 0:T], sgb[1].ap[:, 0:T]
            add, last = square_sum(sa, [st_], sgb[0].free, sgb[1].free)
            padd = plain_sum(uvb[0].ap, uvb[0].free)
            tails[1] = dict(sq=sa, last=last, sum=uvb[0].ap)

            def finish(ft, d):
                add(X2[:, ft, :], d)
                tails[1]["tok"] = padd(X2[:, ft, :], d, vec("fin_g", ft))
            return finish

        def tail2(sgb, uvb):
            padd = plain_sum(uvb[0].ap, uvb[0].free)
            tails[2] = dict(sum=uvb[0].ap)

            def finish(ft, d):
                tails[2]["tok"] = padd(X1[:, ft, :], d)
            return finish

        acc = ffn(X2, [None] * 8, "w_up", "w_down", HN, False, None, rstd1, root, tail1)
        probe("x3", X2, acc)
        if dump is not None and "x3" in dump:
            barrier()
        top[0] = mark

        sh_a, sc_a, gt_a, sh_f, sc_f, gt_f = (lambda k, o=o, n=1: mod[:, o + k:o + k + n] for o in (0, 8, 16, 24, 32, 40))
        cmb = []
        for n, (g, o, sc, sh) in enumerate((("ln0_g", "ln0_b", sc_a, sh_a), ("ln1_g", "ln1_b", sc_f, sh_f))):
            gs, bs, ga, ba = (comb[:, 32 * n + 8 * j:32 * n + 8 * j + 8] for j in range(4))
            c1 = dve.op(lambda e: e.tensor_tensor(gs, vec(g, 0, 8), sc(0, n=8), ALU.mult), md2, v_tok)
            c2 = dve.op(lambda e: e.tensor_tensor(bs, vec(o, 0, 8), sc(0, n=8), ALU.mult))
            c3 = dve.op(lambda e: e.tensor_tensor(bs, bs, sh(0, n=8), ALU.add), c2)
            c4 = dve.op(lambda e: e.tensor_scalar(ga, vec(g, 0, 8), ALPHA, None, ALU.mult))
            c5 = dve.op(lambda e: e.tensor_scalar(ba, vec(o, 0, 8), ALPHA, None, ALU.mult))
            cmb.append((gs, bs, ga, ba, [c1, c3, c4, c5]))

        def modulated(X, ready, c, tmp):
            gs, bs, _, _, tok = cmb[c]
            res = []
            late = None
            for k in range(8):
                b = tmp.take()
                h = act.op(lambda e: e.activation(b.ap, X[:, k, :], ACT.Identity, scale=gs[:, k:k + 1], bias=bs[:, k:k + 1]), ready[k](), tok, b.free)
                late = split_late(late, b, (XH[0][:, k, :], XH[1][:, k, :]), h, res)
            split_late(late, None, None, None, res)
            return [(XH[0][:, k, :], XH[1][:, k, :], r) for k, r in enumerate(res)]

        def residual(X, ready, c):
            _, _, ga, ba, tok = cmb[c]
            return [[act.op(lambda e, k=k: e.activation(X[:, k, :], X[:, k, :], ACT.Identity, scale=ga[:, k:k + 1], bias=ba[:, k:k + 1]), ready[k], tok)]
                    for k in range(8)]

        sm = sb([128, T])
        rstd = sb([128, T])
        keep = top[0]
        tmp = Rot([sb([128, T]) for _ in range(4)])
        rfin, mu = sb([128, T]), sb([128, T])
        t1 = tails[1]
        pb = mmps.take()
        t = ones_sum([(t1["sq"], t1["last"]())], pb.ap, pb.free)[-1]
        a, fin = inv_root(pb.ap, T, rfin, t)
        pb.free = [a]
        xc = centred(X2, (t1["sum"], t1["tok"]), mu, tmp, rstd, "fin_g", (rfin, fin))
        HX = modulated(X2, xc, 0, tmp)
        smt = product("w_in2", 28, HX, lambda ps, t: [act.op(lambda e: e.copy(sm, ps), t)])
        sp_t = []

        def put_residual():
            _, _, ga, ba, ctok = cmb[0]
            for k in range(8):
                x = act.op(lambda e: e.activation(X2[:, k, :], X2[:, k, :], ACT.Identity, scale=ga[:, k:k + 1], bias=ba[:, k:k + 1]),
                           HX[k][2], ctok)
                sp_t.append(dma(sp, spill[:, k, :], X2[:, k, :], x, lane=lane8[k]))
                yield

        put_steps = put_residual()
        barrier(())
        top[0] = keep
        X1 = X2
        O = X1

        upper, up_t = const("upper")
        base_g = top[0]
        tile_b = 4 * T
        VT = [at_address(m_addr + n * tile_b, [128, 8, 128]) for n in range(4)]
        gq0, gk0 = (at_address(m_addr + n * tile_b, [128, T]) for n in (4, 5))
        gv0 = at_address(m_addr + 6 * tile_b, [128, 8, 256])
        mS, ms_t = const("mS")
        mT, mt_t = const("mT")
        lev, lv_t = const("lev")
        abt = sb([128, 8, 8])
        beta, la, t1_, gl, G, nG, eG, kl = (sb([128, 8, 4]) for _ in range(8))
        na = sb([128, 4])
        fl = lambda z: z.rearrange("p a b -> p (a b)")
        FT = [[sb([128, T]) for _ in range(2)] for _ in range(4)]
        ft_at = top[0] - 8 * tile_b
        gv1 = sb([128, 8, 256])
        mG, mg_t = const("mG")
        g2 = sb([128, 256])
        g2_t = dma(sp, g2, A["gate2"])
        wk_at = top[0]
        wk = Rot([sb([128, T]) for _ in range(4)])
        tok = {}
        later = []

        def project(ft, evac):
            r = product("w_in2", ft, HX, evac)
            todo = later[:]
            del later[:]
            for f in todo:
                f()
            for _ in range(4):
                next(put_steps, None)
            return r

        def gates():
            pb = mmps.take()

            def ev(ps, t):
                v = ps.rearrange("p (a c) -> p a c", a=8)
                return [dve.op(lambda e: e.tensor_copy(abt[:, :, 0:4], v[:, :, 0:4]), t),
                        dve.op(lambda e: e.tensor_copy(abt[:, :, 4:8], v[:, :, 32:36]), t)]
            at_ = transposes(sm, ev, 8, smt, pb)
            tok["beta"] = act.op(lambda e: e.activation(beta, abt[:, :, 4:8], ACT.Sigmoid), at_)
            act.op(lambda e: e.preload_act_table_set("natural_log_exp_and_others"))
            nat = act.op(lambda e: e.activation(na, vec("alog", 0, 4), ACT.Exp), v_tok)
            x = dve.op(lambda e: e.tensor_tensor(la, abt[:, :, 0:4], vec("dtb", 0, 4).unsqueeze(1).to_broadcast([128, 8, 4]), ALU.add), at_, v_tok)
            y = act.op(lambda e: e.activation(t1_, la, ACT.Abs), x)
            y = act.op(lambda e: e.activation(t1_, t1_, ACT.Exp, scale=-1.0), y)
            y = act.op(lambda e: e.activation(t1_, t1_, ACT.Ln, bias=1.0), y)
            y = dve.op(lambda e: e.scalar_tensor_tensor(la, la, 0.0, t1_, ALU.max, ALU.add), x, y)
            n = dve.op(lambda e: e.tensor_scalar(na, na, -1.0, None, ALU.mult), nat)
            tok["la"] = dve.op(lambda e: e.tensor_tensor(la, la, na.unsqueeze(1).to_broadcast([128, 8, 4]), ALU.mult), y, n)
            later.append(decays)

        def decays():
            lat = tok["la"]
            pb = mmps.take()
            t = pe.op(lambda e: e.matmul(pb.ap[:, 0:32], upper, fl(la), start=True, stop=True), lat, up_t, pb.free)
            g1 = dve.op(lambda e: e.tensor_copy(fl(G), pb.ap[:, 0:32]), t)
            g2 = dve.op(lambda e: e.tensor_scalar(fl(nG), pb.ap[:, 0:32], -1.0, None, ALU.mult), t)
            pb.free = [g1, g2]
            pc = mmps.take()
            t2 = pe.op(lambda e: e.matmul(pc.ap[:, 0:32], ones, fl(la), start=True, stop=True), lat, pc.free)
            act.op(lambda e: e.preload_act_table_set("natural_log_exp_and_others"))
            glt = act.op(lambda e: e.activation(fl(gl), pc.ap[:, 0:32], ACT.Exp), t2)
            k = dve.op(lambda e: e.tensor_tensor(fl(kl), pc.ap[:, 0:32], fl(G), ALU.subtract), t2, g1, glt)
            pc.free = [glt, k]
            tok["kl"] = act.op(lambda e: e.activation(fl(kl), fl(kl), ACT.Exp), k)
            x = act.op(lambda e: e.activation(fl(eG), fl(G), ACT.Exp), g1)
            tok["eG"] = dve.op(lambda e: e.scalar_tensor_tensor(fl(eG), fl(eG), -1.0, fl(beta), ALU.mult, ALU.mult), x, tok["beta"])
            tok["G"], tok["gl"] = [g1, g2], glt

        def conv_silu(ft, dst, *free):
            r = wk.take()
            pt = project(ft, lambda ps, t: [act.op(lambda e: e.copy(r.ap, ps), t, r.free)])
            w = [vec("conv", 12 * j + ft) for j in range(4)]
            x = dve.op(lambda e: e.tensor_scalar(dst, r.ap, w[3], None, ALU.mult), pt, v_tok, free)
            for j in (1, 2, 3):
                x = dve.op(lambda e: e.scalar_tensor_tensor(dst[:, j:], r.ap[:, 0:T - j], w[3 - j], dst[:, j:], ALU.mult, ALU.add), x)
            r.free = [x]
            return act.op(lambda e: e.activation(dst, dst, ACT.Silu), x)

        def unit_length(dst, x, scale, put):
            b = wk.take()
            sq = act.op(lambda e: e.activation(b.ap, dst, ACT.Square), x, b.free)

            def rest():
                pb = mmps.take()
                t = ones_sum([(b.ap, sq)], pb.ap, pb.free)[-1]
                a, d = inv_root(pb.ap, 1, b.ap, t)
                pb.free = [a]
                b.free = [dve.op(lambda e: e.scalar_tensor_tensor(dst, dst, scale, b.ap, ALU.mult, ALU.mult), d)]
                put.extend(b.free)
            later.append(rest)

        def by_token(src, ready, dst, put, scale=None):
            def rest():
                pb = mmps.take()

                def ev(ps, t):
                    v = ps.rearrange("p (a b) -> p a b", a=8)
                    if scale is None:
                        return [dve.op(lambda e: e.tensor_copy(dst, v), t)]
                    return [dve.op(lambda e: e.tensor_tensor(dst, v, scale[0].unsqueeze(2).to_broadcast([128, 8, 128]), ALU.mult), t, tok[scale[1]])]
                put.extend(transposes(src.ap, ev, 8, ready, pb))
                src.free = [pe.last]
            later.append(rest)

        def put_away(ft, slot, fn):
            b = wk.take()
            r = project(ft, lambda ps, t: [act.op(lambda e: fn(e, b.ap, ps), t, b.free)])
            b.free = [dma(sp, spill[:, 8 + slot, :], b.ap, r, lane=slane[slot])]
            away[slot] = b.free

        silu = lambda e, o, i: e.activation(o, i, ACT.Silu)
        slane, away = lanes(10), {}
        q_tok, k_tok, v_tk = ([[] for _ in range(4)] for _ in range(3))
        later.append(gates)
        for h in range(4):
            x = conv_silu(h, FT[h][0])
            unit_length(FT[h][0], x, 128.0 ** -0.5, q_tok[h])
            x = conv_silu(4 + h, FT[h][1])
            unit_length(FT[h][1], x, 1.0, k_tok[h])
            b = wk.take()
            x = conv_silu(8 + h, b.ap, b.free)
            by_token(b, x, VT[h], v_tk[h], (beta[:, :, h], "beta"))
            if h == 0:
                for q in (act, dve):
                    q.extra = q.extra + sp_t
            put_away(12 + h, h, silu)
        gqt, gkt, gvt = [[], []], [[], []], [[], []]
        for hp in range(2):
            if hp == 0:
                gqt[0] = project(16, lambda ps, t: [act.op(lambda e: e.mul(gq0, ps, 0.125), t)])
                gkt[0] = project(18, lambda ps, t: [act.op(lambda e: e.copy(gk0, ps), t)])
            else:
                put_away(17, 8, lambda e, o, i: e.mul(o, i, 0.125))
                put_away(19, 9, lambda e, o, i: e.copy(o, i))
            for hh in range(2):
                b = wk.take()
                x = project(20 + 2 * hp + hh, lambda ps, t: [act.op(lambda e: e.copy(b.ap, ps), t, b.free)])
                by_token(b, x, (gv0, gv1)[hp][:, :, 128 * hh:128 * hh + 128], gvt[hp])
            for hh in range(2):
                put_away(24 + 2 * hp + hh, 4 + 2 * hp + hh, silu)
        for f in later:
            f()
        barrier()

        open_dma.extend([t for x in away.values() for t in x])
        area = [base0, base0 + 4 * tile_b, base0 + 8 * tile_b, base0 + 12 * tile_b]
        Z, AT = (at_address(area[n], [128, 8, 512]) for n in (0, 2))
        WB = []
        for n in range(4):
            x = area[1 + 2 * (n // 2)] + (n % 2) * 2 * tile_b
            WB.append({k: at_address(x + j * tile_b // 2, [128, 512]) for j, k in enumerate(("M", "Tm", "Y", "Ml"))})
        rot = Rot(banks[0:8])
        units = [[(2 * (b % 4) + x, 2 * (b // 4) + hh) for x in range(2) for hh in range(2)] for b in range(8)]
        sl = [slice(128 * n, 128 * n + 128) for n in range(4)]
        v3 = lambda z: z.rearrange("p (n c) -> p n c", n=4)

        def prep(b, wb):
            us = units[b]
            Mm, Tm, Yy, Ml = wb["M"], wb["Tm"], wb["Y"], wb["Ml"]
            Zb, ATb = Z[:, b, :], AT[:, b, :]
            fr = wb.get("free", [])
            lb = [dve.op(lambda e: e.tensor_scalar(Ml[:, sl[n]], ones, la[:, c, h:h + 1], None, ALU.mult), fr, tok["la"], o_tok)
                  for n, (c, h) in enumerate(us)]
            bg = rot.take()
            for n in range(4):
                tg = pe.op(lambda e: e.matmul(bg.ap[:, sl[n]], Ml[:, sl[n]], upper, start=True, stop=True), lb, bg.free, up_t)
            yield
            m3 = mS.unsqueeze(1).to_broadcast([128, 4, 128])
            m4 = mT.unsqueeze(1).to_broadcast([128, 4, 128])
            d1 = dve.op(lambda e: e.scalar_tensor_tensor(v3(Tm), v3(bg.ap), -1.0, m3, ALU.mult, ALU.add), tg, fr, ms_t)
            d2 = dve.op(lambda e: e.tensor_tensor(v3(Yy), v3(bg.ap), m4, ALU.add), tg, fr, mt_t)
            ex = act.op(lambda e: e.activation(Ml, bg.ap, ACT.Exp), d2)
            bg.free = [ex]
            e1 = [act.op(lambda e: e.activation(Tm[:, sl[n]], Tm[:, sl[n]], ACT.Exp, bias=G[:, c, h:h + 1]), d1, tok["G"]) for n, (c, h) in enumerate(us)]
            e2 = [act.op(lambda e: e.activation(Yy[:, sl[n]], Yy[:, sl[n]], ACT.Exp, bias=nG[:, c, h:h + 1]), d2, tok["G"]) for n, (c, h) in enumerate(us)]
            yield
            ba, bq = rot.take(), rot.take()
            for n, (c, h) in enumerate(us):
                cc = slice(128 * c, 128 * c + 128)
                kx, qx = FT[h][1], FT[h][0]
                ta = pe.op(lambda e: e.matmul(ba.ap[:, sl[n]], kx[:, cc], kx[:, cc], start=True, stop=True), ba.free, k_tok[h])
                tq = pe.op(lambda e: e.matmul(bq.ap[:, sl[n]], kx[:, cc], qx[:, cc], start=True, stop=True), bq.free, q_tok[h])
            ms = [dve.op(lambda e: e.scalar_tensor_tensor(Mm[:, sl[n]], ba.ap[:, sl[n]], beta[:, c, h:h + 1], Tm[:, sl[n]], ALU.mult, ALU.mult),
                         ta, e1, fr, tok["beta"]) for n, (c, h) in enumerate(us)]
            ba.free = [ms[-1]]
            at = dve.op(lambda e: e.tensor_tensor(ATb, bq.ap, Yy, ALU.mult), tq, e2)
            bq.free = [at]
            qd = []
            for n, (c, h) in enumerate(us):
                qx = FT[h][0][:, 128 * c:128 * c + 128]
                qd.append(dve.op(lambda e: e.tensor_tensor(qx, qx, Ml[:, sl[n]], ALU.mult), tq, ex))
            i3 = ident.unsqueeze(1).to_broadcast([128, 4, 128])

            def lmask(l, *w):
                m = lev[:, 128 * l:128 * l + 128].unsqueeze(1).to_broadcast([128, 4, 128])
                return dve.op(lambda e: e.tensor_tensor(v3(Ml), v3(Mm), m, ALU.mult), w, ms, lv_t)
            ml = lmask(0, qd)
            yield
            bt = rot.take()
            for n in range(4):
                tt_ = pe.op(lambda e: e.transpose(bt.ap[:, sl[n]], Ml[:, sl[n]], ident), ml, bt.free)
            tm_ = dve.op(lambda e: e.scalar_tensor_tensor(v3(Tm), v3(Ml), -1.0, i3, ALU.mult, ALU.add), ml, ms)
            zt_ = dve.op(lambda e: e.scalar_tensor_tensor(v3(Zb), v3(bt.ap), -1.0, i3, ALU.mult, ALU.add), tt_)
            bt.free = [zt_]
            ml = lmask(1, tt_, tm_)
            yield
            for l in range(1, 7):
                b1 = rot.take()
                for n in range(4):
                    ty = pe.op(lambda e: e.matmul(b1.ap[:, sl[n]], Ml[:, sl[n]], Zb[:, sl[n]], start=True, stop=True), ml, zt_, b1.free)
                if l > 1:
                    b3 = rot.take()
                    for n in range(4):
                        tt_ = pe.op(lambda e: e.transpose(b3.ap[:, sl[n]], Zb[:, sl[n]], ident), b3.free)
                ye = act.op(lambda e: e.copy(Yy, b1.ap), ty, at)
                b1.free = [ye]
                if l > 1:
                    tm_ = act.op(lambda e: e.copy(Tm, b3.ap), tt_, tx)
                    b3.free = [tm_]
                if l < 6:
                    ml = lmask(l + 1, ty)
                yield
                b2 = rot.take()
                for n in range(4):
                    tx = pe.op(lambda e: e.matmul(b2.ap[:, sl[n]], Tm[:, sl[n]], Yy[:, sl[n]], start=True, stop=True), ye, tm_, b2.free)
                zt_ = dve.op(lambda e: e.tensor_tensor(Zb, Zb, b2.ap, ALU.subtract), tx, ty, tt_)
                b2.free = [zt_]
                yield
            wb["free"] = [zt_, tx]

        def together(gens):
            gens = list(gens)
            while gens:
                for g in list(gens):
                    try:
                        next(g)
                    except StopIteration:
                        gens.remove(g)

        act.op(lambda e: e.preload_act_table_set("natural_log_exp_and_others"))
        for r in range(2):
            together([prep(b, WB[n]) for n, b in enumerate((2 * r, 2 * r + 1, 4 + 2 * r, 5 + 2 * r))])
        barrier()
        KT = [at_address(area[1] + h * tile_b, [128, 8, 128]) for h in range(4)]
        small = [at_address(area[3] + n * tile_b // 8, [128, 128]) for n in range(20)]
        OD = [at_address(wk_at + h * tile_b, [128, T]) for h in range(4)]
        rot = Rot([b for p in pairs[0:2] for b in (p[:, 0:512], p[:, 512:1024])])
        rot_o = Rot([b for p in pairs[2:4] for b in (p[:, 0:512], p[:, 512:1024])])
        kt_t = []
        for h in range(4):
            for x in range(2):
                pb = rot.take()
                for n in range(4):
                    c = 4 * x + n
                    t = pe.op(lambda e: e.transpose(pb.ap[:, sl[n]], FT[h][1][:, 128 * c:128 * c + 128], ident), pb.free)
                d = dve.op(lambda e: e.tensor_tensor(KT[h][:, 4 * x:4 * x + 4, :], v3(pb.ap),
                                                     kl[:, 4 * x:4 * x + 4, h].unsqueeze(2).to_broadcast([128, 4, 128]), ALU.mult), t, tok["kl"])
                pb.free = [d]
                kt_t.append(d)
        S = [[small[2 * h], small[2 * h + 1]] for h in range(4)]
        vn = [[small[8 + 2 * h], small[9 + 2 * h]] for h in range(4)]
        rb_ = small[16:20]
        s_tok, rb_free = [[] for _ in range(4)], [[] for _ in range(4)]
        vn_free, s_read = [[[], []] for _ in range(4)], [[[], []] for _ in range(4)]
        o_tk = [[] for _ in range(4)]
        for c in range(8):
            cc = slice(128 * c, 128 * c + 128)
            po, rx, rd, vt_ = [rot_o.take() for _ in range(4)], [None] * 4, [None] * 4, [None] * 4
            for h in range(4):
                if c == 0:
                    rx[h] = VT[h][:, 0, :]
                    continue
                p1, So = rot.take(), S[h][c % 2]
                t = pe.op(lambda e: e.matmul(p1.ap[:, 0:128], FT[h][1][:, cc], So, start=True, stop=True), p1.free, s_tok[h])
                rd[h] = dve.op(lambda e: e.scalar_tensor_tensor(rb_[h], p1.ap[:, 0:128], eG[:, c, h:h + 1], VT[h][:, c, :], ALU.mult, ALU.add),
                               t, rb_free[h], tok["eG"])
                p1.free = [rd[h]]
                rx[h] = rb_[h]
            for h in range(4):
                b, n = 4 * (h // 2) + c // 2, 2 * (c % 2) + h % 2
                if c > 0:
                    pe.op(lambda e: e.matmul(po[h].ap[:, 0:128], S[h][c % 2], FT[h][0][:, cc], start=True, stop=False), po[h].free)
                p2, vx = rot.take(), vn[h][c % 2]
                t = pe.op(lambda e: e.matmul(p2.ap[:, 0:128], Z[:, b, sl[n]], rx[h], start=True, stop=True), p2.free, rd[h])
                rb_free[h] = [t]
                vt_[h] = act.op(lambda e: e.copy(vx, p2.ap[:, 0:128]), t, vn_free[h][c % 2])
                p2.free = [vt_[h]]
            for h in range(4):
                b, n = 4 * (h // 2) + c // 2, 2 * (c % 2) + h % 2
                vx = vn[h][c % 2]
                if c < 7:
                    p3, So, Sn = rot.take(), S[h][c % 2], S[h][(c + 1) % 2]
                    t = pe.op(lambda e: e.matmul(p3.ap[:, 0:128], KT[h][:, c, :], vx, start=True, stop=True), p3.free, vt_[h], kt_t)
                    if c == 0:
                        s_tok[h] = dve.op(lambda e: e.tensor_copy(Sn, p3.ap[:, 0:128]), t)
                    else:
                        s_tok[h] = dve.op(lambda e: e.scalar_tensor_tensor(Sn, So, gl[:, c, h:h + 1], p3.ap[:, 0:128], ALU.mult, ALU.add),
                                          t, s_read[h][(c + 1) % 2], s_tok[h], tok["gl"])
                    p3.free = [s_tok[h]]
                to = pe.op(lambda e: e.matmul(po[h].ap[:, 0:128], vx, AT[:, b, sl[n]], start=(c == 0), stop=True), vt_[h], po[h].free)
                vn_free[h][c % 2] = [to]
                s_read[h][c % 2] = [to]
                oa = act.op(lambda e: e.copy(OD[h][:, cc], po[h].ap[:, 0:128]), to)
                po[h].free = [oa]
                o_tk[h].append(oa)
        barrier()
        for b_ in pbufs:
            b_.free = []
        scanm = at_address(area[1], [128, T])
        sc_t = dma(sp, scanm, A["c_scanm"])
        zl = lanes(4)
        zD = [at_address(area[3] + h * tile_b, [128, T]) for h in range(4)]
        zD_t = [dma(sp, zD[h], spill[:, 8 + h, :], away[h], lane=zl[h]) for h in range(4)]
        gq1, gk1 = (at_address(m_addr + n * tile_b, [128, T]) for n in (0, 1))
        gql = lanes(2)
        gqt[1] = [dma(sp, gq1, spill[:, 16, :], away[8], lane=gql[0])]
        gkt[1] = [dma(sp, gk1, spill[:, 17, :], away[9], lane=gql[1])]
        nrm = [tuple(at_address(x, [128, T]) for x in p) for p in 2 * [(m_addr + 2 * tile_b, m_addr + 3 * tile_b),
                                                                      (area[1] + 2 * tile_b, area[1] + 3 * tile_b)]]
        ox, outs = [None] * 8, [None] * 8

        def gated_norm(o, rdy, gname, z, z_t, f, sq, r):
            a = act.op(lambda e: e.activation(sq, o, ACT.Square), rdy)
            zo = dve.op(lambda e: e.scalar_tensor_tensor(z, o, vec(gname), z, ALU.mult, ALU.mult), rdy, z_t)
            yield
            pb = mmps.take()
            t = ones_sum([(sq, a)], pb.ap, pb.free)[-1]
            a, x = inv_root(pb.ap, 128, r, t, tables=False)
            pb.free = [a]
            yield
            d = dve.op(lambda e: e.tensor_tensor(o, z, r, ALU.mult), x, zo)
            outs[f] = (o, d)
            if f >= 4:
                hi, lo = XH[0][:, f, :], XH[1][:, f, :]
                over = [outs[n][1] for n in range(4)]
                a = act.op(lambda e: e.copy(hi, o), d, over)
                yield
                x = dve.op(lambda e: e.tensor_tensor(lo, o, hi.bitcast(F32), ALU.subtract), a, d, over)
                ox[f] = (hi, lo, [a, x])
            yield

        def end_delta():
            for x in (0, 2):
                gens = [gated_norm(OD[h], o_tk[h], "dn_g", zD[h], zD_t[h], h, *nrm[h]) for h in (x, x + 1)]
                for _ in range(3):
                    for g in gens:
                        next(g)
                    yield

        def gla(hp):
            base = (ft_at, area[0])[hp]
            step = tile_b
            if hp == 0:
                tiles = [base + n * step for n in range(8)]
            else:
                tiles = [area[0] + n * step for n in range(4)] + [area[2] + n * step for n in range(4)]
            bb, tA, tB = (at_address(x, [128, T]) for x in tiles[0:3])
            kdt = at_address(tiles[3], [128, 8, 128])
            St = at_address(tiles[4], [128, 16, 128])
            at = at_address(tiles[6], [128, 2, 8, 128])
            bl, egl = sb([128, 16]), sb([128, 16])
            q, k, vt = ((gq0, gk0, gv0), (gq1, gk1, gv1))[hp]
            qt, kt = gqt[hp], gkt[hp]
            pb = mmps.take()
            for h in range(2):
                t = pe.op(lambda e: e.matmul(pb.ap[:, 512 * h:512 * h + 512], g2[:, 128 * hp:128 * hp + 128],
                                             sm[:, 512 * h:512 * h + 512], start=True, stop=True), g2_t, smt, pb.free)
            a = act.op(lambda e: e.activation(tA, pb.ap, ACT.Identity, bias=vec("gla_bg", hp)), t, v_tok)
            pb.free = [a]
            x = act.op(lambda e: e.activation(tB, tA, ACT.Abs), a)
            x = act.op(lambda e: e.activation(tB, tB, ACT.Exp, scale=-1.0), x)
            x = act.op(lambda e: e.activation(tB, tB, ACT.Ln, bias=1.0), x)
            yield
            d = dve.op(lambda e: e.scalar_tensor_tensor(tA, tA, 0.0, tB, ALU.min, ALU.subtract), x)
            d = dve.op(lambda e: e.tensor_scalar(tA, tA, 1.0 / 16, None, ALU.mult), d)
            bt = dve.op(lambda e: e.tensor_tensor_scan(bb, scanm, tA, 0.0, ALU.mult, ALU.add), d, sc_t)
            b3 = bb.rearrange("p (c t) -> p c t", t=64)
            blt = dve.op(lambda e: e.tensor_copy(bl.unsqueeze(2), b3[:, :, 63:64]), bt)
            d = dve.op(lambda e: e.tensor_tensor(tB.rearrange("p (c t) -> p c t", t=64), bl.unsqueeze(2).to_broadcast([128, 16, 64]),
                                                 b3, ALU.subtract), blt)
            e2 = act.op(lambda e: e.activation(tB, tB, ACT.Exp), d)
            e1 = act.op(lambda e: e.activation(tA, bb, ACT.Exp), bt)
            e3 = act.op(lambda e: e.activation(bb, bb, ACT.Exp, scale=-1.0), e1, d)
            egt = act.op(lambda e: e.activation(egl, bl, ACT.Exp), blt)
            yield
            kd = dve.op(lambda e: e.tensor_tensor(tB, tB, k, ALU.mult), e2, kt)
            qd = dve.op(lambda e: e.tensor_tensor(q, q, tA, ALU.mult), e1, qt)
            kn = dve.op(lambda e: e.tensor_tensor(k, k, bb, ALU.mult), e3, kd)
            pb = mmps.take()
            kdT = transposes(tB, lambda ps, t: [act.op(lambda e: e.copy(kdt.rearrange("p a b -> p (a b)"), ps), t)], 8, kd, pb)
            yield
            st = [dve.op(lambda e: e.memset(St[:, 0, :], 0.0))]
            att = []
            for hh in range(2):
                rows = slice(64 * hh, 64 * hh + 64)
                pb = mmps.take()
                for a_ in range(8):
                    cc = slice(128 * a_, 128 * a_ + 128)
                    t = pe.op(lambda e: e.matmul(pb.ap[:, cc], k[rows, cc], q[rows, cc], start=True, stop=True), kn, qd, pb.free)
                d = dve.op(lambda e: e.tensor_tensor(at[:, hh, :, :], pb.ap.rearrange("p (a b) -> p a b", a=8),
                                                     mG.unsqueeze(1).to_broadcast([128, 8, 128]), ALU.mult), t, mg_t)
                pb.free = [d]
                att.append(d)
                yield
            for c in range(15):
                a_, r = c // 2, slice(64 * (c % 2), 64 * (c % 2) + 64)
                pb = mmps.take()
                t = pe.op(lambda e: e.matmul(pb.ap[:, 0:256], kdt[r, a_, :], vt[r, a_, :], start=True, stop=True), kdT, gvt[hp], pb.free)
                ns = []
                for hh in range(2):
                    rows = slice(64 * hh, 64 * hh + 64)
                    ns.append(dve.op(lambda e: e.scalar_tensor_tensor(St[rows, c + 1, :], St[rows, c, :], egl[rows, c:c + 1],
                                                                      pb.ap[rows, 128 * hh:128 * hh + 128], ALU.mult, ALU.add), t, st, egt))
                pb.free = ns
                st = ns
                if c % 2:
                    yield
            o_t, os_ = [], []
            for hh in range(2):
                rows = slice(64 * hh, 64 * hh + 64)
                pb = mmps.take()
                for a_ in range(8):
                    cc = slice(128 * a_, 128 * a_ + 128)
                    pe.op(lambda e: e.matmul(pb.ap[:, cc], vt[:, a_, 128 * hh:128 * hh + 128], at[:, hh, a_, :],
                                             start=True, stop=False, skip_group_check=True), att, pb.free)
                    for x in range(2):
                        c = 2 * a_ + x
                        ch = slice(64 * c, 64 * c + 64)
                        t = pe.op(lambda e: e.matmul(pb.ap[:, ch], St[rows, c, :], q[rows, ch],
                                                     start=False, stop=True, skip_group_check=True), st)
                o = (tA, tB)[hh]
                oa = act.op(lambda e: e.copy(o, pb.ap), t, qd, kdT)
                pb.free = [oa]
                o_t.append(oa)
                os_.append(o)
                yield
            ends = []
            for hh in range(2):
                z = at_address(tiles[5 + hh], [128, T])
                n = 4 + 2 * hp + hh
                z_t = dma(sp, z, spill[:, 8 + n, :], away[n], o_t, lane=zl[2 * hp + hh])
                sq, r = (at_address(tiles[x], [128, T]) for x in ((0, 3), (4, 7))[hh])
                ends.append(gated_norm(os_[hh], o_t, "gla_g", z, z_t, n, sq, r))
            for _ in range(4):
                for g in ends:
                    next(g)
                yield

        act.op(lambda e: e.preload_act_table_set("natural_log_exp_and_others"))
        together([gla(0), gla(1), end_delta()])
        top[0] = base_g
        o_order = (4, 5, 6, 7, 0, 3, 1, 2)
        for k in o_order[4:]:
            o, d = outs[k]
            r = split((XH[0][:, k, :], XH[1][:, k, :]), o, d, outs[6][1], outs[7][1], ox[6][2], ox[7][2])
            ox[k] = (XH[0][:, k, :], XH[1][:, k, :], r)
        bt = barrier()
        rt = [dma(sp, X1[:, k, :], spill[:, k, :], bt, sp_t, lane=lane8[k]) for k in range(8)]
        xa = []
        tmp = Rot([sb([128, T]) for _ in range(4)])
        mu, sum1 = sb([128, T]), sb([128, T])
        add1 = plain_sum(sum1)
        for ft in range(8):
            def ev(ps, t):
                d = dve.op(lambda e: e.scalar_tensor_tensor(X1[:, ft, :], ps, gt_a(ft), X1[:, ft, :], ALU.mult, ALU.add), t, rt[ft], md2)
                xa.append(add1(X1[:, ft, :], d))
                return [d]
            product("w_o", ft, ox, ev, order=o_order)
        xc = centred(X1, (sum1, xa[-1]), mu, tmp, rstd)
        HX2 = modulated(X1, xc, 1, tmp)
        al = residual(X1, [h[2] for h in HX2], 1)
        top[0] = mark
        acc = ffn(X1, al, "w_up2", "w_down2", HX2, True, gt_f, None, None, tail2)
        probe("preln2", X1, acc)
        if dump is not None and "preln2" in dump:
            barrier()
        top[0] = mark
        tmp = Rot([sb([128, T]) for _ in range(4)])
        rstd, mu = sb([128, T]), sb([128, T])
        xc = centred(X1, (tails[2]["sum"], tails[2]["tok"]), mu, tmp, rstd)
        xo = [act.op(lambda e, k=k: e.activation(X1[:, k, :], X1[:, k, :], ACT.Identity, scale=vec("ln2_g", k), bias=vec("ln2_b", k)), xc[k](), v_tok)
              for k in range(8)]
        st = [dma(sp, out[:, k, :], X1[:, k, :], xo[k], lane=lane8[k]) for k in range(8)]
        assert w_at[2] == len(plan)
        sp.op(None, st, dumps, sp_t)
        queues = (pe, act, dve, pool, sp)
        for q in queues:
            q.mark()
        for q in queues:
            q.number()
        print("sbuf", high[0], "sems", sem_n[0], [len(q.ops) for q in queues]) if dump is not None else None
        block = ctx.enter_context(nc.Block())
        block.tensor(lambda e: pe.emit(e))
        block.scalar(lambda e: act.emit(e))
        block.vector(lambda e: dve.emit(e))
        block.gpsimd(lambda e: pool.emit(e))
        block.sync(lambda e: sp.emit(e))


def layouts(i):
    f = lambda a: np.ascontiguousarray(a)
    a = {k: np.asarray(v) for k, v in i.items()}

    def wp(w):
        k, n = w.shape
        return f(w.reshape(k // 128, 128, n // 128, 128).transpose(2, 1, 0, 3))

    def cols(v):
        v = v.reshape(-1, 128)
        return v.T

    d = {"xT": f(a["x"][0].T.reshape(8, 128, T).transpose(1, 0, 2))}
    d["w_in"] = wp(a["w_in"][0])
    d["w_gate"] = f(np.concatenate([wp(a["w_gate"][0, b]) for b in range(4)]))
    r = 0
    for b, n in enumerate((512, 256, 512, 512)):
        d[f"w_br{b}"] = wp(a["w_branch"][0, r:r + n])
        r += n
    d["w_glu"] = wp(a["s5_w_glu"][0])
    d["w_out"] = wp(a["w_out"][0])
    d["w_up"] = wp(a["w_up"][0])
    d["w_down"] = wp(a["w_down"][0])
    w2 = a["w_in_2"][0]
    z = lambda n: np.zeros((1024, n), np.float32)
    small = np.concatenate([w2[:, 2048:2052], z(28), w2[:, 2052:2056], z(28), w2[:, 3592:3608], z(48)], axis=1)
    d["w_in2"] = wp(np.concatenate([w2[:, 0:2048], w2[:, 2056:3592], small], axis=1))
    d["w_o"] = wp(a["w_o_2"][0])
    d["w_up2"] = wp(a["ffn_w_up_2"][0])
    d["w_down2"] = wp(a["ffn_w_down_2"][0])
    d["w_ada"] = f(a["w_ada_2"][0].reshape(8, 128, 6144))
    d["pool_w"] = f(a["pool_w"][0].transpose(1, 0, 2))
    d["rel_bias"] = f(np.concatenate([a["rel_bias"], np.zeros((96, 12), np.float32)]))
    st = lambda v: v.reshape(16, 128, 16)
    bc = [st(a["s5_b_re"][0]), st(a["s5_b_im"][0]), st(a["s5_c_re"][0].transpose(0, 2, 1)), st(a["s5_c_im"][0].transpose(0, 2, 1))]
    d["s5bc"] = f(np.stack(bc).transpose(2, 0, 1, 3).reshape(128, 4, 256))
    d["gate2"] = f(np.concatenate([np.zeros((64, 256), np.float32), a["gla_w_gate2_2"][0], np.zeros((48, 256), np.float32)]))
    rep = lambda v: np.broadcast_to(v.reshape(1, -1), (128, v.size))
    v = {"attn_g": cols(a["attn_norm_g"]), "ffn_g": cols(a["ffn_norm_g"]), "fin_g": cols(a["final_norm_g"]),
         "ln0_g": cols(a["ln0_g_2"]), "ln0_b": cols(a["ln0_b_2"]), "ln1_g": cols(a["ln1_g_2"]), "ln1_b": cols(a["ln1_b_2"]),
         "ln2_g": cols(a["ln2_g_2"]), "ln2_b": cols(a["ln2_b_2"]), "pool_s": cols(a["pool_scale"]), "s5_d": cols(a["s5_d"]),
         "c": cols(a["c_2"]), "b_ada": cols(a["b_ada_2"]),
         "conv": a["dn_conv_2"][0].reshape(48, 128).T, "dn_g": cols(a["dn_norm_g_2"]), "gla_bg": cols(a["gla_b_gate_2"]),
         "gla_g": cols(a["gla_norm_g_2"]), "fconv": a["ffn_conv_2"][0].reshape(132, 128).T, "fconv_b": cols(a["ffn_conv_b_2"]),
         "alog": rep(a["dn_a_log_2"]), "dtb": rep(a["dn_dt_bias_2"]),
         "a_re": cols(a["s5_a_re"]), "a_im": cols(a["s5_a_im"]), "ldt": cols(np.repeat(a["s5_log_dt"][0], 64))}
    d["vecs"] = f(np.concatenate([v[n] for n in VCOLS], axis=1))
    for k, c in shape_constants().items():
        d["c_" + k] = c
    return d


def kernel(**inputs):
    import concourse.bacc as bacc
    from concourse.bass_utils import run_bass_kernel_spmd

    arrays = layouts(inputs)
    nc = bacc.Bacc("TRN2", target_bir_lowering=False, num_devices=1)
    A = {k: nc.dram_tensor("in_" + k, v.shape, F32, kind="ExternalInput").ap() for k, v in arrays.items()}
    out = nc.dram_tensor("out_0", (128, 8, T), F32, kind="ExternalOutput").ap()
    scr = nc.dram_tensor("scr", (3, T, 264), F32, kind="Internal").ap()
    spill = nc.dram_tensor("spill", (128, 18, T), F32, kind="Internal").ap()
    bsc = nc.dram_tensor("bsc", (4, 3, 384), F32, kind="Internal").ap()
    build(nc, A, out, scr, spill, bsc)
    r = run_bass_kernel_spmd(nc, [{"in_" + k: v for k, v in arrays.items()}], core_ids=[0])
    o = r.results[0]["out_0"]
    return np.ascontiguousarray(o.transpose(1, 0, 2).reshape(1024, T).T).reshape(1, T, 1024)
```
